# Optimizing a Trainium2 kernel written in Bass

```python
import jax, jax.numpy as jnp
from jax import lax
import numpy as np

D_MODEL = 1024
BATCH = 1
SEQ = 512
DEPTH = 2

CHUNK = 64
Q_BLOCK = 128
NORM_EPS = 1e-6

BRANCH_W = 512
N_BRANCH = 3

GLA_HEADS = 4
GLA_DK = 64
GLA_DV = 128
GLA_GATE_RANK = 16
GLA_TAU = 16.0

DSA_HEADS = 8
DSA_Q_RANK = 256
DSA_LAT = 128
DSA_DV = 64
IDX_HEADS = 4
IDX_DIM = 64
DSA_TOPK_MAX = 256

RWKV_HEADS = 8
RWKV_HEAD = 64
RWKV_W_RANK = 64
RWKV_A_RANK = 64
RWKV_G_RANK = 128
RWKV_LN_EPS = 64e-5
RWKV_SIZES = (RWKV_HEADS * RWKV_HEAD, RWKV_HEADS * RWKV_HEAD, RWKV_HEADS * RWKV_HEAD, RWKV_W_RANK, RWKV_A_RANK, RWKV_G_RANK)
RWKV_WIDTH = 3 * RWKV_HEADS * RWKV_HEAD + RWKV_W_RANK + RWKV_A_RANK + RWKV_G_RANK

IN_SIZES = (GLA_HEADS * GLA_DK, GLA_HEADS * GLA_DK, GLA_HEADS * GLA_DV, GLA_GATE_RANK, GLA_HEADS * GLA_DV,
            DSA_Q_RANK, DSA_LAT, IDX_DIM, IDX_HEADS,
            RWKV_WIDTH,
            N_BRANCH * D_MODEL)
IN_WIDTH = (2 * GLA_HEADS * GLA_DK + 2 * GLA_HEADS * GLA_DV + GLA_GATE_RANK
            + DSA_Q_RANK + DSA_LAT + IDX_DIM + IDX_HEADS + RWKV_WIDTH + N_BRANCH * D_MODEL)

PEER_HEADS = 8
PEER_NKEYS = 128
PEER_N = PEER_NKEYS * PEER_NKEYS
PEER_QDIM = 128
PEER_TOPK = 16
PEER_BLOCK = 128

kernel_name = 'hybrid_gla_dsa_rwkv7_peer_adaln'

def _rms(x, g, eps=NORM_EPS):
    xf = x.astype(jnp.float32)
    y = xf * lax.rsqrt(jnp.mean(xf * xf, axis=-1, keepdims=True) + eps)
    return (y * g).astype(x.dtype)

def _split(p, sizes):
    cuts = [int(s) for s in np.cumsum(sizes)[:-1]]
    return jnp.split(p, cuts, axis=-1)

def _shift(p):
    return jnp.pad(p, ((0, 0), (1, 0), (0, 0)))[:, :-1]

def _gla(q, k, v, a_lr, r, w_a2, b_a, g_o):
    f32 = jnp.float32
    B, S, _ = q.shape
    nc = S // CHUNK
    H, dk, dv = GLA_HEADS, GLA_DK, GLA_DV
    q = q.astype(f32).reshape(B, nc, CHUNK, H, dk) * (dk ** -0.5)
    k = k.astype(f32).reshape(B, nc, CHUNK, H, dk)
    v = v.astype(f32).reshape(B, nc, CHUNK, H, dv)
    log_a = jax.nn.log_sigmoid((a_lr @ w_a2 + b_a).astype(f32)) / GLA_TAU
    log_a = log_a.reshape(B, nc, CHUNK, H, dk)
    cum = jnp.cumsum(log_a, axis=2)
    tot = cum[:, :, -1]
    k_dec = k * jnp.exp(tot[:, :, None] - cum)
    upd = jnp.einsum('bnchk,bnchv->nbhkv', k_dec, v)
    chunk_decay = jnp.exp(tot).transpose(1, 0, 2, 3)

    def step(state, inp):
        d, u = inp
        state = d[..., None] * state + u
        return state, state

    _, states = lax.scan(step, jnp.zeros((B, H, dk, dv), f32), (chunk_decay, upd))
    o = jnp.einsum('bnchk,nbhkv->bnchv', q, states).reshape(B, S, H, dv)
    o = _rms(o, g_o).reshape(B, S, H * dv) * jax.nn.silu(r.astype(f32))
    return o

def _dsa(qc, kvc, idx_k, idx_w, g_qc, w_uq, w_iq, g_kv, w_uv):
    f32 = jnp.float32
    B, S, _ = kvc.shape
    topk = min(DSA_TOPK_MAX, S // 4)
    nb = S // Q_BLOCK
    qc = _rms(qc, g_qc)
    q = (qc @ w_uq).reshape(B, nb, Q_BLOCK, DSA_HEADS, DSA_LAT).transpose(1, 0, 2, 3, 4)
    qi = (qc @ w_iq).reshape(B, nb, Q_BLOCK, IDX_HEADS, IDX_DIM).transpose(1, 0, 2, 3, 4)
    wi = idx_w.reshape(B, nb, Q_BLOCK, IDX_HEADS).transpose(1, 0, 2, 3)
    kv = _rms(kvc, g_kv)
    key_chunk = jnp.arange(S) // CHUNK

    def block(args):
        bi, qb, qib, wb = args
        q_chunk = (bi * Q_BLOCK + jnp.arange(Q_BLOCK)) // CHUNK
        admissible = key_chunk[None, :] <= q_chunk[:, None]
        s_idx = jax.nn.relu(jnp.einsum('bthd,bsd->bths', qib, idx_k))
        score = jnp.einsum('bths,bth->bts', s_idx, wb).astype(f32)
        score = jnp.where(admissible[None], score, -jnp.inf)
        top_val, top_idx = lax.top_k(score, topk)
        valid = top_val > -jnp.inf
        kv_sel = jax.vmap(lambda kvb, ib: kvb[ib])(kv, top_idx)
        logits = jnp.einsum('bthd,btkd->bthk', qb, kv_sel).astype(f32) * (DSA_LAT ** -0.5)
        logits = jnp.where(valid[:, :, None, :], logits, -jnp.inf)
        p = jax.nn.softmax(logits, axis=-1).astype(kv.dtype)
        return jnp.einsum('bthk,btkd->bthd', p, kv_sel)

    o = lax.map(block, (jnp.arange(nb), q, qi, wi))
    o = o.transpose(1, 0, 2, 3, 4).reshape(B, S, DSA_HEADS, DSA_LAT)
    o = jnp.einsum('bshd,hde->bshe', o, w_uv).reshape(B, S, DSA_HEADS * DSA_DV)
    return o.astype(f32)

def _rwkv7(p, mu, w0, w_w2, a0, w_a2, w_g2, k_k, k_a, r_k, ln_g, ln_b):
    f32 = jnp.float32
    B, S, _ = p.shape
    H, N = RWKV_HEADS, RWKV_HEAD
    p = p.astype(f32)
    p = p + (_shift(p) - p) * mu
    r, k, v, w_lr, a_lr, g_lr = _split(p, RWKV_SIZES)
    log_w = -jax.nn.softplus(-(w0 + jnp.tanh(w_lr) @ w_w2)) - 0.5
    decay = jnp.exp(-jnp.exp(log_w))
    a = jax.nn.sigmoid(a0 + a_lr @ w_a2)
    g = jax.nn.sigmoid(g_lr) @ w_g2
    kk = (k * k_k).reshape(B, S, H, N)
    kk = kk * lax.rsqrt(jnp.sum(kk * kk, axis=-1, keepdims=True) + 1e-12)
    k = k * (1.0 + (a - 1.0) * k_a)
    r_h, k_h, v_h, a_h, w_h = [t.reshape(B, S, H, N) for t in (r, k, v, a, decay)]

    def step(state, inp):
        r_t, w_t, k_t, v_t, a_t, b_t = inp
        sa = jnp.einsum('bhij,bhj->bhi', state, a_t)
        state = (state * w_t[:, :, None, :] + sa[..., None] * b_t[:, :, None, :]
                 + v_t[..., None] * k_t[:, :, None, :])
        return state, jnp.einsum('bhij,bhj->bhi', state, r_t)

    xs = tuple(jnp.swapaxes(t, 0, 1) for t in (r_h, w_h, k_h, v_h, -kk, kk * a_h))
    _, y = lax.scan(step, jnp.zeros((B, H, N, N), f32), xs)
    y = jnp.swapaxes(y, 0, 1)
    mean = jnp.mean(y, axis=-1, keepdims=True)
    var = jnp.mean(jnp.square(y - mean), axis=-1, keepdims=True)
    yn = ((y - mean) * lax.rsqrt(var + RWKV_LN_EPS)).reshape(B, S, H * N) * ln_g + ln_b
    bonus = (jnp.sum(r_h * k_h * r_k, axis=-1, keepdims=True) * v_h).reshape(B, S, H * N)
    return (yn + bonus) * g

def _peer(h, w_q, sub_keys, u, v):
    f32 = jnp.float32
    B, S, D = h.shape
    nb = (B * S) // PEER_BLOCK
    hb = h.reshape(nb, PEER_BLOCK, D)

    def block(xb):
        q = (xb @ w_q).reshape(PEER_BLOCK, PEER_HEADS, 2, PEER_QDIM // 2)
        s = jnp.einsum('thpd,hpnd->thpn', q, sub_keys).astype(f32)
        s1, i1 = lax.top_k(s[:, :, 0], PEER_TOPK)
        s2, i2 = lax.top_k(s[:, :, 1], PEER_TOPK)
        cand = (s1[..., :, None] + s2[..., None, :]).reshape(PEER_BLOCK, PEER_HEADS, PEER_TOPK * PEER_TOPK)
        cand_idx = (i1[..., :, None] * PEER_NKEYS + i2[..., None, :]).reshape(PEER_BLOCK, PEER_HEADS, PEER_TOPK * PEER_TOPK)
        top_s, pos = lax.top_k(cand, PEER_TOPK)
        e_idx = jnp.take_along_axis(cand_idx, pos, axis=-1)
        gate = jax.nn.softmax(top_s, axis=-1)
        u_sel = u[e_idx]
        v_sel = v[e_idx]
        act = jax.nn.gelu(jnp.einsum('thkd,td->thk', u_sel, xb).astype(f32), approximate=False)
        return jnp.einsum('thk,thkd->td', (gate * act).astype(xb.dtype), v_sel)

    return lax.map(block, hb).reshape(B, S, D)

def setup_inputs(seed: int = 0) -> dict:
    key = jax.random.key(seed)
    ks = iter(jax.random.split(key, 48))
    L, D = DEPTH, D_MODEL
    Wr = RWKV_HEADS * RWKV_HEAD

    def nrm(shape, scale):
        return jax.random.normal(next(ks), shape, jnp.float32) * scale

    def gain(shape):
        return 1.0 + nrm(shape, 0.02)

    return {
        'x': nrm((BATCH, SEQ, D), 1.0),
        'c': nrm((BATCH, D), 1.0),
        'w_ada': nrm((L, D, 6 * D), 0.5 * D ** -0.5),
        'b_ada': nrm((L, 6 * D), 0.01),
        'g_norm_mix': gain((L, D)),
        'g_norm_ffn': gain((L, D)),
        'w_in': nrm((L, D, IN_WIDTH), D ** -0.5),
        'gla_w_a2': nrm((L, GLA_GATE_RANK, GLA_HEADS * GLA_DK), GLA_GATE_RANK ** -0.5),
        'gla_b_a': nrm((L, GLA_HEADS * GLA_DK), 0.01),
        'gla_g_o': gain((L, GLA_DV)),
        'dsa_g_qc': gain((L, DSA_Q_RANK)),
        'dsa_w_uq': nrm((L, DSA_Q_RANK, DSA_HEADS * DSA_LAT), DSA_Q_RANK ** -0.5),
        'dsa_w_iq': nrm((L, DSA_Q_RANK, IDX_HEADS * IDX_DIM), DSA_Q_RANK ** -0.5),
        'dsa_g_kv': gain((L, DSA_LAT)),
        'dsa_w_uv': nrm((L, DSA_HEADS, DSA_LAT, DSA_DV), DSA_LAT ** -0.5),
        'rwkv_mu': jax.random.uniform(next(ks), (L, RWKV_WIDTH), jnp.float32, 0.2, 0.8),
        'rwkv_w0': nrm((L, Wr), 0.5),
        'rwkv_w_w2': nrm((L, RWKV_W_RANK, Wr), RWKV_W_RANK ** -0.5),
        'rwkv_a0': nrm((L, Wr), 0.1),
        'rwkv_w_a2': nrm((L, RWKV_A_RANK, Wr), RWKV_A_RANK ** -0.5),
        'rwkv_w_g2': nrm((L, RWKV_G_RANK, Wr), RWKV_G_RANK ** -0.5),
        'rwkv_k_k': 0.85 + nrm((L, Wr), 0.02),
        'rwkv_k_a': gain((L, Wr)),
        'rwkv_r_k': nrm((L, RWKV_HEADS, RWKV_HEAD), 0.1),
        'rwkv_ln_g': gain((L, Wr)),
        'rwkv_ln_b': nrm((L, Wr), 0.01),
        'w_branch': nrm((L, N_BRANCH, BRANCH_W, D), BRANCH_W ** -0.5),
        'w_out': nrm((L, D, D), D ** -0.5),
        'peer_w_q': nrm((L, D, PEER_HEADS * PEER_QDIM), D ** -0.5),
        'peer_keys': nrm((L, PEER_HEADS, 2, PEER_NKEYS, PEER_QDIM // 2), (PEER_QDIM // 2) ** -0.5),
        'peer_u': nrm((L, PEER_N, D), D ** -0.5),
        'peer_v': nrm((L, PEER_N, D), 0.5),
        'g_final': gain((D,)),
    }

def reference(x, c, w_ada, b_ada, g_norm_mix, g_norm_ffn, w_in, gla_w_a2, gla_b_a, gla_g_o,
              dsa_g_qc, dsa_w_uq, dsa_w_iq, dsa_g_kv, dsa_w_uv,
              rwkv_mu, rwkv_w0, rwkv_w_w2, rwkv_a0, rwkv_w_a2, rwkv_w_g2, rwkv_k_k, rwkv_k_a, rwkv_r_k,
              rwkv_ln_g, rwkv_ln_b, w_branch, w_out, peer_w_q, peer_keys, peer_u, peer_v, g_final):
    B, S, D = x.shape
    cond = jax.nn.silu(c)
    for l in range(DEPTH):
        mod = cond @ w_ada[l] + b_ada[l]
        sh_m, sc_m, gt_m, sh_f, sc_f, gt_f = [m[:, None, :] for m in jnp.split(mod, 6, axis=-1)]
        h = _rms(x, g_norm_mix[l]) * (1.0 + sc_m) + sh_m
        gq, gk, gv, galr, gr, qc, kvc, ik, iw, prw, gates = _split(h @ w_in[l], IN_SIZES)
        y_a = _gla(gq, gk, gv, galr, gr, gla_w_a2[l], gla_b_a[l], gla_g_o[l])
        y_b = _dsa(qc, kvc, ik, iw, dsa_g_qc[l], dsa_w_uq[l], dsa_w_iq[l], dsa_g_kv[l], dsa_w_uv[l])
        y_c = _rwkv7(prw, rwkv_mu[l], rwkv_w0[l], rwkv_w_w2[l], rwkv_a0[l], rwkv_w_a2[l], rwkv_w_g2[l],
                     rwkv_k_k[l], rwkv_k_a[l], rwkv_r_k[l], rwkv_ln_g[l], rwkv_ln_b[l])
        g_a, g_b, g_c = jnp.split(jax.nn.sigmoid(gates), N_BRANCH, axis=-1)
        merged = (g_a * (y_a.astype(x.dtype) @ w_branch[l, 0])
                  + g_b * (y_b.astype(x.dtype) @ w_branch[l, 1])
                  + g_c * (y_c.astype(x.dtype) @ w_branch[l, 2]))
        x = x + gt_m * (merged @ w_out[l])
        h2 = _rms(x, g_norm_ffn[l]) * (1.0 + sc_f) + sh_f
        x = x + gt_f * _peer(h2, peer_w_q[l], peer_keys[l], peer_u[l], peer_v[l])
    return _rms(x, g_final)


_drawn_inputs = setup_inputs


def setup_inputs(seed=0):
    import zlib

    import numpy as np

    out = dict(_drawn_inputs(seed))
    spreads = {}
    factors = {'b_ada': 2.9,
     'g_norm_mix': 3.862,
     'g_norm_ffn': 16.094,
     'gla_b_a': 22.35,
     'gla_g_o': 6.92,
     'dsa_g_qc': 7.732,
     'dsa_g_kv': 8.0,
     'rwkv_a0': 4.826,
     'rwkv_k_k': 64.0,
     'rwkv_k_a': 6.784,
     'rwkv_ln_g': 50.247,
     'rwkv_ln_b': 64.0,
     'g_final': 7.675}
    for name, (base, spread) in spreads.items():
        noise = np.random.default_rng([zlib.crc32(name.encode()), seed]).standard_normal(out[name].shape)
        drawn = base * np.exp(spread * noise) if base else spread * noise
        out[name] = __import__('jax').numpy.asarray(drawn.astype(out[name].dtype))
    for name, factor in factors.items():
        out[name] = (out[name] * factor).astype(out[name].dtype)
    return out
```

```python
from contextlib import ExitStack

import numpy as np

import concourse.bass as bass
from concourse import mybir

F32 = mybir.dt.float32
U32 = mybir.dt.uint32
ALU = mybir.AluOpType
ACT = mybir.ActivationFunctionType
AX = mybir.AxisListType

P = 128
L, S, D = 2, 512, 1024
TT, KD = S // P, D // P
NB = 512
IN_W = 6868
GQ, GV, GA, QC, PR, GATES = 0, 512, 1024, 1552, 2004, 3796
CH, NCH = 64, S // 64
TOPK = 128
NEG, MARK, DROP = -3.0e38, -3.3e38, -1.0e30
EPS, LN_EPS, KK_EPS = 1e-6, 64e-5, 1e-12
KAPPA = float(np.exp(-0.5))
EH, ET, NK, NE = 8, 16, 128, 16384
SLOTS = EH * ET
RING = 2
GRP = 8

COLS = {}
_at = 0
for _n, _w in (("b_ada", 48), ("g_norm_mix", 8), ("g_norm_ffn", 8), ("gla_b_a", 2), ("gla_g_o", 1), ("dsa_g_qc", 2),
               ("dsa_g_kv", 1), ("rwkv_mu", 14), ("rwkv_w0", 4), ("rwkv_a0", 4), ("rwkv_k_k", 4), ("rwkv_k_a", 4),
               ("rwkv_r_k", 4), ("rwkv_ln_g", 4), ("rwkv_ln_b", 4)):
    COLS[_n] = _at
    _at += _w
NCOL = _at

CONST = {}
_at = 0
for _n, _w in (("ident", P), ("ones", P), ("bones", P), ("tri", 2 * P), ("lvl", 7 * P), ("m64", S), ("m128", S), ("iota", ET)):
    CONST[_n] = (_at, _at + _w)
    _at += _w
NCONST = _at

SW_GA, SW_WA, SW_G2, SW_KEY, SW_N = 0, 256, 768, 1280, 2304

BLOCKS = ([("ada", i) for i in range(12)] + [("rw", i) for i in (3, 1, 0, 2)] + [("gla", 0), ("gla", 1), ("gla", 2)]
          + [("dsa", 0), ("up", 0)] + [("merge", m) for m in range(8)] + [("out", 0), ("out", 1)] + [("pq", 0), ("pq", 1)])
RW_W = (512, 512, 512, 256)


class Banks:

    def __init__(self, sem, prefix, order):
        self.n = {name: i for i, name in enumerate(order)}
        assert len(self.n) == len(order)
        self.filled_sems = [sem(f"{prefix}_filled{b}") for b in range(8)]
        self.freed_sems = [sem(f"{prefix}_freed{b}") for b in range(8)]
        self.per = [len(range(b, len(order), 8)) for b in range(8)]

    def bank(self, name):
        return self.n[name] % 8

    def filled(self, name):
        return self.filled_sems[self.bank(name)]

    def freed(self, name):
        return self.freed_sems[self.bank(name)]

    def full(self, name, lap):
        b = self.bank(name)
        return self.filled_sems[b], lap * self.per[b] + (self.n[name] // 8 + 1)

    def free(self, name, lap):
        b = self.bank(name)
        return self.freed_sems[b], lap * self.per[b] + (self.n[name] // 8 + 1)


def layer_banks():
    o = ["mod", ("ss", 0)]
    o += [("rp", c) for c in (12, 13)] + [("z", c) for c in range(4)] + [("za", c) for c in range(4)]
    o += [("rp", c) for c in (4, 5, 6, 7, 0, 1, 2, 3, 8, 9, 10, 11)]
    o += [("kkn", c) for c in range(4)] + [("bon", c) for c in range(4)]
    for t in range(TT):
        o += [("ab", t, p, q) for q in range(2) for p in range(2)] + [("kb", t, p, q) for q in range(2) for p in range(2)]
        o += [("tm", t, w) for w in range(3)] + [("m0", t, q) for q in range(2)]
        for lv in range(1, 7):
            o += [("u", t, lv, q) for q in range(2)]
            for q in range(2):
                o += ([("tu", t, lv, q)] if lv < 6 else []) + [("ut", t, lv, q)]
        o += [("g", t, 0), ("g", t, 1), ("sa", t), ("y", t, 0), ("y", t, 1)] + ([("s", t)] if t < 3 else [])
    for c in range(4):
        o += [("mu", c)]
    for c in range(4):
        o += [("var", c)]
    for c in range(4):
        o += [("g2", c)]
    o += [("gq", c) for c in range(4)] + [("gv", t) for t in range(TT)] + [("ga", 0)] + [("gz", c) for c in range(2)]
    o += [("gr", c) for c in range(4)] + [("kt", c) for c in range(2)] + [("upd", n) for n in range(NCH)]
    o += [("o", h) for h in range(4)] + [("on", h) for h in range(4)]
    o += [("qc", c) for c in range(4)] + [("iw", 0), ("qn", 0), ("kn", 0)] + [("iq", c) for c in range(2)]
    o += [("ix", b, h) for b in range(1, 4) for h in range(4)] + [("uq", h) for h in range(8)] + [("kvt", 0)]
    for i in range(36):
        o += ([("lg", i)] if i < 32 else []) + ([("pt", i - 2)] if 2 <= i < 34 else [])
        o += [("cx", (i - 4) // 4)] if i >= 4 and i % 4 == 3 else []
    o += [("uv", c) for c in range(4)]
    for m in range(KD):
        o += [x for r in range(3) for x in (("gt", m, r), ("br", m, r))]
    o += [("wo", m) for m in range(KD)] + [("ss", 1)] + [("pq", h) for h in range(EH)]
    o += [("h2", t, h) for t in range(TT) for h in range(2)]
    return o


TILE_BANKS = [("sc", p, q) for q in range(2) for p in range(2)] + [("acc", 0), ("acc", 1), ("xt", 0), ("xt", 1)]


def trunk(nc, fixed, cols, consts, x_t, w_ada, w_in, w_small, w_uq, w_iq, w_uv, w_merge, w_out, w_pq, uv, out,
          depth=L, stop=None):
    ctx = ExitStack()
    with ctx:
        def sb(name, n, dt=F32):
            return ctx.enter_context(nc.sbuf_tensor(name, [P, n], dt))

        def sem(name):
            return ctx.enter_context(nc.semaphore(name))

        psum = [ctx.enter_context(nc.psum_tensor(f"bank{b}", [P, NB], F32)) for b in range(8)]

        def v3(ap, c):
            return ap.rearrange("p (c t) -> p c t", c=c)

        con = sb("con", NCONST)
        xT = v3(sb("xT", KD * S)[:], KD)
        hT = v3(sb("hT", KD * S)[:], KD)
        allcols = sb("allcols", L * NCOL)
        col = sb("col", NCOL)
        fix = sb("fix", 2 * KD)
        sc = sb("sc", 64)
        cond = sb("cond", KD)
        modc = sb("modc", 48)
        gain = sb("gain", 2 * KD)
        omka = sb("omka", 4)
        sw = sb("sw", SW_N)
        rstd = sb("rstd", S)
        SLOT = 36 * P
        REG = 37700
        reg = sb("reg", REG)
        ring = [reg[:, i * SLOT:(i + 1) * SLOT] for i in range(RING)]
        base = RING * SLOT
        ya, yb, yc = (v3(reg[:, base + i * 2048:base + (i + 1) * 2048], 4) for i in range(3))
        base += 3 * 2048

        def at(o, n, dt=None):
            assert base + o + n <= REG, (base + o + n, REG)
            r = reg[:, base + o:base + o + n]
            return r if dt is None else r.bitcast(dt)

        def const(name):
            a, b = CONST[name]
            return con[:, a:b]

        ident, ones, bones = const("ident"), const("ones"), const("bones")
        tri, lvl, m64, m128, iota16 = const("tri"), v3(const("lvl"), 7), const("m64"), const("m128"), const("iota")

        def cl(name, i=0, n=1, p0=0, p1=P):
            return col[p0:p1, COLS[name] + i:COLS[name] + i + n]

        r_pt = [at(19456 + i * 513, 513) for i in range(2)]
        r_r, r_k, r_v = (v3(at(i * 2048, 2048), 4) for i in range(3))
        r_lr, r_gl = at(6144, 512), at(6656, 512)
        r_sg, r_cs, r_a = (v3(at(7168 + i * 2048, 2048), 4) for i in range(3))
        r_kk = v3(at(13312, 2048), 4)
        r_x = at(15360, 4096)
        r_t1, r_t2 = v3(r_x[:, 0:2048], 4), v3(r_x[:, 2048:4096], 4)
        r_ar = r_x.rearrange("p (c t w s) -> p c t w s", c=4, t=4, w=2)
        r_bon, r_y = yb, ya
        r_tm = v3(at(19456, 1536), 3)
        r_g, r_sa = v3(at(20992, 512), 8), v3(at(21504, 512), 8)
        r_s = v3(at(22016, 256), 4)
        r_mid, r_f = at(22272, 16), at(22288, 12)
        r_ab = v3(at(7168, 2048), 8)
        r_ak = v3(at(9216, 2048), 8)
        r_tt, r_tn = v3(at(11264, 1024), 8), v3(at(0, 1024), 8)
        r_u, r_m = v3(at(1024, 1024), 8), v3(at(12288, 1024), 8)
        g_q, g_k = v3(at(0, 1024), 2), v3(at(1024, 1024), 2)
        g_v = v3(at(2048, 2048), 4)
        g_a, g_r = at(4096, 512), v3(at(4608, 2048), 4)
        g_la, g_cum, g_ab = (v3(at(6656 + i * 1024, 1024), 2) for i in range(3))
        g_tm = v3(at(9728, 1024), 4)
        g_st = at(10752, 2048).rearrange("p (n c v) -> p n c v", n=NCH, c=2)
        g_o, g_o2 = v3(at(12800, 2048), 4), v3(at(14848, 2048), 4)
        g_tot, g_dec = v3(at(16896, 16), 2), v3(at(16912, 16), 2)
        d_qc, d_kv, d_ik = v3(at(0, 1024), 2), at(1024, 512), at(1536, 512)
        d_qi, d_kt = v3(at(2048, 1024), 2), v3(at(3072, 512), 4)
        d_sq = v3(at(3584, 1536), 3)
        d_q = v3(at(5120, 4096), 8)
        d_cx = v3(at(9216, 4096), 8)
        d_nm = v3(at(13312, 2048), 4)
        d_rl = [at(15360 + i * 512, 512) for i in range(4)]
        d_pt = [at(17408 + i * 512, 512) for i in range(4)]
        d_iw = v3(at(19456, 16), 4)
        d_m8 = at(19472, 8)
        d_mx, d_sm, d_n = at(19480, 32), at(19512, 32), at(19544, 32)
        m_g = [at(i * 512, 512) for i in range(2)]
        m_t = at(1024, 512)
        m_o = v3(at(1536, 4096), 8)
        e_row = [reg[:, i * 2048:(i + 1) * 2048] for i in range(GRP)]

        def ep(o, n, dt=None):
            assert GRP * 2048 + o + n <= REG
            r = reg[:, GRP * 2048 + o:GRP * 2048 + o + n]
            return r if dt is None else r.bitcast(dt)

        e_q, e_h = v3(ep(0, 4096), 8), v3(ep(4096, 4096), 4)
        e_qc, e_hc = v3(ep(8192, 1024), 8), ep(9216, 1024)
        e_s = v3(ep(10240, 2048), 16)
        e_c = v3(ep(12288, 2048), 8)
        e_oh = ep(14336, 2048)
        e_oh2 = ep(16384, 2048)
        e_v = v3(ep(18432, 256), 16)
        e_i = v3(ep(18688, 256, U32), 16)
        e_if = v3(ep(18944, 256), 16)
        e_top, e_pos = v3(ep(19200, 128), 8), v3(ep(19328, 128, U32), 8)
        e_pa, e_paf = ep(19456, 128, U32), ep(19584, 128)
        e_pb, e_pbf = ep(19712, 128, U32), ep(19840, 128)
        e_n1, e_n2 = ep(19968, 128), ep(20096, 128)
        e_ex, e_gate = v3(ep(20224, 128), 8), ep(20352, 128)
        e_sum = ep(20480, 8)
        e_idx = sb("e_idx", SLOTS, U32)
        e_ic = sb("e_ic", GRP, U32)
        e_diag = v3(sb("e_diag", GRP * P)[:], GRP)
        e_dot, e_ge, e_wg, e_gc = (ep(20488 + i * 8, 8) for i in range(4))
        e_acc = e_oh
        e_off = sb("e_off", 1)
        zeros = sb("zeros", P)

        loaded = sem("loaded")
        landed = [sem(f"block_landed{i}") for i in range(RING)]
        used = [sem(f"block_used{i}") for i in range(RING)]
        nblock = [len(range(i, len(BLOCKS), RING)) for i in range(RING)]
        small_landed = sem("small_landed")
        joined = sem("joined")
        stored = sem("stored")
        B = Banks(sem, "layer", layer_banks())
        T = Banks(sem, "tile", TILE_BANKS)

        class Sig:
            def __init__(self, name, n):
                self.sem, self.n = sem(name), n

            def at(self, lap, k=None):
                return self.sem, lap * self.n + (self.n if k is None else k)

        G = {n: Sig(n, k) for n, k in (
            ("squares", 2), ("h_ready", 2 * KD), ("cond_ready", 1),
            ("pt_ready", 14), ("pt_used", 14), ("mixed", 14), ("lr_ready", 2), ("sig_ready", 2),
            ("kk_raw", 1), ("kk_sq", 1), ("kk_rs", 4), ("bon_in", 1), ("cs_done", 1), ("eprev", 1), ("ep", 1), ("em", 1),
            ("f_ready", 1), ("ar_half", 1), ("rk_ready", 1), ("s_zero", 1),
            ("ab_masked", 32), ("tm_copied", 12), ("level_masked", 7 * TT), ("t_updated", 7 * TT * 2),
            ("u_copied", 6 * TT * 2), ("g_copied", 2 * TT), ("sa_copied", TT), ("y_copied", 2 * TT), ("state", TT),
            ("y_cent", 4), ("y_sq", 4), ("y_rs", 4),
            ("gla_in", 13), ("gz_abs", 2), ("gz_exp", 2), ("gla_la", 1), ("gla_dec", 2), ("gla_kd", 1), ("kt_copied", 2),
            ("gla_state", NCH), ("o_sq", 4), ("o_rs", 4),
            ("dsa_in", 5), ("dsa_sq", 2), ("dsa_rs", 2), ("dsa_n", 2), ("iq_copied", 2), ("relu", 12), ("relu_used", 12),
            ("uq_copied", 8), ("kvt_copied", 1), ("lg_max", 32), ("lg_exp", 32), ("p_ready", 32), ("pt_copied", 32), ("cx_copied", 8),
            ("gate", 24), ("gate_used", 24), ("merged", 8), ("x_mixed", KD),
            ("pq_copied", EH), ("h2_copied", 2 * TT))}
        E_ = {n: Sig(n, k) for n, k in (
            ("tile_in", 1), ("scored", 4), ("routed", 1), ("soft_in", 1), ("soft", 1), ("acc_copied", 1), ("tile_out", 1),
            ("idx_used", 1))}
        rows_landed = [sem(f"rows_landed{s}") for s in range(GRP)]
        rows_used = [sem(f"rows_used{s}") for s in range(GRP)]
        dots = [sem(f"dot{s}") for s in range(GRP)]
        diags = [sem(f"diag{s}") for s in range(GRP)]
        idx_ready = sem("idx_ready")
        passed = sem("passed")
        const_set = sem("const_set")
        rstd_ready = sem("rstd_ready")
        scaled = sem("scaled")
        stored_mm = sem("final_sum")

        NJOIN = 7

        def join(eng, lap, k, n=NJOIN):
            eng.sem_inc(passed, 1)
            eng.drain().then_inc(joined, 1)
            eng.wait_ge(joined, 3 * (lap * n + k - 1) + 1)
            eng.sem_inc(passed, 1)

        def block_at(name):
            i = BLOCKS.index(name)
            return ring[i % RING], i % RING, i // RING + 1

        def stop_at(name):
            return stop is not None and stop == name

        def bc(ap, shape):
            return ap.to_broadcast(shape)

        block = ctx.enter_context(nc.Block())

        @block.sync
        def _(sp):
            for dst, src in ((con[:], consts), (allcols[:], cols), (fix[:], fixed),
                             (xT, x_t.rearrange("(k p) t -> p k t", p=P))):
                sp.dma_start(dst, src).then_inc(loaded, 16)
            for s_ in B.freed_sems + T.freed_sems + used + rows_used + [joined]:
                sp.sem_inc(s_, 1)
            with sp.Fori(0, depth) as l:
                sp.wait_ge(joined, 3 * (l * NJOIN) + 1)
                sp.sem_inc(passed, 1)

                def fetch(name):
                    dst, slot, turn = block_at(name)
                    kind, i = name

                    def part(to, src):
                        sp.dma_start(to, src).then_inc(landed[slot], 16)
                    sp.wait_ge(used[slot], l * nblock[slot] + turn)
                    sp.sem_inc(passed, 1)
                    if kind == "ada":
                        part(v3(dst[:, 0:4096], 8), w_ada.rearrange("l (k p) n -> l p k n", p=P)[bass.ds(l, 1), :, :, i * 512:(i + 1) * 512].squeeze(0))
                    elif kind in ("rw", "gla", "dsa"):
                        c0, w = {"rw": lambda: (PR + 512 * i, RW_W[i]), "gla": lambda: ((GQ, 512), (GV, 512), (GA, 528))[i],
                                 "dsa": lambda: (QC, 452)}[kind]()
                        src = w_in.rearrange("l (k p) n -> l p k n", p=P)[bass.ds(l, 1), :, :, c0:c0 + w].squeeze(0)
                        part(v3(dst[:, 0:8 * w], 8), src)
                    elif kind == "up":
                        part(v3(dst[:, 0:2048], 2), w_uq.rearrange("l (k p) n -> l p k n", p=P)[bass.ds(l, 1)].squeeze(0))
                        part(v3(dst[:, 2048:2560], 2), w_iq.rearrange("l (k p) n -> l p k n", p=P)[bass.ds(l, 1)].squeeze(0))
                        part(v3(dst[:, 2560:3072], 8), w_uv.rearrange("l h p e -> l p h e")[bass.ds(l, 1)].squeeze(0))
                    elif kind == "merge":
                        part(dst, w_merge.rearrange("l m p n -> m l p n")[i, bass.ds(l, 1)].squeeze(0))
                    else:
                        w = w_out if kind == "out" else w_pq
                        part(v3(dst[:, 0:4096], 8), w.rearrange("l (k p) n -> l p k n", p=P)[bass.ds(l, 1), :, :, i * 512:(i + 1) * 512].squeeze(0))

                for n, name in enumerate(BLOCKS):
                    if n == 3:
                        sp.dma_start(sw[:], w_small[bass.ds(l, 1)].squeeze(0)).then_inc(small_landed, 16)
                    fetch(name)
            for k in range(KD):
                sp.wait_ge(stored, k + 1)
                sp.dma_start(out[k * P:(k + 1) * P, :], hT[:, k, :]).then_inc(loaded, 16)
            sp.wait_ge(loaded, 16 * (4 + KD))

        LANDED = {name: sum(3 if b == ("up", 0) else 1 for b in BLOCKS[i % RING:i + 1:RING]) for i, name in enumerate(BLOCKS)}
        LAND_N = [sum(3 if b == ("up", 0) else 1 for b in BLOCKS[i::RING]) for i in range(RING)]

        @block.tensor
        def _(pe):
            mm = nc.tensor.matmul

            def arrive(name, l):
                dst, slot, _ = block_at(name)
                pe.wait_ge(landed[slot], 16 * (l * LAND_N[slot] + LANDED[name]))
                return dst

            def leave(ins, name):
                ins.then_inc(used[block_at(name)[1]], 1)

            def opened(name, l, banks=B):
                pe.wait_ge(*banks.free(name, l))
                return psum[banks.bank(name)]

            def need(sig, l, k=None):
                pe.wait_ge(*G[sig].at(l, k))

            def summed(name, l, parts, n=NB):
                ps = opened(name, l)
                for i, (a, b) in enumerate(parts):
                    last = mm(ps[:, 0:n], a, b, start=(i == 0), stop=(i == len(parts) - 1))
                last.then_inc(B.filled(name), 1)
                return last

            def norm(l, w):
                need("squares", l, w + 1)
                summed(("ss", w), l, [(ones, hT[:, k, :]) for k in range(KD)])

            pe.wait_ge(loaded, 64)
            with pe.Fori(0, depth) as l:
                if True:
                    need("cond_ready", l)
                    ps = opened("mod", l)
                    for i in range(12):
                        w = v3(arrive(("ada", i), l)[:, 0:4096], 8)
                        for j in range(4):
                            for k in range(KD):
                                last = mm(ps[:, 4 * i + j:4 * i + j + 1], w[:, k, j * P:(j + 1) * P], cond[:, k:k + 1],
                                          start=(k == 0), stop=(k == KD - 1))
                        leave(last, ("ada", i))
                    pe.drain().then_inc(B.filled("mod"), 1)
                norm(l, 0)
                need("h_ready", l, KD)

                def block_of(name, l, jobs, width):
                    w = v3(arrive(name, l)[:, 0:8 * width], 8)
                    for i, (job, j, m) in enumerate(jobs):
                        ps = opened(job, l)
                        for k in range(KD):
                            last = mm(ps[0:m, :], w[:, k, j:j + m], hT[:, k, :], start=(k == 0), stop=(k == KD - 1))
                        if i == len(jobs) - 1:
                            leave(last, name)
                            pe.drain().then_inc(B.filled(job), 1)
                        else:
                            last.then_inc(B.filled(job), 1)

                block_of(("rw", 3), l, [(("rp", 12), 0, P), (("rp", 13), P, P)], 256)
                pe.wait_ge(small_landed, 16 * (l + 1))
                need("lr_ready", l, 1)
                for c in range(4):
                    ps = opened(("z", c), l)
                    mm(ps[:, :], sw[0:64, SW_WA + c * P:SW_WA + (c + 1) * P], r_lr[0:64, :], start=True, stop=True).then_inc(B.filled(("z", c)), 1)
                for c in range(4):
                    ps = opened(("za", c), l)
                    mm(ps[:, :], sw[64:P, SW_WA + c * P:SW_WA + (c + 1) * P], r_lr[64:P, :], start=True, stop=True).then_inc(B.filled(("za", c)), 1)

                for i, c0 in ((1, 4), (0, 0), (2, 8)):
                    block_of(("rw", i), l, [(("rp", c0 + j), j * P, P) for j in range(4)], 512)
                need("kk_sq", l)
                for c in range(4):
                    summed(("kkn", c), l, [(bones, r_t1[:, c, :])])
                need("bon_in", l)
                for c in range(4):
                    summed(("bon", c), l, [(bones, r_t2[:, c, :])])
                need("rk_ready", l)
                need("s_zero", l)
                for t in range(TT):
                    ts = slice(t * P, (t + 1) * P)
                    for nm, src in (("ab", r_kk), ("kb", r_k)):
                        for q in range(2):
                            for p in range(2):
                                ps = v3(opened((nm, t, p, q), l)[:, :], 2)
                                lo, hi = 64 * p, 64 * p + 64
                                for i in range(2):
                                    c = 2 * q + i
                                    last = mm(ps[:, i, :], src[lo:hi, c, ts], r_ar[lo:hi, c, t, :, :].rearrange("p w s -> p (w s)"),
                                              start=True, stop=True)
                                last.then_inc(B.filled((nm, t, p, q)), 1)
                    for wi, src in enumerate((r_kk, r_k, r_v)):
                        ps = opened(("tm", t, wi), l)
                        for c in range(4):
                            last = nc.tensor.transpose(ps[:, c * P:(c + 1) * P], src[:, c, ts], ident)
                        last.then_inc(B.filled(("tm", t, wi)), 1)
                    need("level_masked", l, 7 * t + 1)
                    for q in range(2):
                        ps = opened(("m0", t, q), l)
                        for i in range(4):
                            last = nc.tensor.transpose(ps[:, i * P:(i + 1) * P], r_m[:, 4 * q + i, :], ident)
                        last.then_inc(B.filled(("m0", t, q)), 1)
                    for lv in range(1, 7):
                        for q in range(2):
                            need("level_masked", l, 7 * t + lv + 1)
                            need("t_updated", l, 14 * t + 2 * (lv - 1) + q + 1)
                            ps = opened(("u", t, lv, q), l)
                            for i in range(4):
                                h = 4 * q + i
                                last = mm(ps[:, i * P:(i + 1) * P], r_m[:, h, :], r_tn[:, h, :], start=True, stop=True)
                            last.then_inc(B.filled(("u", t, lv, q)), 1)
                        for q in range(2):
                            need("u_copied", l, 12 * t + 2 * (lv - 1) + q + 1)
                            if lv < 6:
                                ps = opened(("tu", t, lv, q), l)
                                for i in range(4):
                                    h = 4 * q + i
                                    last = mm(ps[:, i * P:(i + 1) * P], r_tt[:, h, :], r_u[:, h, :], start=True, stop=True)
                                last.then_inc(B.filled(("tu", t, lv, q)), 1)
                            ps = opened(("ut", t, lv, q), l)
                            for i in range(4):
                                h = 4 * q + i
                                last = mm(ps[:, i * P:(i + 1) * P], r_u[:, h, :], r_tt[:, h, :], start=True, stop=True)
                            last.then_inc(B.filled(("ut", t, lv, q)), 1)
                    need("tm_copied", l, 3 * t + 3)
                    need("ab_masked", l, 8 * t + 8)
                    if t:
                        need("state", l, t)
                    for p in range(2):
                        ps = opened(("g", t, p), l)
                        lo, hi = 64 * p, 64 * p + 64
                        for c in range(4):
                            h = 2 * c + p
                            mm(ps[:, c * 64:c * 64 + 64], r_ar[lo:hi, c, t, 0, :], r_s[lo:hi, c, :], start=True, stop=False)
                            last = mm(ps[:, c * 64:c * 64 + 64], r_ak[:, h, 0:P], r_tm[:, 2, h * 64:h * 64 + 64], start=False, stop=True)
                        last.then_inc(B.filled(("g", t, p)), 1)
                    need("t_updated", l, 14 * (t + 1))
                    need("g_copied", l, 2 * (t + 1))
                    ps = opened(("sa", t), l)
                    for h in range(8):
                        last = mm(ps[:, h * 64:h * 64 + 64], r_tt[:, h, :], r_g[:, h, :], start=True, stop=True)
                    last.then_inc(B.filled(("sa", t)), 1)
                    need("sa_copied", l, t + 1)
                    for p in range(2):
                        ps = opened(("y", t, p), l)
                        lo, hi = 64 * p, 64 * p + 64
                        pe.sem_inc(passed, 1)
                        for c in range(4):
                            h = 2 * c + p
                            o = ps[lo:hi, c * P:(c + 1) * P]
                            mm(o, r_s[lo:hi, c, :], r_ar[lo:hi, c, t, 1, :], start=True, stop=False)
                            mm(o, r_sa[:, h, :], r_ab[:, h, P:2 * P], start=False, stop=False)
                            last = mm(o, r_tm[:, 2, h * 64:h * 64 + 64], r_ak[:, h, P:2 * P], start=False, stop=True)
                        last.then_inc(B.filled(("y", t, p)), 1)
                    if t < 3:
                        ps = opened(("s", t), l)
                        for h in range(8):
                            p, c = h % 2, h // 2
                            o = ps[64 * p:64 * p + 64, c * 64:c * 64 + 64]
                            mm(o, r_tm[:, 0, h * 64:h * 64 + 64], r_sa[:, h, :], start=True, stop=False)
                            last = mm(o, r_tm[:, 1, h * 64:h * 64 + 64], r_tm[:, 2, h * 64:h * 64 + 64], start=False, stop=True)
                        last.then_inc(B.filled(("s", t)), 1)
                need("y_copied", l)
                for c in range(4):
                    summed(("mu", c), l, [(bones, r_y[:, c, :])])
                for c in range(4):
                    need("y_sq", l, c + 1)
                    summed(("var", c), l, [(bones, r_t1[:, c, :])])
                for c in range(4):
                    summed(("g2", c), l, [(sw[:, SW_G2 + c * P:SW_G2 + (c + 1) * P], r_gl)])
                join(pe, l, 2)

                block_of(("gla", 0), l, [(("gq", c), c * P, P) for c in range(4)], 512)
                w = v3(arrive(("gla", 1), l)[:, 0:4096], 8)
                for t in range(TT):
                    ps = opened(("gv", t), l)
                    for k in range(KD):
                        last = mm(ps[:, :], hT[:, k, t * P:(t + 1) * P], w[:, k, :], start=(k == 0), stop=(k == KD - 1))
                    if t == TT - 1:
                        leave(last, ("gla", 1))
                        pe.drain().then_inc(B.filled(("gv", t)), 1)
                    else:
                        last.then_inc(B.filled(("gv", t)), 1)
                w = v3(arrive(("gla", 2), l)[:, 0:4224], 8)
                ps = opened(("ga", 0), l)
                for k in range(KD):
                    last = mm(ps[0:16, :], w[:, k, 0:16], hT[:, k, :], start=(k == 0), stop=(k == KD - 1))
                last.then_inc(B.filled(("ga", 0)), 1)
                need("gla_in", l, 9)
                for c in range(2):
                    ps = opened(("gz", c), l)
                    mm(ps[:, :], sw[0:16, SW_GA + c * P:SW_GA + (c + 1) * P], g_a[0:16, :], start=True, stop=True).then_inc(B.filled(("gz", c)), 1)
                block_of_jobs = [(("gr", c), 16 + c * P, P) for c in range(4)]
                for i, (job, j, m) in enumerate(block_of_jobs):
                    ps = opened(job, l)
                    for k in range(KD):
                        last = mm(ps[:, :], w[:, k, j:j + m], hT[:, k, :], start=(k == 0), stop=(k == KD - 1))
                    if i == 3:
                        leave(last, ("gla", 2))
                        pe.drain().then_inc(B.filled(job), 1)
                    else:
                        last.then_inc(B.filled(job), 1)
                need("gla_kd", l)
                for c in range(2):
                    ps = opened(("kt", c), l)
                    for t in range(TT):
                        last = nc.tensor.transpose(ps[:, t * P:(t + 1) * P], g_k[:, c, t * P:(t + 1) * P], ident)
                    last.then_inc(B.filled(("kt", c)), 1)
                need("kt_copied", l)
                need("gla_in", l, 13)
                for n in range(NCH):
                    lo, hi = 64 * (n % 2), 64 * (n % 2) + 64
                    ps = opened(("upd", n), l)
                    for c in range(2):
                        last = mm(ps[:, c * 256:(c + 1) * 256], g_tm[lo:hi, n // 2, c * P:(c + 1) * P],
                                  g_v[lo:hi, n // 2, c * 256:(c + 1) * 256], start=True, stop=True)
                    last.then_inc(B.filled(("upd", n)), 1)
                need("gla_state", l)
                for h in range(4):
                    lo, hi = 64 * (h % 2), 64 * (h % 2) + 64
                    ps = opened(("o", h), l)
                    for n in range(NCH):
                        last = mm(ps[:, n * 64:n * 64 + 64], g_st[lo:hi, n, h // 2, :], g_q[lo:hi, h // 2, n * 64:n * 64 + 64],
                                  start=True, stop=True)
                    last.then_inc(B.filled(("o", h)), 1)
                for h in range(4):
                    need("o_sq", l, h + 1)
                    summed(("on", h), l, [(ones, g_o2[:, h, :])])
                join(pe, l, 3)

                w = v3(arrive(("dsa", 0), l)[:, 0:8 * 452], 8)
                for c in range(3):
                    ps = opened(("qc", c), l)
                    for k in range(KD):
                        last = mm(ps[:, :], w[:, k, c * P:(c + 1) * P], hT[:, k, :], start=(k == 0), stop=(k == KD - 1))
                    last.then_inc(B.filled(("qc", c)), 1)
                ps = opened(("qc", 3), l)
                for p in range(2):
                    for k in range(KD):
                        last = mm(ps[64 * p:64 * p + 64, :], w[:, k, 384:448], hT[:, k, :], start=(k == 0), stop=(k == KD - 1))
                last.then_inc(B.filled(("qc", 3)), 1)
                ps = opened(("iw", 0), l)
                for t in range(TT):
                    for k in range(KD):
                        last = mm(ps[:, t * 4:t * 4 + 4], hT[:, k, t * P:(t + 1) * P], w[:, k, 448:452], start=(k == 0), stop=(k == KD - 1))
                leave(last, ("dsa", 0))
                pe.drain().then_inc(B.filled(("iw", 0)), 1)
                need("dsa_sq", l, 1)
                summed(("qn", 0), l, [(ones, d_sq[:, c, :]) for c in range(2)])
                need("dsa_sq", l, 2)
                summed(("kn", 0), l, [(ones, d_sq[:, 2, :])])
                up = arrive(("up", 0), l)
                w_q, w_i, w_v = v3(up[:, 0:2048], 2), v3(up[:, 2048:2560], 2), v3(up[:, 2560:3072], 8)
                need("dsa_n", l, 1)
                for c in range(2):
                    summed(("iq", c), l, [(w_i[:, k, c * P:(c + 1) * P], d_qc[:, k, :]) for k in range(2)])
                need("iq_copied", l)
                need("dsa_in", l, 5)
                for b in range(1, 4):
                    for h in range(4):
                        lo, hi, w = 64 * (h % 2), 64 * (h % 2) + 64, P * (b + 1)
                        ps = opened(("ix", b, h), l)
                        mm(ps[:, 0:w], d_qi[lo:hi, h // 2, b * P:(b + 1) * P], d_ik[lo:hi, 0:w], start=True, stop=True)\
                            .then_inc(B.filled(("ix", b, h)), 1)
                for h in range(8):
                    summed(("uq", h), l, [(w_q[:, k, h * P:(h + 1) * P], d_qc[:, k, :]) for k in range(2)])
                need("dsa_n", l, 2)
                ps = opened(("kvt", 0), l)
                for t in range(TT):
                    last = nc.tensor.transpose(ps[:, t * P:(t + 1) * P], d_kv[:, t * P:(t + 1) * P], ident)
                last.then_inc(B.filled(("kvt", 0)), 1)
                need("uq_copied", l)
                need("kvt_copied", l)
                for i in range(36):
                    if i < 32:
                        b, h = i // 8, i % 8
                        w = P * (b + 1)
                        ps = opened(("lg", i), l)
                        mm(ps[:, 0:w], d_q[:, h, b * P:(b + 1) * P], d_kv[:, 0:w], start=True, stop=True).then_inc(B.filled(("lg", i)), 1)
                    if 2 <= i < 34:
                        j = i - 2
                        need("p_ready", l, j + 1)
                        ps = opened(("pt", j), l)
                        for s_ in range(j // 8 + 1):
                            last = nc.tensor.transpose(ps[:, s_ * P:(s_ + 1) * P], d_rl[j % 4][:, s_ * P:(s_ + 1) * P], ident)
                        last.then_inc(B.filled(("pt", j)), 1)
                    if i >= 4 and i % 4 == 3:
                        j = i - 4
                        ps = opened(("cx", j // 4), l)
                        need("pt_copied", l, j + 1)
                        for jj in range(j - 3, j + 1):
                            for s_ in range(jj // 8 + 1):
                                last = mm(ps[:, (jj % 4) * P:(jj % 4 + 1) * P], d_kt[:, s_, :], d_pt[jj % 4][:, s_ * P:(s_ + 1) * P],
                                          start=(s_ == 0), stop=(s_ == jj // 8))
                        last.then_inc(B.filled(("cx", j // 4)), 1)
                need("cx_copied", l)
                for c in range(4):
                    ps = opened(("uv", c), l)
                    for p in range(2):
                        last = mm(ps[64 * p:64 * p + 64, :], w_v[:, 2 * c + p, :], d_cx[:, 2 * c + p, :], start=True, stop=True)
                    if c == 3:
                        leave(last, ("up", 0))
                        pe.drain().then_inc(B.filled(("uv", c)), 1)
                    else:
                        last.then_inc(B.filled(("uv", c)), 1)
                join(pe, l, 4)

                for m in range(KD):
                    w = arrive(("merge", m), l).rearrange("p (r k n) -> p r k n", r=3, k=12)
                    for r, y in enumerate((ya, yb, yc)):
                        summed(("gt", m, r), l, [(w[:, r, k, :], hT[:, k, :]) for k in range(KD)])
                        ps = opened(("br", m, r), l)
                        for k in range(4):
                            last = mm(ps[:, :], w[:, r, 8 + k, :], y[:, k, :], start=(k == 0), stop=(k == 3))
                        if r < 2:
                            last.then_inc(B.filled(("br", m, r)), 1)
                    leave(last, ("merge", m))
                    pe.drain().then_inc(B.filled(("br", m, 2)), 1)
                need("merged", l)

                def out_block(kind, job, src, l):
                    for i in range(2):
                        w = v3(arrive((kind, i), l)[:, 0:4096], 8)
                        for j in range(4):
                            m = 4 * i + j
                            ps = opened((job, m), l)
                            for k in range(KD):
                                last = mm(ps[:, :], w[:, k, j * P:(j + 1) * P], src[:, k, :], start=(k == 0), stop=(k == KD - 1))
                            if j == 3:
                                leave(last, (kind, i))
                                pe.drain().then_inc(B.filled((job, m)), 1)
                            else:
                                last.then_inc(B.filled((job, m)), 1)

                out_block("out", "wo", m_o, l)
                join(pe, l, 5)
                norm(l, 1)
                need("h_ready", l, 2 * KD)
                join(pe, l, 6)
                out_block("pq", "pq", hT, l)
                for t in range(TT):
                    for hf in range(2):
                        ps = opened(("h2", t, hf), l)
                        for i in range(4):
                            last = nc.tensor.transpose(ps[:, i * P:(i + 1) * P], hT[:, 4 * hf + i, t * P:(t + 1) * P], ident)
                        last.then_inc(B.filled(("h2", t, hf)), 1)
                join(pe, l, 7)
                with pe.Fori(0, TT) as t:
                    lap = l * TT + t
                    pe.wait_ge(*E_["tile_in"].at(lap))
                    for q in range(2):
                        for p in range(2):
                            ps = opened(("sc", p, q), lap, T)
                            for i in range(4):
                                h = 4 * q + i
                                last = mm(ps[:, i * P:(i + 1) * P], e_qc[64 * p:64 * p + 64, h, :],
                                          sw[64 * p:64 * p + 64, SW_KEY + h * P:SW_KEY + (h + 1) * P], start=True, stop=True)
                            last.then_inc(T.filled(("sc", p, q)), 1)
                    for j in range(2):
                        opened(("acc", j), lap, T)
                    acc = [psum[T.bank(("acc", j))] for j in range(2)]
                    for j in range(2):
                        mm(acc[j][:, :], zeros[:], e_hc[:, 0:NB], start=True, stop=False)
                    with pe.Fori(0, SLOTS // GRP) as g:
                        for s_ in range(GRP):
                            pe.wait_ge(diags[s_], lap * (SLOTS // GRP) + g + 1)
                            for j in range(2):
                                last = mm(acc[j][:, :], e_diag[:, s_, :], e_row[s_][:, D + j * NB:D + (j + 1) * NB], start=False, stop=False)
                            last.then_inc(rows_used[s_], 1)
                    for j in range(2):
                        mm(acc[j][:, :], zeros[:], e_hc[:, 0:NB], start=False, stop=True).then_inc(T.filled(("acc", j)), 1)
                    pe.wait_ge(*E_["acc_copied"].at(lap))
                    for j in range(2):
                        ps = opened(("xt", j), lap, T)
                        for i in range(4):
                            last = nc.tensor.transpose(ps[:, i * P:(i + 1) * P], e_acc[:, j * NB + i * P:j * NB + (i + 1) * P], ident)
                        last.then_inc(T.filled(("xt", j)), 1)
                join(pe, l, 8)
            pe.wait_ge(G["squares"].sem, depth * 2 + 1)
            pe.wait_ge(T.freed_sems[0], 2)
            for k in range(KD):
                last = mm(psum[0][:, :], ones, hT[:, k, :], start=(k == 0), stop=(k == KD - 1))
            last.then_inc(stored_mm, 1)

        @block.scalar
        def _(act):
            A = nc.scalar.activation

            def need(sig, l, k=None):
                act.wait_ge(*G[sig].at(l, k))

            def full(name, l, banks=B):
                act.wait_ge(*banks.full(name, l))
                return psum[banks.bank(name)]

            def inv_root(out, ps, scale, eps, freed, done):
                A(out, ps, ACT.Ln, bias=eps, scale=scale).then_inc(freed, 1)
                act.drain()
                A(out, out, ACT.Exp, scale=-0.5).then_inc(done, 1)

            act.wait_ge(loaded, 64)
            act.wait_ge(const_set, 1)
            A(cond[:], fix[:, 0:KD], ACT.Silu)
            act.drain()
            with act.Fori(0, depth) as l:
                act.nop().then_inc(G["cond_ready"].sem, 1)

                def norm(w):
                    for k in range(KD):
                        last = A(hT[:, k, :], xT[:, k, :], ACT.Square)
                    last.then_inc(G["squares"].sem, 1)
                    ps = full(("ss", w), l)
                    inv_root(rstd[:], ps[:, :], 1.0 / D, sc[:, 0:1], B.freed(("ss", w)), rstd_ready)
                    for k in range(KD):
                        act.wait_ge(scaled, (l * 2 + w) * KD + k + 1)
                        A(hT[:, k, :], hT[:, k, :], ACT.Identity, bias=modc[:, 24 * w + k:24 * w + k + 1]).then_inc(G["h_ready"].sem, 1)

                norm(0)
                def raw(i, c):
                    ps = full(("rp", c), l)
                    if i >= 2:
                        need("pt_used", l, i - 1)
                    A(r_pt[i % 2][:, 1:513], ps[:, :], ACT.Copy).then_inc(B.freed(("rp", c)), 1)
                    act.drain().then_inc(G["pt_ready"].sem, 1)

                order = (12, 13, 4, 5, 6, 7, 0, 1, 2, 3, 8, 9, 10, 11)
                for i in range(2):
                    raw(i, order[i])
                need("mixed", l, 1)
                A(r_lr[0:64, :], r_lr[0:64, :], ACT.Tanh).then_inc(G["lr_ready"].sem, 1)
                need("mixed", l, 2)
                A(r_gl, r_gl, ACT.Sigmoid).then_inc(G["lr_ready"].sem, 1)
                for nm, dst, b in (("z", r_sg, "rwkv_w0"), ("za", r_a, "rwkv_a0")):
                    for c in range(4):
                        ps = full((nm, c), l)
                        last = A(dst[:, c, :], ps[:, :], ACT.Sigmoid, bias=cl(b, c)).then_inc(B.freed((nm, c)), 1)
                    act.drain().then_inc(G["sig_ready"].sem, 1)
                for i in range(2, 14):
                    raw(i, order[i])
                need("kk_raw", l)
                A(r_t1, r_kk, ACT.Square).then_inc(G["kk_sq"].sem, 1)
                for c in range(4):
                    full(("kkn", c), l)
                for c in range(4):
                    ps = full(("kkn", c), l)
                    inv_root(r_t1[:, c, :], ps[:, :], 1.0, sc[:, 2:3], B.freed(("kkn", c)), G["kk_rs"].sem)
                need("cs_done", l)
                A(r_sg, r_sg, ACT.Exp, scale=-KAPPA).then_inc(G["eprev"].sem, 1)
                A(r_f, r_f, ACT.Exp, scale=-KAPPA).then_inc(G["f_ready"].sem, 1)
                need("ar_half", l)
                A(r_sg, r_cs, ACT.Exp, scale=-KAPPA)
                act.drain().then_inc(G["ep"].sem, 1)
                A(r_cs, r_cs, ACT.Exp, scale=KAPPA).then_inc(G["em"].sem, 1)
                for t in range(TT):
                    for wi in range(3):
                        ps = full(("tm", t, wi), l)
                        if t and wi == 0:
                            need("state", l, t)
                        A(r_tm[:, wi, :], ps[:, :], ACT.Copy).then_inc(B.freed(("tm", t, wi)), 1)
                        act.drain().then_inc(G["tm_copied"].sem, 1)
                    for lv in range(1, 7):
                        for q in range(2):
                            ps = full(("u", t, lv, q), l)
                            if lv > 1:
                                need("t_updated", l, 14 * t + 2 * (lv - 1) + q + 1)
                            A(r_u[:, 4 * q:4 * q + 4, :], ps[:, :], ACT.Copy).then_inc(B.freed(("u", t, lv, q)), 1)
                            act.drain().then_inc(G["u_copied"].sem, 1)
                    for p in range(2):
                        ps = full(("g", t, p), l)
                        A(r_g[:, p:8:2, :], v3(ps[:, 0:256], 4), ACT.Copy).then_inc(B.freed(("g", t, p)), 1)
                        act.drain().then_inc(G["g_copied"].sem, 1)
                    ps = full(("sa", t), l)
                    A(r_sa, ps[:, :], ACT.Copy).then_inc(B.freed(("sa", t)), 1)
                    act.drain().then_inc(G["sa_copied"].sem, 1)
                    for p in range(2):
                        lo, hi = 64 * p, 64 * p + 64
                        ps = full(("y", t, p), l)
                        A(r_y[lo:hi, :, t * P:(t + 1) * P], v3(ps[lo:hi, :], 4), ACT.Copy).then_inc(B.freed(("y", t, p)), 1)
                        act.drain().then_inc(G["y_copied"].sem, 1)
                for c in range(4):
                    need("y_cent", l, c + 1)
                    A(r_t1[:, c, :], r_y[:, c, :], ACT.Square).then_inc(G["y_sq"].sem, 1)
                for c in range(4):
                    ps = full(("var", c), l)
                    inv_root(r_t1[:, c, :], ps[:, :], 1.0 / 64, sc[:, 1:2], B.freed(("var", c)), G["y_rs"].sem)
                join(act, l, 2)

                n_in = G["gla_in"].sem

                def copied(name, dst, func=ACT.Copy, scale=1.0, ps_of=lambda ps: ps[:, :]):
                    ps = full(name, l)
                    A(dst, ps_of(ps), func, scale=scale).then_inc(B.freed(name), 1)
                    return act.drain()

                for c in range(4):
                    copied(("gq", c), (g_q if c < 2 else g_k)[:, c % 2, :], scale=0.125 if c < 2 else 1.0).then_inc(n_in, 1)
                for t in range(TT):
                    copied(("gv", t), g_v[:, t, :]).then_inc(n_in, 1)
                copied(("ga", 0), g_a[0:16, :], ps_of=lambda ps: ps[0:16, :]).then_inc(n_in, 1)
                for c in range(2):
                    ps = full(("gz", c), l)
                    A(g_ab[:, c, :], ps[:, :], ACT.Abs, bias=cl("gla_b_a", c)).then_inc(G["gz_abs"].sem, 1)
                act.drain()
                for c in range(2):
                    A(g_ab[:, c, :], g_ab[:, c, :], ACT.Exp, scale=-1.0)
                act.drain()
                for c in range(2):
                    A(g_ab[:, c, :], g_ab[:, c, :], ACT.Ln, bias=sc[:, 3:4]).then_inc(G["gz_exp"].sem, 1)
                for c in range(4):
                    copied(("gr", c), g_r[:, c, :], ACT.Silu).then_inc(n_in, 1)
                need("gla_la", l)
                A(g_la, g_la, ACT.Exp, scale=1.0 / 16).then_inc(G["gla_dec"].sem, 1)
                A(g_dec, g_tot, ACT.Exp, scale=1.0 / 16).then_inc(G["gla_dec"].sem, 1)
                for c in range(2):
                    ps = full(("kt", c), l)
                    A(g_tm[:, :, c * P:(c + 1) * P], v3(ps[:, :], 4), ACT.Copy).then_inc(B.freed(("kt", c)), 1)
                    act.drain().then_inc(G["kt_copied"].sem, 1)
                for h in range(4):
                    ps = full(("o", h), l)
                    A(g_o2[:, h, :], ps[:, :], ACT.Square).then_inc(G["o_sq"].sem, 1)
                    A(g_o[:, h, :], ps[:, :], ACT.Copy).then_inc(B.freed(("o", h)), 1)
                for h in range(4):
                    ps = full(("on", h), l)
                    inv_root(g_o2[:, h, :], ps[:, :], 1.0 / 128, sc[:, 0:1], B.freed(("on", h)), G["o_rs"].sem)
                join(act, l, 3)

                d_in = G["dsa_in"].sem
                for c in range(2):
                    copied(("qc", c), d_qc[:, c, :]).then_inc(d_in, 1)
                    last = A(d_sq[:, c, :], d_qc[:, c, :], ACT.Square)
                last.then_inc(G["dsa_sq"].sem, 1)
                copied(("qc", 2), d_kv).then_inc(d_in, 1)
                A(d_sq[:, 2, :], d_kv, ACT.Square).then_inc(G["dsa_sq"].sem, 1)
                copied(("qc", 3), d_ik).then_inc(d_in, 1)
                copied(("iw", 0), d_iw.rearrange("p c t -> p (c t)"), ps_of=lambda ps: ps[:, 0:16]).then_inc(d_in, 1)
                ps = full(("qn", 0), l)
                inv_root(d_sq[:, 0, :], ps[:, :], 1.0 / 256, sc[:, 0:1], B.freed(("qn", 0)), G["dsa_rs"].sem)
                ps = full(("kn", 0), l)
                inv_root(d_sq[:, 2, :], ps[:, :], 1.0 / 128, sc[:, 0:1], B.freed(("kn", 0)), G["dsa_rs"].sem)
                for c in range(2):
                    copied(("iq", c), d_qi[:, c, :]).then_inc(G["iq_copied"].sem, 1)
                for i in range(12):
                    b, h = 1 + i // 4, i % 4
                    w = P * (b + 1)
                    ps = full(("ix", b, h), l)
                    if i >= 4:
                        need("relu_used", l, i - 3)
                    A(d_rl[h][:, 0:w], ps[:, 0:w], ACT.Relu).then_inc(B.freed(("ix", b, h)), 1)
                    act.drain().then_inc(G["relu"].sem, 1)
                for h in range(8):
                    copied(("uq", h), d_q[:, h, :]).then_inc(G["uq_copied"].sem, 1)
                copied(("kvt", 0), d_kt.rearrange("p c t -> p (c t)")).then_inc(G["kvt_copied"].sem, 1)

                def turned(j):
                    w = P * (j // 8 + 1)
                    ps = full(("pt", j), l)
                    if j >= 4:
                        act.wait_ge(*B.full(("cx", j // 4 - 1), l))
                    A(d_pt[j % 4][:, 0:w], ps[:, 0:w], ACT.Copy).then_inc(B.freed(("pt", j)), 1)
                    act.drain().then_inc(G["pt_copied"].sem, 1)

                for i in range(38):
                    if i < 32:
                        w = P * (i // 8 + 1)
                        need("lg_max", l, i + 1)
                        A(d_rl[i % 4][:, 0:w], d_rl[i % 4][:, 0:w], ACT.Exp, bias=d_n[:, i:i + 1], scale=P ** -0.5,
                          accum_out=d_sm[:, i:i + 1]).then_inc(G["lg_exp"].sem, 1)
                    if 3 <= i < 35:
                        turned(i - 3)
                    if i >= 6 and i % 4 == 1:
                        n = (i - 6) // 4
                        ps = full(("cx", n), l)
                        A(d_cx[:, 4 * (n % 2):4 * (n % 2) + 4, (n // 2) * P:(n // 2 + 1) * P], v3(ps[:, :], 4), ACT.Copy)\
                            .then_inc(B.freed(("cx", n)), 1)
                        act.drain().then_inc(G["cx_copied"].sem, 1)
                for c in range(4):
                    ps = full(("uv", c), l)
                    A(yb[:, c, :], ps[:, :], ACT.Copy).then_inc(B.freed(("uv", c)), 1)
                join(act, l, 4)

                for i in range(24):
                    m, r = i // 3, i % 3
                    ps = full(("gt", m, r), l)
                    if i >= 2:
                        need("gate_used", l, i - 1)
                    A(m_g[i % 2], ps[:, :], ACT.Sigmoid).then_inc(B.freed(("gt", m, r)), 1)
                    act.drain().then_inc(G["gate"].sem, 1)
                need("x_mixed", l)
                join(act, l, 5)
                norm(1)
                join(act, l, 6)
                for h in range(EH):
                    copied(("pq", h), e_q[:, h, :]).then_inc(G["pq_copied"].sem, 1)
                for t in range(TT):
                    for hf in range(2):
                        copied(("h2", t, hf), e_h[:, t, hf * NB:(hf + 1) * NB]).then_inc(G["h2_copied"].sem, 1)
                join(act, l, 7)
                with act.Fori(0, TT) as t:
                    lap = l * TT + t
                    A(e_qc, e_q[:, :, bass.ds(t * P, P)], ACT.Copy)
                    A(e_hc, e_h.rearrange("p t d -> p (t d)")[:, bass.ds(t * D, D)], ACT.Copy)
                    act.drain().then_inc(E_["tile_in"].sem, 1)
                    for q in range(2):
                        for p in range(2):
                            ps = full(("sc", p, q), lap, T)
                            A(e_s[:, 8 * q + p:8 * q + 8:2, :], v3(ps[:, :], 4), ACT.Copy).then_inc(T.freed(("sc", p, q)), 1)
                            act.drain().then_inc(E_["scored"].sem, 1)
                    act.wait_ge(*E_["soft_in"].at(lap))
                    A(e_ex, e_ex, ACT.Exp).then_inc(E_["soft"].sem, 1)
                    act.wait_ge(*E_["routed"].at(lap))
                    with act.Fori(0, SLOTS // GRP) as g:
                        turn = lap * (SLOTS // GRP) + g
                        A(e_gc, e_gate[:, bass.ds(g * GRP, GRP)], ACT.Copy)
                        for s_ in range(GRP):
                            act.wait_ge(dots[s_], turn + 1)
                            A(e_ge[:, s_:s_ + 1], e_dot[:, s_:s_ + 1], ACT.Gelu)
                            act.drain()
                            A(e_wg[:, s_:s_ + 1], e_gc[:, s_:s_ + 1], ACT.Copy, scale=e_ge[:, s_:s_ + 1])
                            act.drain()
                            act.wait_ge(rows_used[s_], turn + 1)
                            A(e_diag[:, s_, :], ident, ACT.Copy, scale=e_wg[:, s_:s_ + 1]).then_inc(diags[s_], 1)
                    for j in range(2):
                        ps = full(("acc", j), lap, T)
                        last = A(e_acc[:, j * NB:(j + 1) * NB], ps[:, :], ACT.Copy).then_inc(T.freed(("acc", j)), 1)
                    act.drain().then_inc(E_["acc_copied"].sem, 1)
                    act.wait_ge(*E_["tile_out"].at(lap))
                join(act, l, 8)
            for k in range(KD):
                last = A(hT[:, k, :], xT[:, k, :], ACT.Square)
            last.then_inc(G["squares"].sem, 1)
            act.wait_ge(stored_mm, 1)
            A(rstd[:], psum[0][:, :], ACT.Ln, bias=sc[:, 0:1], scale=1.0 / D)
            act.drain()
            A(rstd[:], rstd[:], ACT.Exp, scale=-0.5).then_inc(rstd_ready, 1)

        @block.vector
        def _(dve):
            V = nc.vector

            def need(sig, l, k=None):
                dve.wait_ge(*G[sig].at(l, k))

            def full(name, l, banks=B):
                dve.wait_ge(*banks.full(name, l))
                return psum[banks.bank(name)]

            for i, e in enumerate((EPS, LN_EPS, KK_EPS, 1.0)):
                V.memset(sc[:, i:i + 1], e)
            V.memset(zeros[:], 0.0)
            V.memset(e_off[:], 0.0)
            dve.drain().then_inc(const_set, 1)
            dve.wait_ge(loaded, 64)
            with dve.Fori(0, depth) as l:
                V.tensor_copy(col[:], allcols[:, bass.ds(l * NCOL, NCOL)])
                V.memset(r_pt[0][:, 0:1], 0.0)
                V.memset(r_pt[1][:, 0:1], 0.0)
                dve.drain()
                ps = full("mod", l)
                V.tensor_tensor(modc[:], ps[:, 0:48], cl("b_ada", 0, 48), ALU.add).then_inc(B.freed("mod"), 1)
                dve.drain()
                for w, g in ((0, "g_norm_mix"), (1, "g_norm_ffn")):
                    V.scalar_tensor_tensor(out=gain[:, KD * w:KD * w + KD], in0=modc[:, 24 * w + 8:24 * w + 16], scalar=1.0,
                                           in1=cl(g, 0, KD), op0=ALU.add, op1=ALU.mult)
                V.tensor_scalar(omka[:], cl("rwkv_k_a", 0, 4), -1.0, 1.0, ALU.mult, ALU.add)
                dve.drain()

                def norm(w):
                    dve.wait_ge(rstd_ready, l * 2 + w + 1)
                    for k in range(KD):
                        V.scalar_tensor_tensor(out=hT[:, k, :], in0=xT[:, k, :], scalar=gain[:, KD * w + k:KD * w + k + 1],
                                               in1=rstd[:], op0=ALU.mult, op1=ALU.mult).then_inc(scaled, 1)

                norm(0)
                dst_of = {12: r_lr, 13: r_gl, **{c: r_r[:, c, :] for c in range(4)},
                          **{4 + c: r_k[:, c, :] for c in range(4)}, **{8 + c: r_v[:, c, :] for c in range(4)}}
                for i, c in enumerate((12, 13, 4, 5, 6, 7, 0, 1, 2, 3, 8, 9, 10, 11)):
                    need("pt_ready", l, i + 1)
                    pt, d = r_pt[i % 2], dst_of[c]
                    V.tensor_tensor(d, pt[:, 0:512], pt[:, 1:513], ALU.subtract)
                    dve.drain()
                    V.scalar_tensor_tensor(out=d, in0=d, scalar=cl("rwkv_mu", c), in1=pt[:, 1:513], op0=ALU.mult, op1=ALU.add)\
                        .then_inc(G["mixed"].sem, 1)
                    dve.drain().then_inc(G["pt_used"].sem, 1)
                    if i == 5:
                        need("sig_ready", l, 2)
                        for c_ in range(4):
                            V.tensor_tensor_scan(r_cs[:, c_, :], m128, r_sg[:, c_, :], 0.0, ALU.mult, ALU.add)
                        for c_ in range(4):
                            V.tensor_scalar(r_kk[:, c_, :], r_k[:, c_, :], cl("rwkv_k_k", c_), None, ALU.mult)
                        dve.drain().then_inc(G["kk_raw"].sem, 1)
                        cs16 = r_cs.rearrange("p c (t s) -> p (c t) s", t=4)
                        V.tensor_copy(r_mid, cs16[:, :, 63])
                        dve.drain()
                        V.tensor_tensor(cs16, cs16, bc(r_mid.unsqueeze(2), [P, 16, P]), ALU.subtract)
                        dve.drain()
                        V.tensor_tensor(r_sg, r_cs, r_sg, ALU.subtract)
                        V.tensor_tensor(v3(r_f, 4), r_cs.rearrange("p c (t s) -> p c t s", t=4)[:, :, 0:3, 127],
                                        v3(r_mid, 4)[:, :, 1:4], ALU.add)
                        dve.drain().then_inc(G["cs_done"].sem, 1)
                        for c_ in range(4):
                            V.tensor_scalar(r_t2[:, c_, :], r_a[:, c_, :], cl("rwkv_k_a", c_), omka[:, c_:c_ + 1], ALU.mult, ALU.add)
                        dve.drain()
                        V.tensor_tensor(r_k, r_k, r_t2, ALU.mult)
                        dve.drain()
                for c in range(4):
                    V.scalar_tensor_tensor(out=r_t2[:, c, :], in0=r_r[:, c, :], scalar=cl("rwkv_r_k", c), in1=r_k[:, c, :],
                                           op0=ALU.mult, op1=ALU.mult)
                dve.drain().then_inc(G["bon_in"].sem, 1)
                for c in range(4):
                    need("kk_rs", l, c + 1)
                    V.tensor_tensor(r_kk[:, c, :], r_kk[:, c, :], r_t1[:, c, :], ALU.mult)
                for c in range(4):
                    ps = full(("bon", c), l)
                    V.tensor_tensor(r_bon[:, c, :], ps[:, :], r_v[:, c, :], ALU.mult).then_inc(B.freed(("bon", c)), 1)
                need("eprev", l)
                dve.sem_inc(passed, 1)
                dve.drain()
                half = [r_ar[:, :, :, w, :].rearrange("p c t s -> p (c t) s") for w in range(2)]

                def by_tile(x):
                    return x.rearrange("p c (t s) -> p (c t) s", t=4)
                V.scalar_tensor_tensor(out=half[0], in0=by_tile(r_kk), scalar=-1.0, in1=by_tile(r_sg), op0=ALU.mult, op1=ALU.mult)
                V.tensor_tensor(r_kk, r_kk, r_a, ALU.mult)
                dve.drain().then_inc(G["ar_half"].sem, 1)
                need("ep", l)
                V.tensor_tensor(half[1], by_tile(r_r), by_tile(r_sg), ALU.mult)
                need("em", l)
                V.tensor_tensor(r_kk, r_kk, r_cs, ALU.mult)
                V.tensor_tensor(r_k, r_k, r_cs, ALU.mult)
                dve.drain().then_inc(G["rk_ready"].sem, 1)
                V.memset(r_s, 0.0).then_inc(G["s_zero"].sem, 1)
                need("f_ready", l)
                for t in range(TT):
                    if t:
                        need("y_copied", l, 2 * t)
                    for nm, dst in (("ab", r_ab), ("kb", r_ak)):
                        for q in range(2):
                            for p in range(2):
                                ps = full((nm, t, p, q), l)
                                V.tensor_tensor(dst[:, 4 * q + p:4 * q + 4:2, :], v3(ps[:, :], 2), bc(tri.unsqueeze(1), [P, 2, 2 * P]), ALU.mult)\
                                    .then_inc(B.freed((nm, t, p, q)), 1)
                                dve.drain().then_inc(G["ab_masked"].sem, 1)

                    def level(lv):
                        V.tensor_tensor(r_m, r_ab[:, :, 0:P], bc(lvl[:, lv, :].unsqueeze(1), [P, 8, P]), ALU.mult)
                        dve.drain().then_inc(G["level_masked"].sem, 1)
                    if t:
                        need("sa_copied", l, t)
                    level(0)
                    V.tensor_tensor(r_tt, r_m, bc(ident.unsqueeze(1), [P, 8, P]), ALU.add)
                    for q in range(2):
                        ps = full(("m0", t, q), l)
                        V.tensor_tensor(r_tn[:, 4 * q:4 * q + 4, :], v3(ps[:, :], 4), bc(ident.unsqueeze(1), [P, 4, P]), ALU.add)\
                            .then_inc(B.freed(("m0", t, q)), 1)
                        dve.drain().then_inc(G["t_updated"].sem, 1)
                    level(1)
                    for lv in range(1, 7):
                        for q in range(2):
                            hs = slice(4 * q, 4 * q + 4)
                            full(("ut", t, lv, q), l)
                            if lv < 6:
                                ps = full(("tu", t, lv, q), l)
                                V.tensor_tensor(r_tn[:, hs, :], v3(ps[:, :], 4), r_tn[:, hs, :], ALU.add).then_inc(B.freed(("tu", t, lv, q)), 1)
                            ps = full(("ut", t, lv, q), l)
                            V.tensor_tensor(r_tt[:, hs, :], v3(ps[:, :], 4), r_tt[:, hs, :], ALU.add).then_inc(B.freed(("ut", t, lv, q)), 1)
                            dve.drain().then_inc(G["t_updated"].sem, 1)
                            if q == 0 and lv < 6:
                                need("u_copied", l, 12 * t + 2 * lv)
                                level(lv + 1)
                    if t < 3:
                        ps = full(("s", t), l)
                        V.tensor_tensor(r_s, v3(ps[:, 0:256], 4), r_s, ALU.add).then_inc(B.freed(("s", t)), 1)
                        dve.drain()
                        V.tensor_tensor(r_s, r_s, bc(v3(r_f, 4)[:, :, t:t + 1], [P, 4, 64]), ALU.mult)
                        dve.drain().then_inc(G["state"].sem, 1)
                need("y_copied", l)
                for c in range(4):
                    ps = full(("mu", c), l)
                    V.scalar_tensor_tensor(out=r_y[:, c, :], in0=ps[:, :], scalar=-1.0 / 64, in1=r_y[:, c, :], op0=ALU.mult, op1=ALU.add)\
                        .then_inc(B.freed(("mu", c)), 1)
                    dve.drain().then_inc(G["y_cent"].sem, 1)
                for c in range(4):
                    need("y_rs", l, c + 1)
                    V.tensor_tensor(r_y[:, c, :], r_y[:, c, :], r_t1[:, c, :], ALU.mult)
                    dve.drain()
                    V.tensor_scalar(r_y[:, c, :], r_y[:, c, :], cl("rwkv_ln_g", c), cl("rwkv_ln_b", c), ALU.mult, ALU.add)
                    dve.drain()
                    V.tensor_tensor(r_y[:, c, :], r_y[:, c, :], r_bon[:, c, :], ALU.add)
                    dve.drain()
                    ps = full(("g2", c), l)
                    V.tensor_tensor(yc[:, c, :], ps[:, :], r_y[:, c, :], ALU.mult).then_inc(B.freed(("g2", c)), 1)
                V.nop().then_inc(G["state"].sem, 1)
                join(dve, l, 2)

                for c in range(2):
                    need("gz_abs", l, c + 1)
                    ps = full(("gz", c), l)
                    V.tensor_scalar(g_la[:, c, :], ps[:, :], cl("gla_b_a", c), 0.0, ALU.add, ALU.min).then_inc(B.freed(("gz", c)), 1)
                need("gz_exp", l)
                dve.sem_inc(passed, 1)
                dve.drain()
                V.tensor_tensor(g_la, g_la, g_ab, ALU.subtract)
                dve.drain()
                for c in range(2):
                    V.tensor_tensor_scan(g_cum[:, c, :], m64, g_la[:, c, :], 0.0, ALU.mult, ALU.add)
                dve.drain()
                cum = g_cum.rearrange("p c (n s) -> p (c n) s", n=NCH)
                V.tensor_copy(g_tot.rearrange("p c n -> p (c n)"), cum[:, :, 63])
                dve.drain()
                V.tensor_tensor(g_la.rearrange("p c (n s) -> p (c n) s", n=NCH), bc(g_tot.rearrange("p c n -> p (c n)").unsqueeze(2), [P, 16, 64]),
                                cum, ALU.subtract)
                dve.drain().then_inc(G["gla_la"].sem, 1)
                need("gla_dec", l)
                need("gla_in", l, 4)
                V.tensor_tensor(g_k, g_k, g_la, ALU.mult).then_inc(G["gla_kd"].sem, 1)
                for n in range(NCH):
                    ps = full(("upd", n), l)
                    for c in range(2):
                        for p in range(2):
                            lo, hi = 64 * p, 64 * p + 64
                            src = ps[lo:hi, c * 256 + p * P:c * 256 + (p + 1) * P]
                            if n == 0:
                                last = V.tensor_copy(g_st[lo:hi, n, c, :], src)
                            else:
                                last = V.scalar_tensor_tensor(out=g_st[lo:hi, n, c, :], in0=g_st[lo:hi, n - 1, c, :],
                                                              scalar=g_dec[lo:hi, c, n:n + 1], in1=src, op0=ALU.mult, op1=ALU.add)
                    last.then_inc(B.freed(("upd", n)), 1)
                    dve.drain().then_inc(G["gla_state"].sem, 1)
                need("gla_in", l, 13)
                for h in range(4):
                    need("o_rs", l, h + 1)
                    V.scalar_tensor_tensor(out=g_o[:, h, :], in0=g_o[:, h, :], scalar=cl("gla_g_o"), in1=g_o2[:, h, :], op0=ALU.mult, op1=ALU.mult)
                    dve.drain()
                    V.tensor_tensor(ya[:, h, :], g_o[:, h, :], g_r[:, h, :], ALU.mult)
                join(dve, l, 3)

                need("dsa_rs", l, 1)
                for c in range(2):
                    last = V.scalar_tensor_tensor(out=d_qc[:, c, :], in0=d_qc[:, c, :], scalar=cl("dsa_g_qc", c), in1=d_sq[:, 0, :],
                                                  op0=ALU.mult, op1=ALU.mult)
                dve.drain().then_inc(G["dsa_n"].sem, 1)
                need("dsa_rs", l, 2)
                V.scalar_tensor_tensor(out=d_kv, in0=d_kv, scalar=cl("dsa_g_kv"), in1=d_sq[:, 2, :], op0=ALU.mult, op1=ALU.mult)\
                    .then_inc(G["dsa_n"].sem, 1)
                V.memset(d_nm[:, 0, 0:P], 0.0)
                dve.drain()
                V.memset(d_nm[0:64, 0, 64:P], DROP)
                for b in range(1, 4):
                    w = P * (b + 1)
                    s_ = d_nm[:, b, 0:w]
                    for h in range(4):
                        need("relu", l, (b - 1) * 4 + h + 1)
                        if h == 0:
                            V.tensor_scalar(s_, d_rl[h][:, 0:w], d_iw[:, b, h:h + 1], None, ALU.mult).then_inc(G["relu_used"].sem, 1)
                        else:
                            V.scalar_tensor_tensor(out=s_, in0=d_rl[h][:, 0:w], scalar=d_iw[:, b, h:h + 1], in1=s_, op0=ALU.mult, op1=ALU.add)\
                                .then_inc(G["relu_used"].sem, 1)
                        dve.drain()
                    V.memset(d_nm[0:64, b, w - 64:w], NEG)
                    dve.drain()
                    for i in range(TOPK // 8):
                        V.max(d_m8, s_)
                        dve.drain()
                        V.match_replace(s_, d_m8, s_, MARK)
                        dve.drain()
                    V.tensor_scalar(s_, s_, MARK, -DROP, ALU.is_equal, ALU.mult)
                    dve.drain()
                    V.tensor_scalar(s_, s_, DROP, None, ALU.add)
                    dve.drain()
                for i in range(32 + 2):
                    if i < 32:
                        b, h = i // 8, i % 8
                        w = P * (b + 1)
                        ps = full(("lg", i), l)
                        if i >= 4:
                            dve.wait_ge(*B.full(("pt", i - 4), l))
                        dve.sem_inc(passed, 1)
                        V.tensor_tensor_reduce(d_rl[i % 4][:, 0:w], ps[:, 0:w], d_nm[:, b, 0:w], 1.0, NEG, ALU.add, ALU.max, d_mx[:, i:i + 1])\
                            .then_inc(B.freed(("lg", i)), 1)
                        dve.drain()
                        V.tensor_scalar(d_n[:, i:i + 1], d_mx[:, i:i + 1], -(P ** -0.5), None, ALU.mult)
                        dve.drain().then_inc(G["lg_max"].sem, 1)
                    if i >= 2:
                        j = i - 2
                        w = P * (j // 8 + 1)
                        need("lg_exp", l, j + 1)
                        V.reciprocal(d_mx[:, j:j + 1], d_sm[:, j:j + 1])
                        dve.drain()
                        V.tensor_scalar(d_rl[j % 4][:, 0:w], d_rl[j % 4][:, 0:w], d_mx[:, j:j + 1], None, ALU.mult).then_inc(G["p_ready"].sem, 1)
                join(dve, l, 4)

                for m in range(KD):
                    for r in range(3):
                        i = 3 * m + r
                        need("gate", l, i + 1)
                        ps = full(("br", m, r), l)
                        dst = m_o[:, m, :] if r == 0 else m_t
                        V.tensor_tensor(dst, ps[:, :], m_g[i % 2], ALU.mult).then_inc(B.freed(("br", m, r)), 1)
                        dve.drain().then_inc(G["gate_used"].sem, 1)
                        if r:
                            V.tensor_tensor(m_o[:, m, :], m_o[:, m, :], m_t, ALU.add)
                            dve.drain()
                    V.nop().then_inc(G["merged"].sem, 1)
                for m in range(KD):
                    ps = full(("wo", m), l)
                    V.scalar_tensor_tensor(out=xT[:, m, :], in0=ps[:, :], scalar=modc[:, 16 + m:17 + m], in1=xT[:, m, :], op0=ALU.mult, op1=ALU.add)\
                        .then_inc(B.freed(("wo", m)), 1)
                    dve.drain().then_inc(G["x_mixed"].sem, 1)
                join(dve, l, 5)
                norm(1)
                join(dve, l, 6)
                join(dve, l, 7)

                with dve.Fori(0, TT) as t:
                    lap = l * TT + t
                    dve.wait_ge(*E_["scored"].at(lap))
                    dve.sem_inc(passed, 1)
                    for r in range(2):
                        for g in range(16):
                            V.max(e_v[:, g, 8 * r:8 * r + 8], e_s[:, g, :])
                        dve.drain()
                        for g in range(16):
                            V.max_index(e_i[:, g, 8 * r:8 * r + 8], e_v[:, g, 8 * r:8 * r + 8], e_s[:, g, :])
                        if r == 0:
                            dve.drain()
                            for g in range(16):
                                V.match_replace(e_s[:, g, :], e_v[:, g, 0:8], e_s[:, g, :], NEG)
                            dve.drain()
                    dve.drain()
                    V.tensor_copy(e_if, e_i)
                    c4 = e_c.rearrange("p h (a b) -> p h a b", a=ET)
                    for h in range(EH):
                        V.tensor_tensor(c4[:, h], bc(e_v[:, 2 * h, :].unsqueeze(2), [P, ET, ET]), bc(e_v[:, 2 * h + 1, :].unsqueeze(1), [P, ET, ET]), ALU.add)
                    dve.drain()
                    for r in range(2):
                        for h in range(EH):
                            V.max(e_top[:, h, 8 * r:8 * r + 8], e_c[:, h, :])
                        dve.drain()
                        for h in range(EH):
                            V.max_index(e_pos[:, h, 8 * r:8 * r + 8], e_top[:, h, 8 * r:8 * r + 8], e_c[:, h, :])
                        if r == 0:
                            dve.drain()
                            for h in range(EH):
                                V.match_replace(e_c[:, h, :], e_top[:, h, 0:8], e_c[:, h, :], NEG)
                            dve.drain()
                    V.tensor_tensor(e_ex, e_top, bc(e_top[:, :, 0:1], [P, EH, ET]), ALU.subtract)
                    dve.drain().then_inc(E_["soft_in"].sem, 1)
                    pos = e_pos.rearrange("p h k -> p (h k)")
                    V.tensor_scalar(e_pa, pos, 4, None, ALU.logical_shift_right)
                    V.tensor_scalar(e_pb, pos, 15, None, ALU.bitwise_and)
                    dve.drain()
                    V.tensor_copy(e_paf, e_pa)
                    V.tensor_copy(e_pbf, e_pb)
                    dve.drain()
                    for half_, (pf, oh, dst) in enumerate(((e_paf, e_oh, e_n1), (e_pbf, e_oh2, e_n2))):
                        o3 = oh.rearrange("p (k j) -> p k j", j=ET)
                        V.tensor_tensor(o3, bc(pf.unsqueeze(2), [P, SLOTS, ET]), bc(iota16.unsqueeze(1), [P, SLOTS, ET]), ALU.is_equal)
                    dve.drain()
                    for half_, oh in enumerate((e_oh, e_oh2)):
                        o4 = oh.rearrange("p (h k j) -> p h k j", h=EH, j=ET)
                        for h in range(EH):
                            V.tensor_tensor(o4[:, h], o4[:, h], bc(e_if[:, 2 * h + half_, :].unsqueeze(1), [P, ET, ET]), ALU.mult)
                    dve.drain()
                    for oh, dst in ((e_oh, e_n1), (e_oh2, e_n2)):
                        V.tensor_reduce(dst, oh.rearrange("p (k j) -> p k j", j=ET), AX.X, ALU.add)
                    dve.drain()
                    V.scalar_tensor_tensor(out=e_n1, in0=e_n1, scalar=float(NK), in1=e_n2, op0=ALU.mult, op1=ALU.add)
                    dve.drain()
                    V.tensor_scalar(e_idx[:], e_n1, e_off[:, 0:1], None, ALU.add)
                    dve.wait_ge(*E_["soft"].at(lap))
                    V.tensor_reduce(e_sum, e_ex, AX.X, ALU.add)
                    dve.drain()
                    V.reciprocal(e_sum, e_sum)
                    dve.drain()
                    V.tensor_tensor(v3(e_gate, 8), e_ex, bc(e_sum.unsqueeze(2), [P, EH, ET]), ALU.mult)
                    dve.drain().then_inc(E_["routed"].sem, 1)
                    with dve.Fori(0, SLOTS // GRP) as g:
                        turn = lap * (SLOTS // GRP) + g
                        for s_ in range(GRP):
                            dve.wait_ge(rows_landed[s_], 16 * (turn + 1))
                            dve.wait_ge(rows_used[s_], turn + 1)
                            V.tensor_tensor_reduce(e_row[s_][:, 0:D], e_row[s_][:, 0:D], e_hc, 1.0, 0.0, ALU.mult, ALU.add, e_dot[:, s_:s_ + 1])
                            dve.drain().then_inc(dots[s_], 1)
                    for j in range(2):
                        ps = full(("xt", j), lap, T)
                        for i in range(4):
                            k = 4 * j + i
                            xs = xT[:, k, bass.ds(t * P, P)]
                            last = V.scalar_tensor_tensor(out=xs, in0=ps[:, i * P:(i + 1) * P], scalar=modc[:, 40 + k:41 + k], in1=xs,
                                                          op0=ALU.mult, op1=ALU.add)
                        last.then_inc(T.freed(("xt", j)), 1)
                    dve.drain().then_inc(E_["tile_out"].sem, 1)
                V.tensor_scalar(e_off[:], e_off[:], float(NE), None, ALU.add)
                join(dve, l, 8)
            dve.wait_ge(rstd_ready, depth * 2 + 1)
            for k in range(KD):
                V.scalar_tensor_tensor(out=hT[:, k, :], in0=xT[:, k, :], scalar=fix[:, KD + k:KD + k + 1], in1=rstd[:],
                                       op0=ALU.mult, op1=ALU.mult).then_inc(stored, 1)

        @block.gpsimd
        def _(pool):
            with pool.Fori(0, depth) as l:
                with pool.Fori(0, TT) as t:
                    lap = l * TT + t
                    pool.wait_ge(*E_["routed"].at(lap))
                    pool.sem_inc(passed, 1)
                    with pool.Fori(0, SLOTS // GRP) as g:
                        turn = lap * (SLOTS // GRP) + g
                        for s_ in range(GRP):
                            pool.wait_ge(rows_used[s_], turn + 1)
                            pool.sem_inc(passed, 1)
                            pool.tensor_copy(e_ic[:, s_:s_ + 1], e_idx[:, bass.ds(g * GRP + s_, 1)]).then_inc(idx_ready, 1)
                            pool.wait_ge(idx_ready, turn * GRP + s_ + 1)
                            pool.sem_inc(passed, 1)
                            pool.indirect_dma_start(e_row[s_], None, uv, bass.IndirectOffsetOnAxis(ap=e_ic[:, s_:s_ + 1], axis=0))\
                                .then_inc(rows_landed[s_], 16)


_COLS = ('b_ada', 'g_norm_mix', 'g_norm_ffn', 'gla_b_a', 'gla_g_o', 'dsa_g_qc', 'dsa_g_kv', 'rwkv_mu', 'rwkv_w0', 'rwkv_a0',
         'rwkv_k_k', 'rwkv_k_a', 'rwkv_r_k', 'rwkv_ln_g', 'rwkv_ln_b')


def constants():
    i = np.arange(P)
    s, t = i[:, None], i[None, :]
    lv = [((t >> j) % 2 == 1) & ((s >> j) == (t >> j) - 1) for j in range(7)]
    col = np.arange(S)[None, :] + 0 * s
    parts = [s == t, s >= 0 * t, s // 64 == t // 64, s < t, s <= t, *lv, col % CH != 0, col % P != 0]
    iota = np.arange(ET)[None, :] + 0 * s
    return np.concatenate([np.broadcast_to(p, (P, p.shape[1])) for p in parts] + [iota], axis=1).astype(np.float32)


def laid_out(a):
    f = {k: np.asarray(v) for k, v in a.items()}

    def column(v):
        return np.swapaxes(v.reshape(L, -1, P), 1, 2)

    cols = np.concatenate([column(f[n].reshape(L, -1)) for n in _COLS], axis=2)
    cols = np.ascontiguousarray(cols.transpose(1, 0, 2).reshape(P, L * NCOL))
    fixed = np.concatenate([f['c'].reshape(KD, P).T, f['g_final'].reshape(KD, P).T], axis=1)
    keys = f['peer_keys'].transpose(0, 2, 4, 1, 3).reshape(L, P, EH * NK)
    ga = np.concatenate([f['gla_w_a2'], np.zeros((L, P - 16, 256), np.float32)], axis=1)
    small = np.concatenate([ga, np.concatenate([f['rwkv_w_w2'], f['rwkv_w_a2']], axis=1), f['rwkv_w_g2'], keys], axis=2)
    gates = f['w_in'][:, :, GATES:].reshape(L, 8, P, 3, 8, P).transpose(0, 4, 2, 3, 1, 5)
    branch = f['w_branch'].reshape(L, 3, 4, P, 8, P).transpose(0, 4, 3, 1, 2, 5)
    merge = np.concatenate([gates, branch], axis=4).reshape(L, 8, P, 36 * P)
    return dict(fixed=fixed, cols=cols, consts=constants(), x_t=f['x'].reshape(S, D).T, w_ada=f['w_ada'], w_in=f['w_in'],
                w_small=small, w_uq=f['dsa_w_uq'], w_iq=f['dsa_w_iq'], w_uv=f['dsa_w_uv'], w_merge=merge, w_out=f['w_out'],
                w_pq=f['peer_w_q'], uv=np.concatenate([f['peer_u'], f['peer_v']], axis=2).reshape(L * NE, 2 * D))


def kernel(**inputs):
    import concourse.bacc as _bacc
    from concourse.bass_utils import run_bass_kernel_spmd as _run

    nc = _bacc.Bacc("TRN2", target_bir_lowering=False, num_devices=1)
    arrays = {k: np.ascontiguousarray(v) for k, v in laid_out(inputs).items()}
    args = [nc.dram_tensor(k, v.shape, F32, kind="ExternalInput").ap() for k, v in arrays.items()]
    out = nc.dram_tensor("out", (D, S), F32, kind="ExternalOutput").ap()
    trunk(nc, *args, out)
    r = _run(nc, [arrays], core_ids=[0])
    return np.ascontiguousarray(r.results[0]["out"].T).reshape(1, S, D)
```

```python
from contextlib import ExitStack

import numpy as np

import concourse.bass as bass
from concourse import mybir

F32 = mybir.dt.float32
U32 = mybir.dt.uint32
ALU = mybir.AluOpType
ACT = mybir.ActivationFunctionType
AX = mybir.AxisListType

P = 128
L, S, D = 2, 512, 1024
TT, KD = S // P, D // P
NB = 512
IN_W = 6868
GQ, GV, GA, QC, PR, GATES = 0, 512, 1024, 1552, 2004, 3796
CH, NCH = 64, S // 64
TOPK = 128
QUADS = 8
NEG, MARK, DROP = -3.0e38, -3.3e38, -1.0e30
EPS, LN_EPS, KK_EPS = 1e-6, 64e-5, 1e-12
KAPPA = float(np.exp(-0.5))
EH, ET, NK, NE = 8, 16, 128, 16384
SLOTS = EH * ET
RING = 2
GRP = 8
NGRP = EH * ET // GRP
PIECES = (1, 3, 4, 6, 8, 9, 11, 13)

COLS = {}
_at = 0
for _n, _w in (("b_ada", 48), ("g_norm_mix", 8), ("g_norm_ffn", 8), ("gla_b_a", 2), ("gla_g_o", 1), ("dsa_g_qc", 2),
               ("dsa_g_kv", 1), ("rwkv_mu", 14), ("rwkv_w0", 4), ("rwkv_a0", 4), ("rwkv_k_k", 4), ("rwkv_k_a", 4),
               ("rwkv_r_k", 4), ("rwkv_ln_g", 4), ("rwkv_ln_b", 4)):
    COLS[_n] = _at
    _at += _w
NCOL = _at

CONST = {}
_at = 0
for _n, _w in (("ident", P), ("ones", P), ("bones", P), ("tri", 2 * P), ("lvl", 7 * P), ("m64", S), ("m128", S), ("iota", ET)):
    CONST[_n] = (_at, _at + _w)
    _at += _w
NCONST = _at

SW_GA, SW_WA, SW_G2, SW_KEY, SW_UV, SW_N = 0, 256, 768, 1280, 2304, 2816

BLOCKS = ([("ada", i) for i in range(4)] + [("rw", i) for i in (3, 1, 0, 2)] + [("ada", i) for i in range(4, 12)] + [("gla", 0), ("gla", 1), ("gla", 2)]
          + [("dsa", 0), ("up", 0)] + [("mac", m) for m in range(8)] + [("mb", m) for m in range(4)] + [("out", 0), ("out", 1)] + [("pq", 0), ("pq", 1)])
RW_W = (512, 512, 512, 256)


class Banks:

    def __init__(self, sem, prefix, order):
        self.n = {name: i for i, name in enumerate(order)}
        assert len(self.n) == len(order)
        self.filled_sems = [sem(f"{prefix}_filled{b}") for b in range(8)]
        self.freed_sems = [sem(f"{prefix}_freed{b}") for b in range(8)]
        self.per = [len(range(b, len(order), 8)) for b in range(8)]

    def bank(self, name):
        return self.n[name] % 8

    def filled(self, name):
        return self.filled_sems[self.bank(name)]

    def freed(self, name):
        return self.freed_sems[self.bank(name)]

    def full(self, name, lap):
        b = self.bank(name)
        return self.filled_sems[b], lap * self.per[b] + (self.n[name] // 8 + 1)

    def free(self, name, lap):
        b = self.bank(name)
        return self.freed_sems[b], lap * self.per[b] + (self.n[name] // 8 + 1)


def layer_banks():
    o = [("ss", 0), ("mod", 0)]
    o += [("rp", c) for c in (12, 13)] + [("z", c) for c in range(4)] + [("za", c) for c in range(4)]
    o += [("rp", c) for c in (4, 5, 6, 7, 0, 1, 2, 3, 8, 9, 10, 11)]
    o += [("kkn", c) for c in range(4)] + [("bon", c) for c in range(4)]
    for t in range(TT):
        o += [("mod", t + 1)]
        o += [("ab", t, p, q) for q in range(2) for p in range(2)] + [("kb", t, p, q) for q in range(2) for p in range(2)]
        o += [("tm", t, w) for w in range(3)] + [("m0", t, q) for q in range(2)]
        for lv in range(1, 7):
            o += [("u", t, lv, q) for q in range(2)]
            for q in range(2):
                o += ([("tu", t, lv, q)] if lv < 6 else []) + [("ut", t, lv, q)]
        o += [("g", t, 0), ("g", t, 1), ("sa", t), ("y", t, 0), ("y", t, 1)] + ([("s", t)] if t < 3 else [])
    for c in range(4):
        o += [("mu", c)]
    for c in range(4):
        o += [("var", c)]
    for c in range(4):
        o += [("g2", c)]
    o += [("gq", c) for c in range(4)] + [("gv", t) for t in range(TT)] + [("ga", 0)] + [("gz", c) for c in range(2)]
    o += [("gr", c) for c in range(4)] + [("kt", c) for c in range(2)] + [("upd", n) for n in range(NCH)]
    o += [("o", h) for h in range(4)] + [("on", h) for h in range(4)]
    o += [("qc", c) for c in range(4)] + [("iw", 0), ("qn", 0), ("kn", 0)] + [("iq", c) for c in range(2)]
    o += [("ix", b, h) for b in range(1, 4) for h in range(4)] + [("uq", h) for h in range(8)] + [("kvt", 0)]
    o += [x for m in range(KD) for r in (0, 2) for x in (("gt", m, r), ("br", m, r))]
    for i in range(QUADS + 3):
        o += [("pt", i - 2, j) for j in range(4)] if 2 <= i < QUADS + 2 else []
        o += [("lg", i, j) for j in range(4)] if i < QUADS else []
        o += [("cx", i - 3)] if i >= 3 else []
    o += [("uv", c) for c in range(4)]
    o += [x for m in range(KD) for x in (("gt", m, 1), ("br", m, 1))]
    o += [("wo", m) for m in range(KD)] + [("ss", 1)] + [("pq0", i) for i in range(2)] + [("pq", 0)]
    o += [("sc", p, q) for q in range(2) for p in range(2)] + [("pq", h) for h in range(1, EH)]
    o += [("h2", t, h) for t in range(TT) for h in range(2)]
    return o


TILE_BANKS = [("sc", p, q) for q in range(2) for p in range(2)] + [("acc", 0), ("acc", 1), ("xt", 0), ("xt", 1)]


def trunk(nc, fixed, cols, consts, x_t, w_ada, w_in, w_small, w_uq, w_iq, w_mac, w_mb, w_out, w_pq, uv, out,
          depth=L, stop=None):
    ctx = ExitStack()
    with ctx:
        def sb(name, n, dt=F32):
            return ctx.enter_context(nc.sbuf_tensor(name, [P, n], dt))

        def sem(name):
            return ctx.enter_context(nc.semaphore(name))

        psum = [ctx.enter_context(nc.psum_tensor(f"bank{b}", [P, NB], F32)) for b in range(8)]

        def v3(ap, c):
            return ap.rearrange("p (c t) -> p c t", c=c)

        con = sb("con", NCONST)
        xT = v3(sb("xT", KD * S)[:], KD)
        hT = v3(sb("hT", KD * S)[:], KD)
        allcols = sb("allcols", L * NCOL)
        col = sb("col", NCOL)
        fix = sb("fix", 2 * KD)
        sc = sb("sc", 64)
        cond = sb("cond", KD)
        modc = sb("modc", 48)
        gain = sb("gain", 2 * KD)
        omka = sb("omka", 4)
        sw = sb("sw", SW_N)
        rstd = sb("rstd", S)
        SLOT = 36 * P
        REG = 37700
        reg = sb("reg", REG)
        ring = [reg[:, i * SLOT:(i + 1) * SLOT] for i in range(RING)]
        base = RING * SLOT
        ya, yb, yc = (v3(reg[:, base + i * 2048:base + (i + 1) * 2048], 4) for i in range(3))
        base += 3 * 2048

        def at(o, n, dt=None):
            assert base + o + n <= REG, (base + o + n, REG)
            r = reg[:, base + o:base + o + n]
            return r if dt is None else r.bitcast(dt)

        def const(name):
            a, b = CONST[name]
            return con[:, a:b]

        ident, ones, bones = const("ident"), const("ones"), const("bones")
        tri, lvl, m64, m128, iota16 = const("tri"), v3(const("lvl"), 7), const("m64"), const("m128"), const("iota")

        def cl(name, i=0, n=1, p0=0, p1=P):
            return col[p0:p1, COLS[name] + i:COLS[name] + i + n]

        r_pt = [at(19456 + i * 513, 513) for i in range(2)]
        r_r, r_k, r_v = (v3(at(i * 2048, 2048), 4) for i in range(3))
        r_lr, r_gl = at(6144, 512), at(6656, 512)
        r_sg, r_cs, r_a = (v3(at(7168 + i * 2048, 2048), 4) for i in range(3))
        r_kk = v3(at(13312, 2048), 4)
        r_x = at(15360, 4096)
        r_t1, r_t2 = v3(r_x[:, 0:2048], 4), v3(r_x[:, 2048:4096], 4)
        r_ar = r_x.rearrange("p (c t w s) -> p c t w s", c=4, t=4, w=2)
        r_bon, r_y = yb, ya
        r_tm = v3(at(19456, 1536), 3)
        r_g, r_sa = v3(at(20992, 512), 8), v3(at(21504, 512), 8)
        r_s = v3(at(22016, 256), 4)
        r_mid, r_f = at(22272, 16), at(22288, 12)
        r_ab = v3(at(7168, 2048), 8)
        r_ak = v3(at(9216, 2048), 8)
        r_tt, r_tn = v3(at(11264, 1024), 8), v3(at(0, 1024), 8)
        r_u = v3(at(1024, 1024), 8)
        r_m = [v3(at(12288, 1024), 8), v3(yc.rearrange("p c t -> p (c t)")[:, 0:1024], 8)]
        g_q, g_k = v3(at(0, 1024), 2), v3(at(1024, 1024), 2)
        g_v = v3(at(2048, 2048), 4)
        g_a, g_r = at(4096, 512), v3(at(4608, 2048), 4)
        g_la, g_cum, g_ab = (v3(at(6656 + i * 1024, 1024), 2) for i in range(3))
        g_tm = v3(at(9728, 1024), 4)
        g_st = at(10752, 2048).rearrange("p (n c v) -> p n c v", n=NCH, c=2)
        g_o, g_o2 = v3(at(12800, 2048), 4), v3(at(14848, 2048), 4)
        g_tot, g_dec = v3(at(16896, 16), 2), v3(at(16912, 16), 2)
        d_qc, d_kv, d_ik = v3(at(0, 1024), 2), at(1024, 512), at(1536, 512)
        d_qi, d_kt = v3(at(2048, 1024), 2), v3(at(3072, 512), 4)
        d_sq = v3(at(3584, 1536), 3)
        d_q = v3(at(5120, 4096), 8)
        d_cx = d_q
        d_nm = v3(at(13312, 2048), 4)
        d_rl = [at(15360 + i * 512, 512) for i in range(4)]
        d_p = [d_rl, [at(o, 512) for o in (0, 512, 1536, 2048)]]
        d_pt = [[at(17408 + i * 512, 512) for i in range(4)], [at(o, 512) for o in (2560, 3584, 4096, 4608)]]
        d_iw = v3(at(19456, 16), 4)
        d_m8 = at(19472, 8)
        d_mx, d_sm, d_n = at(19480, 32), at(19512, 32), at(19544, 32)
        m_g = [d_pt[0][0], d_pt[0][1]]
        m_t = d_pt[0][2]
        m_o = v3(at(9216, 4096), 8)
        e_row = [reg[:, i * 2048:(i + 1) * 2048] for i in range(GRP)]

        def ep(o, n, dt=None):
            assert GRP * 2048 + o + n <= REG
            r = reg[:, GRP * 2048 + o:GRP * 2048 + o + n]
            return r if dt is None else r.bitcast(dt)

        e_q, e_h = v3(ep(0, 4096), 8), v3(ep(4096, 4096), 4)
        e_qc, e_hc = v3(ep(8192, 1024), 8), ep(9216, 1024)
        e_s = v3(ep(10240, 2048), 16)
        e_c = v3(ep(12288, 2048), 8)
        e_oh = ep(14336, 2048)
        e_oh2 = ep(16384, 2048)
        e_v = v3(ep(18432, 256), 16)
        e_i = v3(ep(18688, 256, U32), 16)
        e_if = v3(ep(18944, 256), 16)
        e_top, e_pos = v3(ep(19200, 128), 8), v3(ep(19328, 128, U32), 8)
        e_pa, e_paf = ep(19456, 128, U32), ep(19584, 128)
        e_pb, e_pbf = ep(19712, 128, U32), ep(19840, 128)
        e_n1, e_n2 = ep(19968, 128), ep(20096, 128)
        e_ex, e_gate = v3(ep(20224, 128), 8), ep(20528, TT * SLOTS)
        e_sum = ep(20480, 8)
        hflat = hT.rearrange("p k t -> p (k t)")
        e_idx = hflat[:, 0:TT * SLOTS].bitcast(U32)
        e_ic = sb("e_ic", GRP, U32)
        e_diag = v3(hflat[:, 512:512 + GRP * P], GRP)
        e_dot, e_ge, e_wg, e_gc = (ep(20488 + i * 8, 8) for i in range(4))
        e_acc = e_oh
        e_off = sb("e_off", 1)
        zeros = sb("zeros", P)

        loaded = sem("loaded")
        landed = [sem(f"block_landed{i}") for i in range(RING)]
        used = [sem(f"block_used{i}") for i in range(RING)]
        nblock = [len(range(i, len(BLOCKS), RING)) for i in range(RING)]
        small_landed = sem("small_landed")
        joined = sem("joined")
        stored = sem("stored")
        B = Banks(sem, "layer", layer_banks())
        T = Banks(sem, "tile", TILE_BANKS)

        class Sig:
            def __init__(self, name, n):
                self.sem, self.n = sem(name), n

            def at(self, lap, k=None):
                return self.sem, lap * self.n + (self.n if k is None else k)

        G = {n: Sig(n, k) for n, k in (
            ("squares", 2), ("h_ready", 2 * KD), ("cond_ready", 1),
            ("pt_ready", 14), ("pt_used", 14), ("mixed", 14), ("lr_ready", 2), ("sig_ready", 2),
            ("kk_raw", 1), ("kk_sq", 1), ("kk_rs", 4), ("bon_in", 1), ("cs_done", 1), ("eprev", 1), ("ep", 1), ("em", 1),
            ("f_ready", 1), ("ar_half", 1), ("rk_ready", 1), ("s_zero", 1),
            ("ab_masked", 32), ("tm_copied", 12), ("level_masked", 7 * TT), ("t_updated", 7 * TT * 2),
            ("u_copied", 6 * TT * 2), ("g_copied", 2 * TT), ("sa_copied", TT), ("y_copied", 2 * TT), ("state", TT),
            ("y_cent", 4), ("y_sq", 4), ("y_rs", 4),
            ("gla_in", 13), ("gz_abs", 2), ("gz_exp", 2), ("gla_la", 1), ("gla_dec", 2), ("gla_kd", 1), ("kt_copied", 2),
            ("gla_state", NCH), ("o_sq", 4), ("o_rs", 4),
            ("dsa_in", 5), ("dsa_sq", 2), ("dsa_rs", 2), ("dsa_n", 2), ("iq_copied", 2), ("relu", 12), ("relu_used", 12),
            ("uq_copied", 8), ("kvt_copied", 1), ("lg_max", QUADS), ("lg_exp", QUADS), ("p_ready", QUADS), ("pt_copied", QUADS), ("cx_copied", QUADS),
            ("gate", 24), ("gate_used", 24), ("merged", 1), ("x_mixed", KD),
            ("h2_copied", 2 * TT))}
        E_ = {n: Sig(n, k) for n, k in (
            ("tile_in", 1), ("rows_in", 1), ("scored", 4), ("routed", 1), ("soft_in", 1), ("soft", 1), ("acc_copied", 1), ("tile_out", 1),
            ("idx_used", 1))}
        rows_landed = [sem(f"rows_landed{s}") for s in range(GRP)]
        rows_used = [sem(f"rows_used{s}") for s in range(GRP)]
        dots = [sem(f"dot{s}") for s in range(GRP)]
        diags = [sem(f"diag{s}") for s in range(GRP)]
        idx_ready = sem("idx_ready")
        passed = sem("passed")
        const_set = sem("const_set")
        rstd_ready = sem("rstd_ready")
        scaled = sem("scaled")
        stored_mm = sem("final_sum")

        NJOIN = 8

        def join(eng, lap, k, n=NJOIN):
            eng.sem_inc(passed, 1)
            eng.drain().then_inc(joined, 1)
            eng.wait_ge(joined, 3 * (lap * n + k - 1) + 1)
            eng.sem_inc(passed, 1)

        def block_at(name):
            i = BLOCKS.index(name)
            return ring[i % RING], i % RING, i // RING + 1

        def stop_at(name):
            return stop is not None and stop == name

        def bc(ap, shape):
            return ap.to_broadcast(shape)

        block = ctx.enter_context(nc.Block())

        @block.sync
        def _(sp):
            for dst, src in ((con[:], consts), (allcols[:], cols), (fix[:], fixed),
                             (xT, x_t.rearrange("(k p) t -> p k t", p=P))):
                sp.dma_start(dst, src).then_inc(loaded, 16)
            for s_ in B.freed_sems + T.freed_sems + used + rows_used + [joined]:
                sp.sem_inc(s_, 1)
            with sp.Fori(0, depth) as l:
                sp.wait_ge(joined, 3 * (l * NJOIN) + 1)
                sp.sem_inc(passed, 1)

                def fetch(name):
                    dst, slot, turn = block_at(name)
                    kind, i = name

                    def part(to, src):
                        sp.dma_start(to, src).then_inc(landed[slot], 16)
                    sp.wait_ge(used[slot], l * nblock[slot] + turn)
                    sp.sem_inc(passed, 1)
                    if kind == "ada":
                        part(v3(dst[:, 0:4096], 8), w_ada.rearrange("l (k p) n -> l p k n", p=P)[bass.ds(l, 1), :, :, i * 512:(i + 1) * 512].squeeze(0))
                    elif kind in ("rw", "gla", "dsa"):
                        c0, w = {"rw": lambda: (PR + 512 * i, RW_W[i]), "gla": lambda: ((GQ, 512), (GV, 512), (GA, 528))[i],
                                 "dsa": lambda: (QC, 452)}[kind]()
                        src = w_in.rearrange("l (k p) n -> l p k n", p=P)[bass.ds(l, 1), :, :, c0:c0 + w].squeeze(0)
                        part(v3(dst[:, 0:8 * w], 8), src)
                    elif kind == "up":
                        part(v3(dst[:, 0:2048], 2), w_uq.rearrange("l (k p) n -> l p k n", p=P)[bass.ds(l, 1)].squeeze(0))
                        part(v3(dst[:, 2048:2560], 2), w_iq.rearrange("l (k p) n -> l p k n", p=P)[bass.ds(l, 1)].squeeze(0))
                    elif kind in ("mac", "mb"):
                        part(dst[:, 0:24 * P], (w_mac if kind == "mac" else w_mb).rearrange("l m p n -> m l p n")[i, bass.ds(l, 1)].squeeze(0))
                    else:
                        w = w_out if kind == "out" else w_pq
                        part(v3(dst[:, 0:4096], 8), w.rearrange("l (k p) n -> l p k n", p=P)[bass.ds(l, 1), :, :, i * 512:(i + 1) * 512].squeeze(0))

                for n, name in enumerate(BLOCKS):
                    if n == 3:
                        sp.dma_start(sw[:], w_small[bass.ds(l, 1)].squeeze(0)).then_inc(small_landed, 16)
                    fetch(name)
            for k in range(KD):
                sp.wait_ge(stored, k + 1)
                sp.dma_start(out[k * P:(k + 1) * P, :], hT[:, k, :]).then_inc(loaded, 16)
            sp.wait_ge(loaded, 16 * (4 + KD))

        LANDED = {name: sum(2 if b == ("up", 0) else 1 for b in BLOCKS[i % RING:i + 1:RING]) for i, name in enumerate(BLOCKS)}
        LAND_N = [sum(2 if b == ("up", 0) else 1 for b in BLOCKS[i::RING]) for i in range(RING)]

        @block.tensor
        def _(pe):
            mm = nc.tensor.matmul

            def arrive(name, l):
                dst, slot, _ = block_at(name)
                pe.wait_ge(landed[slot], 16 * (l * LAND_N[slot] + LANDED[name]))
                return dst

            def leave(ins, name):
                ins.then_inc(used[block_at(name)[1]], 1)

            def opened(name, l, banks=B):
                pe.wait_ge(*banks.free(name, l))
                return psum[banks.bank(name)]

            def need(sig, l, k=None):
                pe.wait_ge(*G[sig].at(l, k))

            def summed(name, l, parts, n=NB):
                ps = opened(name, l)
                for i, (a, b) in enumerate(parts):
                    last = mm(ps[:, 0:n], a, b, start=(i == 0), stop=(i == len(parts) - 1))
                last.then_inc(B.filled(name), 1)
                return last

            def norm(l, w):
                need("squares", l, w + 1)
                summed(("ss", w), l, [(ones, hT[:, k, :]) for k in range(KD)])

            pe.wait_ge(loaded, 64)
            with pe.Fori(0, depth) as l:
                def adaln(part, blocks):
                    ps = opened(("mod", part), l)
                    for i in blocks:
                        w = v3(arrive(("ada", i), l)[:, 0:4096], 8)
                        for j in range(4):
                            for k in range(KD):
                                last = mm(ps[:, 4 * i + j:4 * i + j + 1], w[:, k, j * P:(j + 1) * P], cond[:, k:k + 1],
                                          start=(k == 0), stop=(k == KD - 1))
                        leave(last, ("ada", i))
                    pe.drain().then_inc(B.filled(("mod", part)), 1)

                norm(l, 0)
                need("cond_ready", l)
                adaln(0, range(4))
                need("h_ready", l, KD)

                def block_of(name, l, jobs, width):
                    w = v3(arrive(name, l)[:, 0:8 * width], 8)
                    for i, (job, j, m) in enumerate(jobs):
                        ps = opened(job, l)
                        for k in range(KD):
                            last = mm(ps[0:m, :], w[:, k, j:j + m], hT[:, k, :], start=(k == 0), stop=(k == KD - 1))
                        if i == len(jobs) - 1:
                            leave(last, name)
                            pe.drain().then_inc(B.filled(job), 1)
                        else:
                            last.then_inc(B.filled(job), 1)

                block_of(("rw", 3), l, [(("rp", 12), 0, P), (("rp", 13), P, P)], 256)
                pe.wait_ge(small_landed, 16 * (l + 1))
                need("lr_ready", l, 1)
                for c in range(4):
                    ps = opened(("z", c), l)
                    mm(ps[:, :], sw[0:64, SW_WA + c * P:SW_WA + (c + 1) * P], r_lr[0:64, :], start=True, stop=True).then_inc(B.filled(("z", c)), 1)
                for c in range(4):
                    ps = opened(("za", c), l)
                    mm(ps[:, :], sw[64:P, SW_WA + c * P:SW_WA + (c + 1) * P], r_lr[64:P, :], start=True, stop=True).then_inc(B.filled(("za", c)), 1)

                for i, c0 in ((1, 4), (0, 0), (2, 8)):
                    block_of(("rw", i), l, [(("rp", c0 + j), j * P, P) for j in range(4)], 512)
                need("kk_sq", l)
                for c in range(4):
                    summed(("kkn", c), l, [(bones, r_t1[:, c, :])])
                need("bon_in", l)
                for c in range(4):
                    summed(("bon", c), l, [(bones, r_t2[:, c, :])])
                need("rk_ready", l)
                need("s_zero", l)
                for t in range(TT):
                    adaln(t + 1, range(4 + 2 * t, 6 + 2 * t))
                    ts = slice(t * P, (t + 1) * P)
                    for nm, src in (("ab", r_kk), ("kb", r_k)):
                        for q in range(2):
                            for p in range(2):
                                ps = v3(opened((nm, t, p, q), l)[:, :], 2)
                                lo, hi = 64 * p, 64 * p + 64
                                for i in range(2):
                                    c = 2 * q + i
                                    last = mm(ps[:, i, :], src[lo:hi, c, ts], r_ar[lo:hi, c, t, :, :].rearrange("p w s -> p (w s)"),
                                              start=True, stop=True)
                                last.then_inc(B.filled((nm, t, p, q)), 1)
                    for wi, src in enumerate((r_kk, r_k, r_v)):
                        ps = opened(("tm", t, wi), l)
                        for c in range(4):
                            last = nc.tensor.transpose(ps[:, c * P:(c + 1) * P], src[:, c, ts], ident)
                        last.then_inc(B.filled(("tm", t, wi)), 1)
                    need("level_masked", l, 7 * t + 1)
                    for q in range(2):
                        ps = opened(("m0", t, q), l)
                        for i in range(4):
                            last = nc.tensor.transpose(ps[:, i * P:(i + 1) * P], r_m[0][:, 4 * q + i, :], ident)
                        last.then_inc(B.filled(("m0", t, q)), 1)
                    for lv in range(1, 7):
                        for q in range(2):
                            need("level_masked", l, 7 * t + lv + 1)
                            need("t_updated", l, 14 * t + 2 * (lv - 1) + q + 1)
                            ps = opened(("u", t, lv, q), l)
                            for i in range(4):
                                h = 4 * q + i
                                last = mm(ps[:, i * P:(i + 1) * P], r_m[lv % 2][:, h, :], r_tn[:, h, :], start=True, stop=True)
                            last.then_inc(B.filled(("u", t, lv, q)), 1)
                        for q in range(2):
                            need("u_copied", l, 12 * t + 2 * (lv - 1) + q + 1)
                            if lv < 6:
                                ps = opened(("tu", t, lv, q), l)
                                for i in range(4):
                                    h = 4 * q + i
                                    last = mm(ps[:, i * P:(i + 1) * P], r_tt[:, h, :], r_u[:, h, :], start=True, stop=True)
                                last.then_inc(B.filled(("tu", t, lv, q)), 1)
                            ps = opened(("ut", t, lv, q), l)
                            for i in range(4):
                                h = 4 * q + i
                                last = mm(ps[:, i * P:(i + 1) * P], r_u[:, h, :], r_tt[:, h, :], start=True, stop=True)
                            last.then_inc(B.filled(("ut", t, lv, q)), 1)
                    need("tm_copied", l, 3 * t + 3)
                    need("ab_masked", l, 8 * t + 8)
                    if t:
                        need("state", l, t)
                    for p in range(2):
                        ps = opened(("g", t, p), l)
                        lo, hi = 64 * p, 64 * p + 64
                        for c in range(4):
                            h = 2 * c + p
                            mm(ps[:, c * 64:c * 64 + 64], r_ar[lo:hi, c, t, 0, :], r_s[lo:hi, c, :], start=True, stop=False)
                            last = mm(ps[:, c * 64:c * 64 + 64], r_ak[:, h, 0:P], r_tm[:, 2, h * 64:h * 64 + 64], start=False, stop=True)
                        last.then_inc(B.filled(("g", t, p)), 1)
                    need("t_updated", l, 14 * (t + 1))
                    need("g_copied", l, 2 * (t + 1))
                    ps = opened(("sa", t), l)
                    for h in range(8):
                        last = mm(ps[:, h * 64:h * 64 + 64], r_tt[:, h, :], r_g[:, h, :], start=True, stop=True)
                    last.then_inc(B.filled(("sa", t)), 1)
                    need("sa_copied", l, t + 1)
                    for p in range(2):
                        ps = opened(("y", t, p), l)
                        lo, hi = 64 * p, 64 * p + 64
                        pe.sem_inc(passed, 1)
                        for c in range(4):
                            h = 2 * c + p
                            o = ps[lo:hi, c * P:(c + 1) * P]
                            mm(o, r_s[lo:hi, c, :], r_ar[lo:hi, c, t, 1, :], start=True, stop=False)
                            mm(o, r_sa[:, h, :], r_ab[:, h, P:2 * P], start=False, stop=False)
                            last = mm(o, r_tm[:, 2, h * 64:h * 64 + 64], r_ak[:, h, P:2 * P], start=False, stop=True)
                        last.then_inc(B.filled(("y", t, p)), 1)
                    if t < 3:
                        ps = opened(("s", t), l)
                        for h in range(8):
                            p, c = h % 2, h // 2
                            o = ps[64 * p:64 * p + 64, c * 64:c * 64 + 64]
                            mm(o, r_tm[:, 0, h * 64:h * 64 + 64], r_sa[:, h, :], start=True, stop=False)
                            last = mm(o, r_tm[:, 1, h * 64:h * 64 + 64], r_tm[:, 2, h * 64:h * 64 + 64], start=False, stop=True)
                        last.then_inc(B.filled(("s", t)), 1)
                need("y_copied", l)
                for c in range(4):
                    summed(("mu", c), l, [(bones, r_y[:, c, :])])
                for c in range(4):
                    need("y_sq", l, c + 1)
                    summed(("var", c), l, [(bones, r_t1[:, c, :])])
                for c in range(4):
                    summed(("g2", c), l, [(sw[:, SW_G2 + c * P:SW_G2 + (c + 1) * P], r_gl)])
                join(pe, l, 2)

                block_of(("gla", 0), l, [(("gq", c), c * P, P) for c in range(4)], 512)
                w = v3(arrive(("gla", 1), l)[:, 0:4096], 8)
                for t in range(TT):
                    ps = opened(("gv", t), l)
                    for k in range(KD):
                        last = mm(ps[:, :], hT[:, k, t * P:(t + 1) * P], w[:, k, :], start=(k == 0), stop=(k == KD - 1))
                    if t == TT - 1:
                        leave(last, ("gla", 1))
                        pe.drain().then_inc(B.filled(("gv", t)), 1)
                    else:
                        last.then_inc(B.filled(("gv", t)), 1)
                w = v3(arrive(("gla", 2), l)[:, 0:4224], 8)
                ps = opened(("ga", 0), l)
                for k in range(KD):
                    last = mm(ps[0:16, :], w[:, k, 0:16], hT[:, k, :], start=(k == 0), stop=(k == KD - 1))
                last.then_inc(B.filled(("ga", 0)), 1)
                need("gla_in", l, 9)
                for c in range(2):
                    ps = opened(("gz", c), l)
                    mm(ps[:, :], sw[0:16, SW_GA + c * P:SW_GA + (c + 1) * P], g_a[0:16, :], start=True, stop=True).then_inc(B.filled(("gz", c)), 1)
                block_of_jobs = [(("gr", c), 16 + c * P, P) for c in range(4)]
                for i, (job, j, m) in enumerate(block_of_jobs):
                    ps = opened(job, l)
                    for k in range(KD):
                        last = mm(ps[:, :], w[:, k, j:j + m], hT[:, k, :], start=(k == 0), stop=(k == KD - 1))
                    if i == 3:
                        leave(last, ("gla", 2))
                        pe.drain().then_inc(B.filled(job), 1)
                    else:
                        last.then_inc(B.filled(job), 1)
                need("gla_kd", l)
                for c in range(2):
                    ps = opened(("kt", c), l)
                    for t in range(TT):
                        last = nc.tensor.transpose(ps[:, t * P:(t + 1) * P], g_k[:, c, t * P:(t + 1) * P], ident)
                    last.then_inc(B.filled(("kt", c)), 1)
                need("kt_copied", l)
                need("gla_in", l, 13)
                for n in range(NCH):
                    lo, hi = 64 * (n % 2), 64 * (n % 2) + 64
                    ps = opened(("upd", n), l)
                    for c in range(2):
                        last = mm(ps[:, c * 256:(c + 1) * 256], g_tm[lo:hi, n // 2, c * P:(c + 1) * P],
                                  g_v[lo:hi, n // 2, c * 256:(c + 1) * 256], start=True, stop=True)
                    last.then_inc(B.filled(("upd", n)), 1)
                need("gla_state", l)
                for h in range(4):
                    lo, hi = 64 * (h % 2), 64 * (h % 2) + 64
                    ps = opened(("o", h), l)
                    for n in range(NCH):
                        last = mm(ps[:, n * 64:n * 64 + 64], g_st[lo:hi, n, h // 2, :], g_q[lo:hi, h // 2, n * 64:n * 64 + 64],
                                  start=True, stop=True)
                    last.then_inc(B.filled(("o", h)), 1)
                for h in range(4):
                    need("o_sq", l, h + 1)
                    summed(("on", h), l, [(ones, g_o2[:, h, :])])
                join(pe, l, 3)

                w = v3(arrive(("dsa", 0), l)[:, 0:8 * 452], 8)
                for c in range(3):
                    ps = opened(("qc", c), l)
                    for k in range(KD):
                        last = mm(ps[:, :], w[:, k, c * P:(c + 1) * P], hT[:, k, :], start=(k == 0), stop=(k == KD - 1))
                    last.then_inc(B.filled(("qc", c)), 1)
                ps = opened(("qc", 3), l)
                for p in range(2):
                    for k in range(KD):
                        last = mm(ps[64 * p:64 * p + 64, :], w[:, k, 384:448], hT[:, k, :], start=(k == 0), stop=(k == KD - 1))
                last.then_inc(B.filled(("qc", 3)), 1)
                ps = opened(("iw", 0), l)
                for t in range(TT):
                    for k in range(KD):
                        last = mm(ps[:, t * 4:t * 4 + 4], hT[:, k, t * P:(t + 1) * P], w[:, k, 448:452], start=(k == 0), stop=(k == KD - 1))
                leave(last, ("dsa", 0))
                pe.drain().then_inc(B.filled(("iw", 0)), 1)
                need("dsa_sq", l, 1)
                summed(("qn", 0), l, [(ones, d_sq[:, c, :]) for c in range(2)])
                need("dsa_sq", l, 2)
                summed(("kn", 0), l, [(ones, d_sq[:, 2, :])])
                up = arrive(("up", 0), l)
                w_q, w_i, w_v = v3(up[:, 0:2048], 2), v3(up[:, 2048:2560], 2), v3(sw[:, SW_UV:SW_N], 8)
                need("dsa_n", l, 1)
                for c in range(2):
                    summed(("iq", c), l, [(w_i[:, k, c * P:(c + 1) * P], d_qc[:, k, :]) for k in range(2)])
                need("iq_copied", l)
                need("dsa_in", l, 5)
                for b in range(1, 4):
                    for h in range(4):
                        lo, hi, w = 64 * (h % 2), 64 * (h % 2) + 64, P * (b + 1)
                        ps = opened(("ix", b, h), l)
                        mm(ps[:, 0:w], d_qi[lo:hi, h // 2, b * P:(b + 1) * P], d_ik[lo:hi, 0:w], start=True, stop=True)\
                            .then_inc(B.filled(("ix", b, h)), 1)
                for h in range(8):
                    ps = opened(("uq", h), l)
                    for k in range(2):
                        last = mm(ps[:, :], w_q[:, k, h * P:(h + 1) * P], d_qc[:, k, :], start=(k == 0), stop=(k == 1))
                    if h == 7:
                        leave(last, ("up", 0))
                        pe.drain().then_inc(B.filled(("uq", h)), 1)
                    else:
                        last.then_inc(B.filled(("uq", h)), 1)
                need("dsa_n", l, 2)
                ps = opened(("kvt", 0), l)
                for t in range(TT):
                    last = nc.tensor.transpose(ps[:, t * P:(t + 1) * P], d_kv[:, t * P:(t + 1) * P], ident)
                last.then_inc(B.filled(("kvt", 0)), 1)
                def gated(m, w, branches):
                    for i, (r, y) in enumerate(branches):
                        summed(("gt", m, r), l, [(w[:, i, k, :], hT[:, k, :]) for k in range(KD)])
                        ps = opened(("br", m, r), l)
                        for k in range(4):
                            last = mm(ps[:, :], w[:, i, 8 + k, :], y[:, k, :], start=(k == 0), stop=(k == 3))
                        if i == 0 and len(branches) == 2:
                            last.then_inc(B.filled(("br", m, r)), 1)
                    return last

                for m in range(KD):
                    w = arrive(("mac", m), l)[:, 0:24 * P].rearrange("p (r k n) -> p r k n", r=2, k=12)
                    leave(gated(m, w, ((0, ya), (2, yc))), ("mac", m))
                    pe.drain().then_inc(B.filled(("br", m, 2)), 1)
                need("uq_copied", l)
                need("kvt_copied", l)
                join(pe, l, 4)

                for i in range(QUADS + 3):
                    if 2 <= i < QUADS + 2:
                        n = i - 2
                        need("p_ready", l, n + 1)
                        for j in range(4):
                            ps = opened(("pt", n, j), l)
                            for s_ in range(n // 2 + 1):
                                last = nc.tensor.transpose(ps[:, s_ * P:(s_ + 1) * P], d_p[n % 2][j][:, s_ * P:(s_ + 1) * P], ident)
                            last.then_inc(B.filled(("pt", n, j)), 1)
                    if i < QUADS:
                        b = i // 2
                        for j in range(4):
                            ps = opened(("lg", i, j), l)
                            mm(ps[:, 0:P * (b + 1)], d_q[:, 4 * (i % 2) + j, b * P:(b + 1) * P], d_kv[:, 0:P * (b + 1)], start=True, stop=True)\
                                .then_inc(B.filled(("lg", i, j)), 1)
                    if i >= 3:
                        n = i - 3
                        ps = opened(("cx", n), l)
                        need("pt_copied", l, n + 1)
                        for j in range(4):
                            for s_ in range(n // 2 + 1):
                                last = mm(ps[:, j * P:(j + 1) * P], d_kt[:, s_, :], d_pt[n % 2][j][:, s_ * P:(s_ + 1) * P],
                                          start=(s_ == 0), stop=(s_ == n // 2))
                        last.then_inc(B.filled(("cx", n)), 1)
                need("cx_copied", l)
                for c in range(4):
                    ps = opened(("uv", c), l)
                    for p in range(2):
                        last = mm(ps[64 * p:64 * p + 64, :], w_v[:, 2 * c + p, :], d_cx[:, 2 * c + p, :], start=True, stop=True)
                    last.then_inc(B.filled(("uv", c)), 1)
                join(pe, l, 5)

                for i in range(4):
                    w = arrive(("mb", i), l)[:, 0:24 * P].rearrange("p (m k n) -> p m k n", m=2, k=12)
                    last = gated(2 * i, w[:, 0:1], ((1, yb),))
                    last.then_inc(B.filled(("br", 2 * i, 1)), 1)
                    leave(gated(2 * i + 1, w[:, 1:2], ((1, yb),)), ("mb", i))
                    pe.drain().then_inc(B.filled(("br", 2 * i + 1, 1)), 1)
                need("merged", l)

                for i in range(2):
                    w = v3(arrive(("out", i), l)[:, 0:4096], 8)
                    for j in range(4):
                        m = 4 * i + j
                        ps = opened(("wo", m), l)
                        for k in range(KD):
                            last = mm(ps[:, :], w[:, k, j * P:(j + 1) * P], m_o[:, k, :], start=(k == 0), stop=(k == KD - 1))
                        if j == 3:
                            leave(last, ("out", i))
                            pe.drain().then_inc(B.filled(("wo", m)), 1)
                        else:
                            last.then_inc(B.filled(("wo", m)), 1)
                join(pe, l, 6)
                norm(l, 1)
                need("h_ready", l, 2 * KD)
                join(pe, l, 7)
                def score(lap, banks, turn):
                    pe.wait_ge(*E_["tile_in"].at(lap))
                    for q in range(2):
                        for p in range(2):
                            ps = opened(("sc", p, q), turn, banks)
                            for i in range(4):
                                h = 4 * q + i
                                last = mm(ps[:, i * P:(i + 1) * P], e_qc[64 * p:64 * p + 64, h, :],
                                          sw[64 * p:64 * p + 64, SW_KEY + h * P:SW_KEY + (h + 1) * P], start=True, stop=True)
                            last.then_inc(banks.filled(("sc", p, q)), 1)

                w = [v3(arrive(("pq", i), l)[:, 0:4096], 8) for i in range(2)]
                for i in range(2):
                    ps = opened(("pq0", i), l)
                    for j in range(4):
                        for k in range(KD):
                            last = mm(ps[:, j * P:(j + 1) * P], w[i][:, k, j * P:(j + 1) * P], hT[:, k, 0:P], start=(k == 0), stop=(k == KD - 1))
                    last.then_inc(B.filled(("pq0", i)), 1)
                for h in range(EH):
                    ps = opened(("pq", h), l)
                    for k in range(KD):
                        last = mm(ps[:, P:S], w[h // 4][:, k, (h % 4) * P:(h % 4 + 1) * P], hT[:, k, P:S], start=(k == 0), stop=(k == KD - 1))
                    if h % 4 == 3:
                        leave(last, ("pq", h // 4))
                        pe.drain().then_inc(B.filled(("pq", h)), 1)
                    else:
                        last.then_inc(B.filled(("pq", h)), 1)
                    if h == 0:
                        score(l * TT, B, l)
                for t in range(TT):
                    for hf in range(2):
                        ps = opened(("h2", t, hf), l)
                        for i in range(4):
                            last = nc.tensor.transpose(ps[:, i * P:(i + 1) * P], hT[:, 4 * hf + i, t * P:(t + 1) * P], ident)
                        last.then_inc(B.filled(("h2", t, hf)), 1)
                join(pe, l, 8)

                def expert_tile(lap, more, t=None):
                    acc = [opened(("acc", j), lap, T) for j in range(2)]
                    pe.wait_ge(*E_["rows_in"].at(lap))
                    for j in range(2):
                        mm(acc[j][:, :], zeros[:], e_hc[:, 0:NB], start=True, stop=False)

                    def groups(g0, g1):
                        with pe.Fori(g0, g1) as g:
                            for s_ in range(GRP):
                                pe.wait_ge(diags[s_], lap * NGRP + g + 1)
                                for j in range(2):
                                    last = mm(acc[j][:, :], e_diag[:, s_, :], e_row[s_][:, D + j * NB:D + (j + 1) * NB], start=False, stop=False)
                                last.then_inc(rows_used[s_], 1)
                    groups(0, 1)
                    if more:
                        score(lap + 1, T, l * (TT - 1) + t)
                    groups(1, NGRP)
                    for j in range(2):
                        mm(acc[j][:, :], zeros[:], e_hc[:, 0:NB], start=False, stop=True).then_inc(T.filled(("acc", j)), 1)
                    pe.wait_ge(*E_["acc_copied"].at(lap))
                    for j in range(2):
                        ps = opened(("xt", j), lap, T)
                        for i in range(4):
                            last = nc.tensor.transpose(ps[:, i * P:(i + 1) * P], e_acc[:, j * NB + i * P:j * NB + (i + 1) * P], ident)
                        last.then_inc(T.filled(("xt", j)), 1)

                with pe.Fori(0, TT - 1) as t:
                    expert_tile(l * TT + t, True, t)
                expert_tile(l * TT + TT - 1, False)
                join(pe, l, 9)
            pe.wait_ge(G["squares"].sem, depth * 2 + 1)
            pe.wait_ge(T.freed_sems[0], 2)
            for k in range(KD):
                last = mm(psum[0][:, :], ones, hT[:, k, :], start=(k == 0), stop=(k == KD - 1))
            last.then_inc(stored_mm, 1)

        @block.scalar
        def _(act):
            A = nc.scalar.activation

            def need(sig, l, k=None):
                act.wait_ge(*G[sig].at(l, k))

            def full(name, l, banks=B):
                act.wait_ge(*banks.full(name, l))
                return psum[banks.bank(name)]

            def inv_roots(jobs, scale, eps, done):
                for out_, name in jobs:
                    ps = full(name, l)
                    A(out_, ps[:, :], ACT.Ln, bias=eps, scale=scale).then_inc(B.freed(name), 1)
                act.drain()
                for out_, name in jobs:
                    A(out_, out_, ACT.Exp, scale=-0.5).then_inc(done, 1)

            act.wait_ge(loaded, 64)
            act.wait_ge(const_set, 1)
            A(cond[:], fix[:, 0:KD], ACT.Silu)
            act.drain()
            with act.Fori(0, depth) as l:
                act.nop().then_inc(G["cond_ready"].sem, 1)

                def norm(w):
                    for k in range(KD):
                        last = A(hT[:, k, :], xT[:, k, :], ACT.Square)
                    last.then_inc(G["squares"].sem, 1)
                    inv_roots([(rstd[:], ("ss", w))], 1.0 / D, sc[:, 0:1], rstd_ready)
                    for k in range(KD):
                        act.wait_ge(scaled, (l * 2 + w) * KD + k + 1)
                        A(hT[:, k, :], hT[:, k, :], ACT.Identity, bias=modc[:, 24 * w + k:24 * w + k + 1]).then_inc(G["h_ready"].sem, 1)

                norm(0)
                def raw(i, c):
                    ps = full(("rp", c), l)
                    if i >= 2:
                        need("pt_used", l, i - 1)
                    A(r_pt[i % 2][:, 1:513], ps[:, :], ACT.Copy).then_inc(B.freed(("rp", c)), 1)
                    act.drain().then_inc(G["pt_ready"].sem, 1)

                order = (12, 13, 4, 5, 6, 7, 0, 1, 2, 3, 8, 9, 10, 11)
                for i in range(2):
                    raw(i, order[i])
                need("mixed", l, 1)
                A(r_lr[0:64, :], r_lr[0:64, :], ACT.Tanh).then_inc(G["lr_ready"].sem, 1)
                need("mixed", l, 2)
                A(r_gl, r_gl, ACT.Sigmoid).then_inc(G["lr_ready"].sem, 1)
                for nm, dst, b in (("z", r_sg, "rwkv_w0"), ("za", r_a, "rwkv_a0")):
                    for c in range(4):
                        ps = full((nm, c), l)
                        last = A(dst[:, c, :], ps[:, :], ACT.Sigmoid, bias=cl(b, c)).then_inc(B.freed((nm, c)), 1)
                    act.drain().then_inc(G["sig_ready"].sem, 1)
                for i in range(2, 14):
                    raw(i, order[i])
                need("kk_raw", l)
                A(r_t1, r_kk, ACT.Square).then_inc(G["kk_sq"].sem, 1)
                inv_roots([(r_t1[:, c, :], ("kkn", c)) for c in range(4)], 1.0, sc[:, 2:3], G["kk_rs"].sem)
                need("cs_done", l)
                A(r_sg, r_sg, ACT.Exp, scale=-KAPPA).then_inc(G["eprev"].sem, 1)
                A(r_f, r_f, ACT.Exp, scale=-KAPPA).then_inc(G["f_ready"].sem, 1)
                need("ar_half", l)
                A(r_sg, r_cs, ACT.Exp, scale=-KAPPA)
                act.drain().then_inc(G["ep"].sem, 1)
                A(r_cs, r_cs, ACT.Exp, scale=KAPPA).then_inc(G["em"].sem, 1)
                for t in range(TT):
                    for wi in range(3):
                        ps = full(("tm", t, wi), l)
                        if t and wi == 0:
                            need("state", l, t)
                        A(r_tm[:, wi, :], ps[:, :], ACT.Copy).then_inc(B.freed(("tm", t, wi)), 1)
                        act.drain().then_inc(G["tm_copied"].sem, 1)
                    for lv in range(1, 7):
                        for q in range(2):
                            ps = full(("u", t, lv, q), l)
                            if lv > 1:
                                need("t_updated", l, 14 * t + 2 * (lv - 1) + q + 1)
                            A(r_u[:, 4 * q:4 * q + 4, :], ps[:, :], ACT.Copy).then_inc(B.freed(("u", t, lv, q)), 1)
                            act.drain().then_inc(G["u_copied"].sem, 1)
                    for p in range(2):
                        ps = full(("g", t, p), l)
                        A(r_g[:, p:8:2, :], v3(ps[:, 0:256], 4), ACT.Copy).then_inc(B.freed(("g", t, p)), 1)
                        act.drain().then_inc(G["g_copied"].sem, 1)
                    ps = full(("sa", t), l)
                    A(r_sa, ps[:, :], ACT.Copy).then_inc(B.freed(("sa", t)), 1)
                    act.drain().then_inc(G["sa_copied"].sem, 1)
                    for p in range(2):
                        lo, hi = 64 * p, 64 * p + 64
                        ps = full(("y", t, p), l)
                        A(r_y[lo:hi, :, t * P:(t + 1) * P], v3(ps[lo:hi, :], 4), ACT.Copy).then_inc(B.freed(("y", t, p)), 1)
                        act.drain().then_inc(G["y_copied"].sem, 1)
                for c in range(4):
                    need("y_cent", l, c + 1)
                    A(r_t1[:, c, :], r_y[:, c, :], ACT.Square).then_inc(G["y_sq"].sem, 1)
                inv_roots([(r_t1[:, c, :], ("var", c)) for c in range(4)], 1.0 / 64, sc[:, 1:2], G["y_rs"].sem)
                join(act, l, 2)

                n_in = G["gla_in"].sem

                def copied(name, dst, func=ACT.Copy, scale=1.0, ps_of=lambda ps: ps[:, :]):
                    ps = full(name, l)
                    A(dst, ps_of(ps), func, scale=scale).then_inc(B.freed(name), 1)
                    return act.drain()

                for c in range(4):
                    copied(("gq", c), (g_q if c < 2 else g_k)[:, c % 2, :], scale=0.125 if c < 2 else 1.0).then_inc(n_in, 1)
                for t in range(TT):
                    copied(("gv", t), g_v[:, t, :]).then_inc(n_in, 1)
                copied(("ga", 0), g_a[0:16, :], ps_of=lambda ps: ps[0:16, :]).then_inc(n_in, 1)
                for c in range(2):
                    ps = full(("gz", c), l)
                    A(g_ab[:, c, :], ps[:, :], ACT.Abs, bias=cl("gla_b_a", c)).then_inc(G["gz_abs"].sem, 1)
                act.drain()
                for c in range(2):
                    A(g_ab[:, c, :], g_ab[:, c, :], ACT.Exp, scale=-1.0)
                act.drain()
                for c in range(2):
                    A(g_ab[:, c, :], g_ab[:, c, :], ACT.Ln, bias=sc[:, 3:4]).then_inc(G["gz_exp"].sem, 1)
                for c in range(4):
                    copied(("gr", c), g_r[:, c, :], ACT.Silu).then_inc(n_in, 1)
                need("gla_la", l)
                A(g_la, g_la, ACT.Exp, scale=1.0 / 16).then_inc(G["gla_dec"].sem, 1)
                A(g_dec, g_tot, ACT.Exp, scale=1.0 / 16).then_inc(G["gla_dec"].sem, 1)
                for c in range(2):
                    ps = full(("kt", c), l)
                    A(g_tm[:, :, c * P:(c + 1) * P], v3(ps[:, :], 4), ACT.Copy).then_inc(B.freed(("kt", c)), 1)
                    act.drain().then_inc(G["kt_copied"].sem, 1)
                for h in range(4):
                    ps = full(("o", h), l)
                    A(g_o2[:, h, :], ps[:, :], ACT.Square).then_inc(G["o_sq"].sem, 1)
                    A(g_o[:, h, :], ps[:, :], ACT.Copy).then_inc(B.freed(("o", h)), 1)
                inv_roots([(g_o2[:, h, :], ("on", h)) for h in range(4)], 1.0 / 128, sc[:, 0:1], G["o_rs"].sem)
                join(act, l, 3)

                d_in = G["dsa_in"].sem
                for c in range(2):
                    copied(("qc", c), d_qc[:, c, :]).then_inc(d_in, 1)
                    last = A(d_sq[:, c, :], d_qc[:, c, :], ACT.Square)
                last.then_inc(G["dsa_sq"].sem, 1)
                copied(("qc", 2), d_kv).then_inc(d_in, 1)
                A(d_sq[:, 2, :], d_kv, ACT.Square).then_inc(G["dsa_sq"].sem, 1)
                copied(("qc", 3), d_ik).then_inc(d_in, 1)
                copied(("iw", 0), d_iw.rearrange("p c t -> p (c t)"), ps_of=lambda ps: ps[:, 0:16]).then_inc(d_in, 1)
                inv_roots([(d_sq[:, 0, :], ("qn", 0))], 1.0 / 256, sc[:, 0:1], G["dsa_rs"].sem)
                inv_roots([(d_sq[:, 2, :], ("kn", 0))], 1.0 / 128, sc[:, 0:1], G["dsa_rs"].sem)
                for c in range(2):
                    copied(("iq", c), d_qi[:, c, :]).then_inc(G["iq_copied"].sem, 1)
                for i in range(12):
                    b, h = 1 + i // 4, i % 4
                    w = P * (b + 1)
                    ps = full(("ix", b, h), l)
                    if i >= 4:
                        need("relu_used", l, i - 3)
                    A(d_rl[h][:, 0:w], ps[:, 0:w], ACT.Relu).then_inc(B.freed(("ix", b, h)), 1)
                    act.drain().then_inc(G["relu"].sem, 1)
                for h in range(8):
                    copied(("uq", h), d_q[:, h, :]).then_inc(G["uq_copied"].sem, 1)
                copied(("kvt", 0), d_kt.rearrange("p c t -> p (c t)")).then_inc(G["kvt_copied"].sem, 1)

                def gates(i0, order):
                    for i, (m, r) in enumerate(order, i0):
                        ps = full(("gt", m, r), l)
                        if i >= 2:
                            need("gate_used", l, i - 1)
                        A(m_g[i % 2], ps[:, :], ACT.Sigmoid).then_inc(B.freed(("gt", m, r)), 1)
                        act.drain().then_inc(G["gate"].sem, 1)

                gates(0, [(m, r) for m in range(KD) for r in (0, 2)])
                join(act, l, 4)
                for i in range(QUADS + 3):
                    if i < QUADS:
                        w = P * (i // 2 + 1)
                        need("lg_max", l, i + 1)
                        for j in range(4):
                            A(d_p[i % 2][j][:, 0:w], d_p[i % 2][j][:, 0:w], ACT.Exp, bias=d_n[:, 4 * i + j:4 * i + j + 1], scale=P ** -0.5,
                              accum_out=d_sm[:, 4 * i + j:4 * i + j + 1])
                        act.drain().then_inc(G["lg_exp"].sem, 1)
                    if 2 <= i < QUADS + 2:
                        n = i - 2
                        w = P * (n // 2 + 1)
                        if n >= 2:
                            act.wait_ge(*B.full(("cx", n - 2), l))
                        for j in range(4):
                            ps = full(("pt", n, j), l)
                            A(d_pt[n % 2][j][:, 0:w], ps[:, 0:w], ACT.Copy).then_inc(B.freed(("pt", n, j)), 1)
                        act.drain().then_inc(G["pt_copied"].sem, 1)
                    if i >= 3:
                        n = i - 3
                        ps = full(("cx", n), l)
                        A(d_cx[:, 4 * (n % 2):4 * (n % 2) + 4, (n // 2) * P:(n // 2 + 1) * P], v3(ps[:, :], 4), ACT.Copy)\
                            .then_inc(B.freed(("cx", n)), 1)
                        act.drain().then_inc(G["cx_copied"].sem, 1)
                for c in range(4):
                    ps = full(("uv", c), l)
                    A(yb[:, c, :], ps[:, :], ACT.Copy).then_inc(B.freed(("uv", c)), 1)
                join(act, l, 5)
                gates(2 * KD, [(m, 1) for m in range(KD)])
                need("x_mixed", l)
                join(act, l, 6)
                norm(1)
                join(act, l, 7)
                def scores(banks, turn):
                    for q in range(2):
                        for p in range(2):
                            ps = full(("sc", p, q), turn, banks)
                            A(e_s[:, 8 * q + p:8 * q + 8:2, :], v3(ps[:, :], 4), ACT.Copy).then_inc(banks.freed(("sc", p, q)), 1)
                            act.drain().then_inc(E_["scored"].sem, 1)

                def soft(lap):
                    act.wait_ge(*E_["soft_in"].at(lap))
                    A(e_ex, e_ex, ACT.Exp).then_inc(E_["soft"].sem, 1)

                for i in range(2):
                    ps = full(("pq0", i), l)
                    A(e_qc[:, 4 * i:4 * i + 4, :], v3(ps[:, :], 4), ACT.Copy).then_inc(B.freed(("pq0", i)), 1)
                act.drain().then_inc(E_["tile_in"].sem, 1)
                for h in range(EH):
                    ps = full(("pq", h), l)
                    A(e_q[:, h, P:S], ps[:, P:S], ACT.Copy).then_inc(B.freed(("pq", h)), 1)
                    if h == 0:
                        scores(B, l)
                for t in range(TT):
                    for hf in range(2):
                        copied(("h2", t, hf), e_h[:, t, hf * NB:(hf + 1) * NB]).then_inc(G["h2_copied"].sem, 1)
                soft(l * TT)
                join(act, l, 8)

                def expert_tile(lap, t, more):
                    A(e_hc, e_h[:, t, :] if isinstance(t, int) else e_h.rearrange("p t d -> p (t d)")[:, bass.ds(t * D, D)], ACT.Copy)
                    act.drain().then_inc(E_["rows_in"].sem, 1)
                    act.wait_ge(*E_["routed"].at(lap))

                    def groups(g0, g1):
                        with act.Fori(g0, g1) as g:
                            turn = lap * NGRP + g
                            A(e_gc, e_gate[:, bass.ds(t * SLOTS + g * GRP, GRP)], ACT.Copy)
                            for s_ in range(GRP):
                                act.wait_ge(dots[s_], turn + 1)
                                A(e_ge[:, s_:s_ + 1], e_dot[:, s_:s_ + 1], ACT.Gelu)
                                act.drain()
                                A(e_wg[:, s_:s_ + 1], e_gc[:, s_:s_ + 1], ACT.Copy, scale=e_ge[:, s_:s_ + 1])
                                act.drain()
                                act.wait_ge(rows_used[s_], turn + 1)
                                A(e_diag[:, s_, :], ident, ACT.Copy, scale=e_wg[:, s_:s_ + 1]).then_inc(diags[s_], 1)
                    groups(0, 1)
                    if more:
                        A(e_qc, e_q[:, :, bass.ds((t + 1) * P, P)], ACT.Copy)
                        act.drain().then_inc(E_["tile_in"].sem, 1)
                        scores(T, l * (TT - 1) + t)
                        groups(1, PIECES[5] + 1)
                        soft(lap + 1)
                        groups(PIECES[5] + 1, NGRP)
                    else:
                        groups(1, NGRP)
                    for j in range(2):
                        ps = full(("acc", j), lap, T)
                        A(e_acc[:, j * NB:(j + 1) * NB], ps[:, :], ACT.Copy).then_inc(T.freed(("acc", j)), 1)
                    act.drain().then_inc(E_["acc_copied"].sem, 1)

                with act.Fori(0, TT - 1) as t:
                    expert_tile(l * TT + t, t, True)
                expert_tile(l * TT + TT - 1, TT - 1, False)
                join(act, l, 9)
            for k in range(KD):
                last = A(hT[:, k, :], xT[:, k, :], ACT.Square)
            last.then_inc(G["squares"].sem, 1)
            act.wait_ge(stored_mm, 1)
            A(rstd[:], psum[0][:, :], ACT.Ln, bias=sc[:, 0:1], scale=1.0 / D)
            act.drain()
            A(rstd[:], rstd[:], ACT.Exp, scale=-0.5).then_inc(rstd_ready, 1)

        @block.vector
        def _(dve):
            V = nc.vector

            def need(sig, l, k=None):
                dve.wait_ge(*G[sig].at(l, k))

            def full(name, l, banks=B):
                dve.wait_ge(*banks.full(name, l))
                return psum[banks.bank(name)]

            for i, e in enumerate((EPS, LN_EPS, KK_EPS, 1.0)):
                V.memset(sc[:, i:i + 1], e)
            V.memset(zeros[:], 0.0)
            V.memset(e_off[:], 0.0)
            dve.drain().then_inc(const_set, 1)
            dve.wait_ge(loaded, 64)
            with dve.Fori(0, depth) as l:
                V.tensor_copy(col[:], allcols[:, bass.ds(l * NCOL, NCOL)])
                V.memset(r_pt[0][:, 0:1], 0.0)
                V.memset(r_pt[1][:, 0:1], 0.0)
                dve.drain()
                ps = full(("mod", 0), l)
                V.tensor_tensor(modc[:, 0:16], ps[:, 0:16], cl("b_ada", 0, 16), ALU.add).then_inc(B.freed(("mod", 0)), 1)
                dve.drain()

                def gains(w, g):
                    V.scalar_tensor_tensor(out=gain[:, KD * w:KD * w + KD], in0=modc[:, 24 * w + 8:24 * w + 16], scalar=1.0,
                                           in1=cl(g, 0, KD), op0=ALU.add, op1=ALU.mult)
                gains(0, "g_norm_mix")
                V.tensor_scalar(omka[:], cl("rwkv_k_a", 0, 4), -1.0, 1.0, ALU.mult, ALU.add)
                dve.drain()

                def norm(w):
                    dve.wait_ge(rstd_ready, l * 2 + w + 1)
                    for k in range(KD):
                        V.scalar_tensor_tensor(out=hT[:, k, :], in0=xT[:, k, :], scalar=gain[:, KD * w + k:KD * w + k + 1],
                                               in1=rstd[:], op0=ALU.mult, op1=ALU.mult).then_inc(scaled, 1)

                norm(0)
                dst_of = {12: r_lr, 13: r_gl, **{c: r_r[:, c, :] for c in range(4)},
                          **{4 + c: r_k[:, c, :] for c in range(4)}, **{8 + c: r_v[:, c, :] for c in range(4)}}
                for i, c in enumerate((12, 13, 4, 5, 6, 7, 0, 1, 2, 3, 8, 9, 10, 11)):
                    need("pt_ready", l, i + 1)
                    pt, d = r_pt[i % 2], dst_of[c]
                    V.tensor_tensor(d, pt[:, 0:512], pt[:, 1:513], ALU.subtract)
                    dve.drain()
                    V.scalar_tensor_tensor(out=d, in0=d, scalar=cl("rwkv_mu", c), in1=pt[:, 1:513], op0=ALU.mult, op1=ALU.add)\
                        .then_inc(G["mixed"].sem, 1)
                    dve.drain().then_inc(G["pt_used"].sem, 1)
                    if i == 5:
                        need("sig_ready", l, 2)
                        for c_ in range(4):
                            V.tensor_tensor_scan(r_cs[:, c_, :], m128, r_sg[:, c_, :], 0.0, ALU.mult, ALU.add)
                        for c_ in range(4):
                            V.tensor_scalar(r_kk[:, c_, :], r_k[:, c_, :], cl("rwkv_k_k", c_), None, ALU.mult)
                        dve.drain().then_inc(G["kk_raw"].sem, 1)
                        cs16 = r_cs.rearrange("p c (t s) -> p (c t) s", t=4)
                        V.tensor_copy(r_mid, cs16[:, :, 63])
                        dve.drain()
                        V.tensor_tensor(cs16, cs16, bc(r_mid.unsqueeze(2), [P, 16, P]), ALU.subtract)
                        dve.drain()
                        V.tensor_tensor(r_sg, r_cs, r_sg, ALU.subtract)
                        V.tensor_tensor(v3(r_f, 4), r_cs.rearrange("p c (t s) -> p c t s", t=4)[:, :, 0:3, 127],
                                        v3(r_mid, 4)[:, :, 1:4], ALU.add)
                        dve.drain().then_inc(G["cs_done"].sem, 1)
                        for c_ in range(4):
                            V.tensor_scalar(r_t2[:, c_, :], r_a[:, c_, :], cl("rwkv_k_a", c_), omka[:, c_:c_ + 1], ALU.mult, ALU.add)
                        dve.drain()
                        V.tensor_tensor(r_k, r_k, r_t2, ALU.mult)
                        dve.drain()
                for c in range(4):
                    V.scalar_tensor_tensor(out=r_t2[:, c, :], in0=r_r[:, c, :], scalar=cl("rwkv_r_k", c), in1=r_k[:, c, :],
                                           op0=ALU.mult, op1=ALU.mult)
                dve.drain().then_inc(G["bon_in"].sem, 1)
                for c in range(4):
                    need("kk_rs", l, c + 1)
                    V.tensor_tensor(r_kk[:, c, :], r_kk[:, c, :], r_t1[:, c, :], ALU.mult)
                for c in range(4):
                    ps = full(("bon", c), l)
                    V.tensor_tensor(r_bon[:, c, :], ps[:, :], r_v[:, c, :], ALU.mult).then_inc(B.freed(("bon", c)), 1)
                need("eprev", l)
                dve.sem_inc(passed, 1)
                dve.drain()
                half = [r_ar[:, :, :, w, :].rearrange("p c t s -> p (c t) s") for w in range(2)]

                def by_tile(x):
                    return x.rearrange("p c (t s) -> p (c t) s", t=4)
                V.scalar_tensor_tensor(out=half[0], in0=by_tile(r_kk), scalar=-1.0, in1=by_tile(r_sg), op0=ALU.mult, op1=ALU.mult)
                V.tensor_tensor(r_kk, r_kk, r_a, ALU.mult)
                dve.drain().then_inc(G["ar_half"].sem, 1)
                need("ep", l)
                V.tensor_tensor(half[1], by_tile(r_r), by_tile(r_sg), ALU.mult)
                need("em", l)
                V.tensor_tensor(r_kk, r_kk, r_cs, ALU.mult)
                V.tensor_tensor(r_k, r_k, r_cs, ALU.mult)
                dve.drain().then_inc(G["rk_ready"].sem, 1)
                V.memset(r_s, 0.0).then_inc(G["s_zero"].sem, 1)
                need("f_ready", l)
                for t in range(TT):
                    ps = full(("mod", t + 1), l)
                    m0, m1 = 16 + 8 * t, 24 + 8 * t
                    V.tensor_tensor(modc[:, m0:m1], ps[:, m0:m1], cl("b_ada", m0, 8), ALU.add).then_inc(B.freed(("mod", t + 1)), 1)
                    if t:
                        need("y_copied", l, 2 * t)
                    for nm, dst in (("ab", r_ab), ("kb", r_ak)):
                        for q in range(2):
                            for p in range(2):
                                ps = full((nm, t, p, q), l)
                                V.tensor_tensor(dst[:, 4 * q + p:4 * q + 4:2, :], v3(ps[:, :], 2), bc(tri.unsqueeze(1), [P, 2, 2 * P]), ALU.mult)\
                                    .then_inc(B.freed((nm, t, p, q)), 1)
                                dve.drain().then_inc(G["ab_masked"].sem, 1)

                    if t:
                        need("sa_copied", l, t)
                    need("level_masked", l, 7 * t + 1)
                    V.tensor_tensor(r_tt, r_m[0], bc(ident.unsqueeze(1), [P, 8, P]), ALU.add)
                    for q in range(2):
                        ps = full(("m0", t, q), l)
                        V.tensor_tensor(r_tn[:, 4 * q:4 * q + 4, :], v3(ps[:, :], 4), bc(ident.unsqueeze(1), [P, 4, P]), ALU.add)\
                            .then_inc(B.freed(("m0", t, q)), 1)
                        dve.drain().then_inc(G["t_updated"].sem, 1)
                    for lv in range(1, 7):
                        for q in range(2):
                            hs = slice(4 * q, 4 * q + 4)
                            full(("ut", t, lv, q), l)
                            if lv < 6:
                                ps = full(("tu", t, lv, q), l)
                                V.tensor_tensor(r_tn[:, hs, :], v3(ps[:, :], 4), r_tn[:, hs, :], ALU.add).then_inc(B.freed(("tu", t, lv, q)), 1)
                            ps = full(("ut", t, lv, q), l)
                            V.tensor_tensor(r_tt[:, hs, :], v3(ps[:, :], 4), r_tt[:, hs, :], ALU.add).then_inc(B.freed(("ut", t, lv, q)), 1)
                            dve.drain().then_inc(G["t_updated"].sem, 1)
                    if t < 3:
                        ps = full(("s", t), l)
                        V.tensor_tensor(r_s, v3(ps[:, 0:256], 4), r_s, ALU.add).then_inc(B.freed(("s", t)), 1)
                        dve.drain()
                        V.tensor_tensor(r_s, r_s, bc(v3(r_f, 4)[:, :, t:t + 1], [P, 4, 64]), ALU.mult)
                        dve.drain().then_inc(G["state"].sem, 1)
                gains(1, "g_norm_ffn")
                need("y_copied", l)
                for c in range(4):
                    ps = full(("mu", c), l)
                    V.scalar_tensor_tensor(out=r_y[:, c, :], in0=ps[:, :], scalar=-1.0 / 64, in1=r_y[:, c, :], op0=ALU.mult, op1=ALU.add)\
                        .then_inc(B.freed(("mu", c)), 1)
                    dve.drain().then_inc(G["y_cent"].sem, 1)
                for c in range(4):
                    need("y_rs", l, c + 1)
                    V.tensor_tensor(r_y[:, c, :], r_y[:, c, :], r_t1[:, c, :], ALU.mult)
                    dve.drain()
                    V.tensor_scalar(r_y[:, c, :], r_y[:, c, :], cl("rwkv_ln_g", c), cl("rwkv_ln_b", c), ALU.mult, ALU.add)
                    dve.drain()
                    V.tensor_tensor(r_y[:, c, :], r_y[:, c, :], r_bon[:, c, :], ALU.add)
                    dve.drain()
                    ps = full(("g2", c), l)
                    V.tensor_tensor(yc[:, c, :], ps[:, :], r_y[:, c, :], ALU.mult).then_inc(B.freed(("g2", c)), 1)
                V.nop().then_inc(G["state"].sem, 1)
                join(dve, l, 2)

                for c in range(2):
                    need("gz_abs", l, c + 1)
                    ps = full(("gz", c), l)
                    V.tensor_scalar(g_la[:, c, :], ps[:, :], cl("gla_b_a", c), 0.0, ALU.add, ALU.min).then_inc(B.freed(("gz", c)), 1)
                need("gz_exp", l)
                dve.sem_inc(passed, 1)
                dve.drain()
                V.tensor_tensor(g_la, g_la, g_ab, ALU.subtract)
                dve.drain()
                for c in range(2):
                    V.tensor_tensor_scan(g_cum[:, c, :], m64, g_la[:, c, :], 0.0, ALU.mult, ALU.add)
                dve.drain()
                cum = g_cum.rearrange("p c (n s) -> p (c n) s", n=NCH)
                V.tensor_copy(g_tot.rearrange("p c n -> p (c n)"), cum[:, :, 63])
                dve.drain()
                V.tensor_tensor(g_la.rearrange("p c (n s) -> p (c n) s", n=NCH), bc(g_tot.rearrange("p c n -> p (c n)").unsqueeze(2), [P, 16, 64]),
                                cum, ALU.subtract)
                dve.drain().then_inc(G["gla_la"].sem, 1)
                need("gla_dec", l)
                need("gla_in", l, 4)
                V.tensor_tensor(g_k, g_k, g_la, ALU.mult).then_inc(G["gla_kd"].sem, 1)
                for n in range(NCH):
                    ps = full(("upd", n), l)
                    for c in range(2):
                        for p in range(2):
                            lo, hi = 64 * p, 64 * p + 64
                            src = ps[lo:hi, c * 256 + p * P:c * 256 + (p + 1) * P]
                            if n == 0:
                                last = V.tensor_copy(g_st[lo:hi, n, c, :], src)
                            else:
                                last = V.scalar_tensor_tensor(out=g_st[lo:hi, n, c, :], in0=g_st[lo:hi, n - 1, c, :],
                                                              scalar=g_dec[lo:hi, c, n:n + 1], in1=src, op0=ALU.mult, op1=ALU.add)
                    last.then_inc(B.freed(("upd", n)), 1)
                    dve.drain().then_inc(G["gla_state"].sem, 1)
                need("gla_in", l, 13)
                for h in range(4):
                    need("o_rs", l, h + 1)
                    V.scalar_tensor_tensor(out=g_o[:, h, :], in0=g_o[:, h, :], scalar=cl("gla_g_o"), in1=g_o2[:, h, :], op0=ALU.mult, op1=ALU.mult)
                    dve.drain()
                    V.tensor_tensor(ya[:, h, :], g_o[:, h, :], g_r[:, h, :], ALU.mult)
                join(dve, l, 3)

                need("dsa_rs", l, 1)
                for c in range(2):
                    last = V.scalar_tensor_tensor(out=d_qc[:, c, :], in0=d_qc[:, c, :], scalar=cl("dsa_g_qc", c), in1=d_sq[:, 0, :],
                                                  op0=ALU.mult, op1=ALU.mult)
                dve.drain().then_inc(G["dsa_n"].sem, 1)
                need("dsa_rs", l, 2)
                V.scalar_tensor_tensor(out=d_kv, in0=d_kv, scalar=cl("dsa_g_kv"), in1=d_sq[:, 2, :], op0=ALU.mult, op1=ALU.mult)\
                    .then_inc(G["dsa_n"].sem, 1)
                V.memset(d_nm[:, 0, 0:P], 0.0)
                dve.drain()
                V.memset(d_nm[0:64, 0, 64:P], DROP)
                for b in range(1, 4):
                    w = P * (b + 1)
                    s_ = d_nm[:, b, 0:w]
                    for h in range(4):
                        need("relu", l, (b - 1) * 4 + h + 1)
                        if h == 0:
                            V.tensor_scalar(s_, d_rl[h][:, 0:w], d_iw[:, b, h:h + 1], None, ALU.mult).then_inc(G["relu_used"].sem, 1)
                        else:
                            V.scalar_tensor_tensor(out=s_, in0=d_rl[h][:, 0:w], scalar=d_iw[:, b, h:h + 1], in1=s_, op0=ALU.mult, op1=ALU.add)\
                                .then_inc(G["relu_used"].sem, 1)
                        dve.drain()
                    V.memset(d_nm[0:64, b, w - 64:w], NEG)
                    dve.drain()

                def pick(n):
                    b = 1 + n // (TOPK // 8)
                    s_ = d_nm[:, b, 0:P * (b + 1)]
                    V.max(d_m8, s_)
                    dve.drain()
                    V.match_replace(s_, d_m8, s_, MARK)
                    dve.drain()
                    if n % (TOPK // 8) == TOPK // 8 - 1:
                        V.tensor_scalar(s_, s_, MARK, -DROP, ALU.is_equal, ALU.mult)
                        dve.drain()
                        V.tensor_scalar(s_, s_, DROP, None, ALU.add)
                        dve.drain()

                def merge(i, m, r):
                    need("gate", l, i + 1)
                    ps = full(("br", m, r), l)
                    dst = m_o[:, m, :] if r == 0 else m_t
                    V.tensor_tensor(dst, ps[:, :], m_g[i % 2], ALU.mult).then_inc(B.freed(("br", m, r)), 1)
                    dve.drain().then_inc(G["gate_used"].sem, 1)
                    if r:
                        V.tensor_tensor(m_o[:, m, :], m_o[:, m, :], m_t, ALU.add)
                        dve.drain()

                rounds = 3 * (TOPK // 8) // KD
                for m in range(KD):
                    for n in range(rounds * m, rounds * (m + 1)):
                        if n == rounds * m + rounds // 2:
                            merge(2 * m, m, 0)
                        pick(n)
                    merge(2 * m + 1, m, 2)
                join(dve, l, 4)
                for i in range(QUADS + 1):
                    if i >= 1:
                        n = i - 1
                        w = P * (n // 2 + 1)
                        need("lg_exp", l, n + 1)
                        V.reciprocal(d_mx[:, 4 * n:4 * n + 4], d_sm[:, 4 * n:4 * n + 4])
                        dve.drain()
                        for j in range(4):
                            V.tensor_scalar(d_p[n % 2][j][:, 0:w], d_p[n % 2][j][:, 0:w], d_mx[:, 4 * n + j:4 * n + j + 1], None, ALU.mult)
                        dve.drain().then_inc(G["p_ready"].sem, 1)
                    if i < QUADS:
                        b = i // 2
                        w = P * (b + 1)
                        for j in range(4):
                            ps = full(("lg", i, j), l)
                            if i >= 2:
                                dve.wait_ge(*B.full(("pt", i - 2, j), l))
                            dve.sem_inc(passed, 1)
                            V.tensor_tensor_reduce(d_p[i % 2][j][:, 0:w], ps[:, 0:w], d_nm[:, b, 0:w], 1.0, NEG, ALU.add, ALU.max,
                                                   d_mx[:, 4 * i + j:4 * i + j + 1]).then_inc(B.freed(("lg", i, j)), 1)
                        dve.drain()
                        V.tensor_scalar(d_n[:, 4 * i:4 * i + 4], d_mx[:, 4 * i:4 * i + 4], -(P ** -0.5), None, ALU.mult)
                        dve.drain().then_inc(G["lg_max"].sem, 1)
                join(dve, l, 5)

                for m in range(KD):
                    merge(2 * KD + m, m, 1)
                V.nop().then_inc(G["merged"].sem, 1)
                for m in range(KD):
                    ps = full(("wo", m), l)
                    V.scalar_tensor_tensor(out=xT[:, m, :], in0=ps[:, :], scalar=modc[:, 16 + m:17 + m], in1=xT[:, m, :], op0=ALU.mult, op1=ALU.add)\
                        .then_inc(B.freed(("wo", m)), 1)
                    dve.drain().then_inc(G["x_mixed"].sem, 1)
                join(dve, l, 6)
                norm(1)
                join(dve, l, 7)

                c4 = e_c.rearrange("p h (a b) -> p h a b", a=ET)
                pos = e_pos.rearrange("p h k -> p (h k)")

                def best(r, vals, places, src, n):
                    for g in range(n):
                        V.max(vals[:, g, 8 * r:8 * r + 8], src[:, g, :])
                    dve.drain()

                def places_of(r, vals, places, src, n):
                    for g in range(n):
                        V.max_index(places[:, g, 8 * r:8 * r + 8], vals[:, g, 8 * r:8 * r + 8], src[:, g, :])
                    dve.drain()

                def strike(vals, src, n):
                    for g in range(n):
                        V.match_replace(src[:, g, :], vals[:, g, 0:8], src[:, g, :], NEG)
                    dve.drain()

                def piece(i, lap, t):
                    if i == 0:
                        dve.wait_ge(*E_["scored"].at(lap))
                        dve.sem_inc(passed, 1)
                        best(0, e_v, e_i, e_s, 16)
                        places_of(0, e_v, e_i, e_s, 16)
                    elif i == 1:
                        strike(e_v, e_s, 16)
                        best(1, e_v, e_i, e_s, 16)
                    elif i == 2:
                        places_of(1, e_v, e_i, e_s, 16)
                        V.tensor_copy(e_if, e_i)
                        for h in range(EH):
                            V.tensor_tensor(c4[:, h], bc(e_v[:, 2 * h, :].unsqueeze(2), [P, ET, ET]),
                                            bc(e_v[:, 2 * h + 1, :].unsqueeze(1), [P, ET, ET]), ALU.add)
                        dve.drain()
                    elif i == 3:
                        best(0, e_top, e_pos, e_c, EH)
                        places_of(0, e_top, e_pos, e_c, EH)
                    elif i == 4:
                        strike(e_top, e_c, EH)
                        best(1, e_top, e_pos, e_c, EH)
                    elif i == 5:
                        places_of(1, e_top, e_pos, e_c, EH)
                        V.tensor_tensor(e_ex, e_top, bc(e_top[:, :, 0:1], [P, EH, ET]), ALU.subtract)
                        V.tensor_scalar(e_pa, pos, 4, None, ALU.logical_shift_right)
                        V.tensor_scalar(e_pb, pos, 15, None, ALU.bitwise_and)
                        dve.drain().then_inc(E_["soft_in"].sem, 1)
                        V.tensor_copy(e_paf, e_pa)
                        V.tensor_copy(e_pbf, e_pb)
                        dve.drain()
                    elif i == 6:
                        for pf, oh in ((e_paf, e_oh), (e_pbf, e_oh2)):
                            V.tensor_tensor(oh.rearrange("p (k j) -> p k j", j=ET), bc(pf.unsqueeze(2), [P, SLOTS, ET]),
                                            bc(iota16.unsqueeze(1), [P, SLOTS, ET]), ALU.is_equal)
                        dve.drain()
                        for half_, oh in enumerate((e_oh, e_oh2)):
                            o4 = oh.rearrange("p (h k j) -> p h k j", h=EH, j=ET)
                            for h in range(EH):
                                V.tensor_tensor(o4[:, h], o4[:, h], bc(e_if[:, 2 * h + half_, :].unsqueeze(1), [P, ET, ET]), ALU.mult)
                        dve.drain()
                    else:
                        for oh, dst in ((e_oh, e_n1), (e_oh2, e_n2)):
                            V.tensor_reduce(dst, oh.rearrange("p (k j) -> p k j", j=ET), AX.X, ALU.add)
                        dve.drain()
                        V.scalar_tensor_tensor(out=e_n1, in0=e_n1, scalar=float(NK), in1=e_n2, op0=ALU.mult, op1=ALU.add)
                        dve.drain()
                        V.tensor_scalar(e_idx[:, bass.ds(t * SLOTS, SLOTS)], e_n1, e_off[:, 0:1], None, ALU.add)
                        dve.wait_ge(*E_["soft"].at(lap))
                        V.tensor_reduce(e_sum, e_ex, AX.X, ALU.add)
                        dve.drain()
                        V.reciprocal(e_sum, e_sum)
                        dve.drain()
                        V.tensor_tensor(v3(e_gate[:, bass.ds(t * SLOTS, SLOTS)], 8), e_ex, bc(e_sum.unsqueeze(2), [P, EH, ET]), ALU.mult)
                        dve.drain().then_inc(E_["routed"].sem, 1)

                def expert_tile(lap, t, more):
                    dve.wait_ge(*E_["rows_in"].at(lap))
                    dve.sem_inc(passed, 1)

                    def groups(g0, g1):
                        with dve.Fori(g0, g1) as g:
                            turn = lap * NGRP + g
                            for s_ in range(GRP):
                                dve.wait_ge(rows_landed[s_], 16 * (turn + 1))
                                dve.wait_ge(rows_used[s_], turn + 1)
                                V.tensor_tensor_reduce(e_row[s_][:, 0:D], e_row[s_][:, 0:D], e_hc, 1.0, 0.0, ALU.mult, ALU.add, e_dot[:, s_:s_ + 1])
                                dve.drain().then_inc(dots[s_], 1)
                    g0 = 0
                    if more:
                        for i, g1 in enumerate(PIECES):
                            groups(g0, g1 + 1)
                            piece(i, lap + 1, t + 1)
                            g0 = g1 + 1
                    groups(g0, NGRP)
                    for j in range(2):
                        ps = full(("xt", j), lap, T)
                        for i in range(4):
                            k = 4 * j + i
                            xs = xT[:, k, bass.ds(t * P, P)]
                            last = V.scalar_tensor_tensor(out=xs, in0=ps[:, i * P:(i + 1) * P], scalar=modc[:, 40 + k:41 + k], in1=xs,
                                                          op0=ALU.mult, op1=ALU.add)
                        last.then_inc(T.freed(("xt", j)), 1)
                    dve.drain().then_inc(E_["tile_out"].sem, 1)

                for i in range(len(PIECES)):
                    if i == len(PIECES) - 1:
                        need("h2_copied", l)
                    piece(i, l * TT, 0)
                join(dve, l, 8)
                with dve.Fori(0, TT - 1) as t:
                    expert_tile(l * TT + t, t, True)
                expert_tile(l * TT + TT - 1, TT - 1, False)
                V.tensor_scalar(e_off[:], e_off[:], float(NE), None, ALU.add)
                join(dve, l, 9)
            dve.wait_ge(rstd_ready, depth * 2 + 1)
            for k in range(KD):
                V.scalar_tensor_tensor(out=hT[:, k, :], in0=xT[:, k, :], scalar=fix[:, KD + k:KD + k + 1], in1=rstd[:],
                                       op0=ALU.mult, op1=ALU.mult).then_inc(stored, 1)

        @block.gpsimd
        def _(pool):
            def need(sig, l, k=None):
                pool.wait_ge(*G[sig].at(l, k))

            pool.wait_ge(loaded, 64)
            with pool.Fori(0, depth) as l:
                for t in range(TT):
                    need("ab_masked", l, 8 * t + 4)
                    for lv in range(7):
                        if lv == 2:
                            need("t_updated", l, 14 * t + 2)
                        elif lv > 2:
                            need("u_copied", l, 12 * t + 2 * (lv - 2))
                        elif t and lv == 0:
                            need("u_copied", l, 12 * t)
                        for h0 in range(0, 8, 4):
                            last = nc.gpsimd.tensor_tensor(r_m[lv % 2][:, h0:h0 + 4, :], r_ab[:, h0:h0 + 4, 0:P],
                                                           bc(lvl[:, lv, :].unsqueeze(1), [P, 4, P]), ALU.mult)
                        last.then_inc(G["level_masked"].sem, 1)
                with pool.Fori(0, TT) as t:
                    lap = l * TT + t
                    pool.wait_ge(*E_["routed"].at(lap))
                    pool.sem_inc(passed, 1)
                    with pool.Fori(0, NGRP) as g:
                        turn = lap * NGRP + g
                        for s_ in range(GRP):
                            pool.wait_ge(rows_used[s_], turn + 1)
                            pool.sem_inc(passed, 1)
                            pool.tensor_copy(e_ic[:, s_:s_ + 1], e_idx[:, bass.ds(t * SLOTS + g * GRP + s_, 1)]).then_inc(idx_ready, 1)
                            pool.wait_ge(idx_ready, turn * GRP + s_ + 1)
                            pool.sem_inc(passed, 1)
                            pool.indirect_dma_start(e_row[s_], None, uv, bass.IndirectOffsetOnAxis(ap=e_ic[:, s_:s_ + 1], axis=0))\
                                .then_inc(rows_landed[s_], 16)


_COLS = ('b_ada', 'g_norm_mix', 'g_norm_ffn', 'gla_b_a', 'gla_g_o', 'dsa_g_qc', 'dsa_g_kv', 'rwkv_mu', 'rwkv_w0', 'rwkv_a0',
         'rwkv_k_k', 'rwkv_k_a', 'rwkv_r_k', 'rwkv_ln_g', 'rwkv_ln_b')


def constants():
    i = np.arange(P)
    s, t = i[:, None], i[None, :]
    lv = [((t >> j) % 2 == 1) & ((s >> j) == (t >> j) - 1) for j in range(7)]
    col = np.arange(S)[None, :] + 0 * s
    parts = [s == t, s >= 0 * t, s // 64 == t // 64, s < t, s <= t, *lv, col % CH != 0, col % P != 0]
    iota = np.arange(ET)[None, :] + 0 * s
    return np.concatenate([np.broadcast_to(p, (P, p.shape[1])) for p in parts] + [iota], axis=1).astype(np.float32)


def laid_out(a):
    f = {k: np.asarray(v) for k, v in a.items()}

    def column(v):
        return np.swapaxes(v.reshape(L, -1, P), 1, 2)

    cols = np.concatenate([column(f[n].reshape(L, -1)) for n in _COLS], axis=2)
    cols = np.ascontiguousarray(cols.transpose(1, 0, 2).reshape(P, L * NCOL))
    fixed = np.concatenate([f['c'].reshape(KD, P).T, f['g_final'].reshape(KD, P).T], axis=1)
    keys = f['peer_keys'].transpose(0, 2, 4, 1, 3).reshape(L, P, EH * NK)
    ga = np.concatenate([f['gla_w_a2'], np.zeros((L, P - 16, 256), np.float32)], axis=1)
    small = np.concatenate([ga, np.concatenate([f['rwkv_w_w2'], f['rwkv_w_a2']], axis=1), f['rwkv_w_g2'], keys,
                            f['dsa_w_uv'].transpose(0, 2, 1, 3).reshape(L, P, 512)], axis=2)
    gates = f['w_in'][:, :, GATES:].reshape(L, 8, P, 3, 8, P).transpose(0, 4, 2, 3, 1, 5)
    branch = f['w_branch'].reshape(L, 3, 4, P, 8, P).transpose(0, 4, 3, 1, 2, 5)
    merge = np.concatenate([gates, branch], axis=4)
    w_mac = merge[:, :, :, 0::2].reshape(L, 8, P, 24 * P)
    w_mb = merge[:, :, :, 1].reshape(L, 4, 2, P, 12, P).transpose(0, 1, 3, 2, 4, 5).reshape(L, 4, P, 24 * P)
    return dict(fixed=fixed, cols=cols, consts=constants(), x_t=f['x'].reshape(S, D).T, w_ada=f['w_ada'], w_in=f['w_in'],
                w_small=small, w_uq=f['dsa_w_uq'], w_iq=f['dsa_w_iq'], w_mac=w_mac, w_mb=w_mb, w_out=f['w_out'],
                w_pq=f['peer_w_q'], uv=np.concatenate([f['peer_u'], f['peer_v']], axis=2).reshape(L * NE, 2 * D))


def kernel(**inputs):
    import concourse.bacc as _bacc
    from concourse.bass_utils import run_bass_kernel_spmd as _run

    nc = _bacc.Bacc("TRN2", target_bir_lowering=False, num_devices=1)
    arrays = {k: np.ascontiguousarray(v) for k, v in laid_out(inputs).items()}
    args = [nc.dram_tensor(k, v.shape, F32, kind="ExternalInput").ap() for k, v in arrays.items()]
    out = nc.dram_tensor("out", (D, S), F32, kind="ExternalOutput").ap()
    trunk(nc, *args, out)
    r = _run(nc, [arrays], core_ids=[0])
    return np.ascontiguousarray(r.results[0]["out"].T).reshape(1, S, D)
```

```python
from contextlib import ExitStack

import numpy as np

import concourse.bass as bass
from concourse import mybir

F32 = mybir.dt.float32
U32 = mybir.dt.uint32
ALU = mybir.AluOpType
ACT = mybir.ActivationFunctionType
AX = mybir.AxisListType

P = 128
L, S, D = 2, 512, 1024
TT, KD = S // P, D // P
NB = 512
IN_W = 6868
GQ, GV, GA, QC, PR, GATES = 0, 512, 1024, 1552, 2004, 3796
CH, NCH = 64, S // 64
TOPK = 128
QUADS = 8
NEG, MARK, DROP = -3.0e38, -3.3e38, -1.0e30
EPS, LN_EPS, KK_EPS = 1e-6, 64e-5, 1e-12
KAPPA = float(np.exp(-0.5))
EH, ET, NK, NE = 8, 16, 128, 16384
SLOTS = EH * ET
RING = 2
GRP = 8
NGRP = EH * ET // GRP
PIECES = (1, 3, 4, 6, 8, 9, 11, 13)

COLS = {}
_at = 0
for _n, _w in (("b_ada", 48), ("g_norm_mix", 8), ("g_norm_ffn", 8), ("gla_b_a", 2), ("gla_g_o", 1), ("dsa_g_qc", 2),
               ("dsa_g_kv", 1), ("rwkv_mu", 14), ("rwkv_w0", 4), ("rwkv_a0", 4), ("rwkv_k_k", 4), ("rwkv_k_a", 4),
               ("rwkv_r_k", 4), ("rwkv_ln_g", 4), ("rwkv_ln_b", 4)):
    COLS[_n] = _at
    _at += _w
NCOL = _at

CONST = {}
_at = 0
for _n, _w in (("ident", P), ("ones", P), ("bones", P), ("tri", 2 * P), ("lvl", 7 * P), ("m64", S), ("m128", S), ("iota", ET)):
    CONST[_n] = (_at, _at + _w)
    _at += _w
NCONST = _at

SW_GA, SW_WA, SW_G2, SW_KEY, SW_UV, SW_N = 0, 256, 768, 1280, 2304, 2816

BLOCKS = ([("ada", i) for i in range(3)] + [("rw", i) for i in (3, 1, 0, 2)] + [("gla", 0), ("gla", 1), ("gla", 2)]
          + [("dsa", 0), ("up", 0)] + [("mac", m) for m in range(8)] + [("mb", m) for m in range(4)] + [("out", 0), ("out", 1)] + [("pq", 0), ("pq", 1)])
RW_W = (512, 512, 512, 256)
ADA_AFTER = {("ada", 1): 2, ("rw", 1): 3, ("rw", 0): 4, ("rw", 2): 9}
ADA_RING = 3
ADA_HALVES = 18
ADA_LENT = (3, 17)


class Banks:

    def __init__(self, sem, prefix, order):
        self.n = {name: i for i, name in enumerate(order)}
        assert len(self.n) == len(order)
        self.filled_sems = [sem(f"{prefix}_filled{b}") for b in range(8)]
        self.freed_sems = [sem(f"{prefix}_freed{b}") for b in range(8)]
        self.per = [len(range(b, len(order), 8)) for b in range(8)]

    def bank(self, name):
        return self.n[name] % 8

    def filled(self, name):
        return self.filled_sems[self.bank(name)]

    def freed(self, name):
        return self.freed_sems[self.bank(name)]

    def full(self, name, lap):
        b = self.bank(name)
        return self.filled_sems[b], lap * self.per[b] + (self.n[name] // 8 + 1)

    def free(self, name, lap):
        b = self.bank(name)
        return self.freed_sems[b], lap * self.per[b] + (self.n[name] // 8 + 1)


def rwkv_steps():
    units = [(t, q) for t in range(TT) for q in range(2)]
    for step in range(5 * (len(units) - 1) + 10):
        for half in range(2):
            for u, (t, q) in enumerate(units):
                if 0 <= step - 5 * u < 10:
                    yield half, t, q, step - 5 * u


def layer_banks():
    o = [("ss", 0), ("mod", 0)]
    o += [("rp", c) for c in (12, 13)] + [("z", c) for c in range(4)] + [("za", c) for c in range(4)]
    o += [("rp", c) for c in (4, 5, 6, 7, 0, 1, 2, 3)] + [("mod", 1)] + [("rp", c) for c in (8, 9, 10, 11)]
    o += [("kkn", c) for c in range(4)] + [("bon", c) for c in range(4)] + [("mod", 2)]
    for half, t, q, stage in rwkv_steps():
        if stage == 0:
            o += [("tm", t, q, 0), ("tm", t, q, 1)] if half else \
                [(x, t, p, q) for x in ("ab", "kb") for p in range(2)]
        elif stage == 1:
            o += [] if half else [("m0", t, q)]
        elif stage < 8:
            o += ([("tu", t, stage - 1, q)] if stage < 7 else []) + [("ut", t, stage - 1, q)] if half else [("u", t, stage - 1, q)]
        elif stage == 8:
            o += [("sa", t, q)] if half else [("g", t, 0, q), ("g", t, 1, q)]
        else:
            o += ([("s", t, q)] if t < TT - 1 else []) if half else [("y", t, 0, q), ("y", t, 1, q)]
    o += [("mu", c) for c in range(4)] + [("gq", c) for c in range(2)] + [("var", c) for c in range(4)]
    o += [("gq", c) for c in (2, 3)] + [("g2", c) for c in range(4)]
    o += [("gv", t) for t in range(TT)] + [("ga", 0)] + [("gz", c) for c in range(2)]
    o += [("gr", c) for c in range(4)] + [("qc", 0)] + [("kt", c) for c in range(2)] + [("qc", 1)] + [("upd", n) for n in range(NCH)]
    o += [("qc", 2), ("qc", 3), ("iw", 0), ("qn", 0), ("kn", 0)] + [("o", h) for h in range(4)] + [("iq", c) for c in range(2)]
    o += [("on", h) for h in range(4)]
    o += [("ix", b, h) for b in range(1, 4) for h in range(4)] + [("uq", h) for h in range(8)] + [("kvt", 0)]
    o += [x for m in range(KD) for r in (0, 2) for x in (("gt", m, r), ("br", m, r))]
    for i in range(QUADS + 3):
        o += [("pt", i - 2, j) for j in range(4)] if 2 <= i < QUADS + 2 else []
        o += [("lg", i, j) for j in range(4)] if i < QUADS else []
        o += [("cx", i - 3)] if i >= 3 else []
    o += [("uv", c) for c in range(4)]
    o += [x for m in range(KD) for x in (("gt", m, 1), ("br", m, 1))]
    o += [("wo", m) for m in range(KD)] + [("ss", 1)]
    o += [x for i in range(2) for x in (("pq0", i), ("pq", i), ("sc", 0, i), ("sc", 1, i))] + [("pq", h) for h in range(2, EH)]
    o += [("h2", t, h) for t in range(TT) for h in range(2)]
    return o


TILE_BANKS = [("sc", p, q) for q in range(2) for p in range(2)] + [("acc", 0), ("acc", 1), ("xt", 0), ("xt", 1)]


def trunk(nc, fixed, cols, consts, x_t, w_ada, w_in, w_small, w_uq, w_iq, w_mac, w_mb, w_out, w_pq, uv, out,
          depth=L, stop=None):
    ctx = ExitStack()
    with ctx:
        def sb(name, n, dt=F32):
            return ctx.enter_context(nc.sbuf_tensor(name, [P, n], dt))

        def sem(name):
            return ctx.enter_context(nc.semaphore(name))

        psum = [ctx.enter_context(nc.psum_tensor(f"bank{b}", [P, NB], F32)) for b in range(8)]

        def v3(ap, c):
            return ap.rearrange("p (c t) -> p c t", c=c)

        con = sb("con", NCONST)
        xT = v3(sb("xT", KD * S)[:], KD)
        hT = v3(sb("hT", KD * S)[:], KD)
        allcols = sb("allcols", L * NCOL)
        col = sb("col", NCOL)
        fix = sb("fix", 2 * KD)
        sc = sb("sc", 64)
        cond = sb("cond", KD)
        modc = sb("modc", 48)
        gain = sb("gain", 2 * KD)
        omka = sb("omka", 4)
        sw = sb("sw", SW_N)
        rstd = sb("rstd", S)
        SLOT = 36 * P
        REG = 37700
        reg = sb("reg", REG)
        ring = [reg[:, i * SLOT:(i + 1) * SLOT] for i in range(RING)]
        base = RING * SLOT
        ya, yb, yc = (v3(reg[:, base + i * 2048:base + (i + 1) * 2048], 4) for i in range(3))
        base += 3 * 2048

        def at(o, n, dt=None):
            assert base + o + n <= REG, (base + o + n, REG)
            r = reg[:, base + o:base + o + n]
            return r if dt is None else r.bitcast(dt)

        def const(name):
            a, b = CONST[name]
            return con[:, a:b]

        ident, ones, bones = const("ident"), const("ones"), const("bones")
        tri, lvl, m64, m128, iota16 = const("tri"), v3(const("lvl"), 7), const("m64"), const("m128"), const("iota")

        def cl(name, i=0, n=1, p0=0, p1=P):
            return col[p0:p1, COLS[name] + i:COLS[name] + i + n]

        a_half = [v3(y.rearrange("p c t -> p (c t)"), 8) for y in (ya, yb)]
        a_sum = [*(yc[:, i, :] for i in range(4)), *(at(20482 + i * 512, 512) for i in range(3))]
        a_at = [a_sum[i] for i in (0, 1, 2, 3, 4, 5, 6, 0, 1, 2, 3, 4)]
        r_pt = [at(19456 + i * 513, 513) for i in range(2)]
        r_r, r_k, r_v = (v3(at(i * 2048, 2048), 4) for i in range(3))
        r_lr, r_gl = at(6144, 512), at(6656, 512)
        r_sg, r_cs, r_a = (v3(at(7168 + i * 2048, 2048), 4) for i in range(3))
        r_kk = v3(at(13312, 2048), 4)
        r_x = at(15360, 4096)
        r_t1, r_t2 = v3(r_x[:, 0:2048], 4), v3(r_x[:, 2048:4096], 4)
        r_ar = r_x.rearrange("p (c t w s) -> p c t w s", c=4, t=4, w=2)
        r_bon, r_y = yb, ya
        r_tm = v3(at(19456, 1536), 3)
        r_g, r_sa = v3(at(20992, 512), 8), v3(at(21504, 512), 8)
        r_s = v3(at(22018, 256), 4)
        r_mid, r_f = at(22274, 16), at(22290, 12)
        r_ab = v3(at(7168, 2048), 8)
        r_ak = v3(at(9216, 2048), 8)
        r_tt, r_tn = v3(at(11264, 1024), 8), v3(at(0, 1024), 8)
        r_u = v3(at(1024, 1024), 8)
        r_m = [v3(at(12288, 1024), 8), v3(yc.rearrange("p c t -> p (c t)")[:, 0:1024], 8)]
        g_q, g_k = v3(at(0, 1024), 2), v3(at(1024, 1024), 2)
        g_v = v3(at(2048, 2048), 4)
        g_a, g_r = at(4096, 512), v3(at(4608, 2048), 4)
        g_la, g_cum, g_ab = (v3(at(6656 + i * 1024, 1024), 2) for i in range(3))
        g_tm = v3(at(9728, 1024), 4)
        g_st = at(10752, 2048).rearrange("p (n c v) -> p n c v", n=NCH, c=2)
        g_o, g_o2 = v3(at(12800, 2048), 4), v3(at(14848, 2048), 4)
        g_tot, g_dec = v3(at(16896, 16), 2), v3(at(16912, 16), 2)
        d_qc, d_kv, d_ik = v3(at(17408, 1024), 2), at(19584, 512), at(20096, 512)
        d_qi, d_kt = v3(at(2048, 1024), 2), v3(at(3072, 512), 4)
        d_sq = v3(at(20608, 1536), 3)
        d_q = v3(at(5120, 4096), 8)
        d_cx = d_q
        d_nm = v3(at(13312, 2048), 4)
        d_rl = [at(15360 + i * 512, 512) for i in range(4)]
        d_p = [d_rl, [at(o, 512) for o in (0, 512, 1536, 2048)]]
        d_pt = [[at(17408 + i * 512, 512) for i in range(4)], [at(o, 512) for o in (2560, 3584, 4096, 4608)]]
        d_iw = v3(at(19456, 16), 4)
        d_m8 = at(19472, 8)
        d_mx, d_sm, d_n = at(19480, 32), at(19512, 32), at(19544, 32)
        m_g = [d_pt[0][0], d_pt[0][1]]
        m_t = d_pt[0][2]
        m_o = v3(at(9216, 4096), 8)
        free_first = BLOCKS.index(("pq", 0)) % RING
        e_row = [reg[:, i * 2048:(i + 1) * 2048] for i in (5, 6, 7, *((3, 4, 2, 0, 1) if free_first else (0, 1, 2, 3, 4)))]

        def ep(o, n, dt=None):
            assert GRP * 2048 + o + n <= REG
            r = reg[:, GRP * 2048 + o:GRP * 2048 + o + n]
            return r if dt is None else r.bitcast(dt)

        e_q, e_h = v3(ep(0, 4096), 8), v3(ep(4096, 4096), 4)
        e_qc, e_hc = v3(ep(8192, 1024), 8), ep(9216, 1024)
        e_s = v3(ep(10240, 2048), 16)
        e_c = v3(ep(12288, 2048), 8)
        e_oh = ep(14336, 2048)
        e_oh2 = ep(16384, 2048)
        e_v = v3(ep(18432, 256), 16)
        e_i = v3(ep(18688, 256, U32), 16)
        e_if = v3(ep(18944, 256), 16)
        e_top, e_pos = v3(ep(19200, 128), 8), v3(ep(19328, 128, U32), 8)
        e_pa, e_paf = ep(19456, 128, U32), ep(19584, 128)
        e_pb, e_pbf = ep(19712, 128, U32), ep(19840, 128)
        e_n1, e_n2 = ep(19968, 128), ep(20096, 128)
        e_ex, e_gate = v3(ep(20224, 128), 8), ep(20528, TT * SLOTS)
        e_sum = ep(20480, 8)
        hflat = hT.rearrange("p k t -> p (k t)")
        e_idx = sb("e_idx", TT * SLOTS, U32)
        e_ic = sb("e_ic", GRP, U32)
        e_diag = v3(hflat[:, 512:512 + GRP * P], GRP)
        e_dot, e_ge, e_wg, e_gc = (ep(20488 + i * 8, 8) for i in range(4))
        e_acc = e_oh
        e_off = sb("e_off", 1)
        zeros = sb("zeros", P)

        loaded = sem("loaded")
        landed = [sem(f"block_landed{i}") for i in range(RING)]
        used = [sem(f"block_used{i}") for i in range(RING)]
        nblock = [len(range(i, len(BLOCKS), RING)) for i in range(RING)]
        ada_landed = [sem(f"ada_half_landed{i}") for i in range(2)]
        ada_used = [sem(f"ada_half_used{i}") for i in range(2)]
        small_landed = sem("small_landed")
        joined = sem("joined")
        stored = sem("stored")
        B = Banks(sem, "layer", layer_banks())
        T = Banks(sem, "tile", TILE_BANKS)

        class Sig:
            def __init__(self, name, n):
                self.sem, self.n = sem(name), n

            def at(self, lap, k=None):
                return self.sem, lap * self.n + (self.n if k is None else k)

        G = {n: Sig(n, k) for n, k in (
            ("squares", 2), ("h_ready", 2 * KD), ("cond_ready", 1), ("ada_summed", 6), ("ada_half_summed", ADA_HALVES - 4),
            ("pt_ready", 14), ("pt_used", 14), ("mixed", 14), ("lr_ready", 2), ("sig_ready", 2),
            ("kk_raw", 1), ("kk_sq", 1), ("kk_rs", 4), ("bon_in", 1), ("cs_done", 1), ("eprev", 1), ("ep", 1), ("em", 1),
            ("f_ready", 1), ("ar_half", 1), ("rk_ready", 1), ("s_zero", 1),
            ("ab_masked", 8 * TT), ("tm_copied", 2 * TT), ("g_copied", 2 * TT), ("sa_copied", 2 * TT), ("y_copied", 2 * TT), ("state", 2 * TT - 2),
            ("level_masked0", 7 * TT), ("level_masked1", 7 * TT), ("t_updated0", 13 * TT), ("t_updated1", 13 * TT),
            ("u_copied0", 6 * TT), ("u_copied1", 6 * TT),
            ("y_cent", 4), ("y_sq", 4), ("y_rs", 4),
            ("gla_in", 13), ("gz_abs", 2), ("gz_exp", 2), ("gla_la", 1), ("gla_dec", 2), ("gla_kd", 1), ("kt_copied", 2),
            ("gla_state", NCH), ("o_sq", 4), ("o_rs", 4),
            ("dsa_in", 5), ("dsa_sq", 2), ("dsa_rs", 2), ("dsa_n", 2), ("iq_copied", 2), ("relu", 12), ("relu_used", 12),
            ("uq_copied", 8), ("kvt_copied", 1), ("lg_max", QUADS), ("lg_exp", QUADS), ("p_ready", QUADS), ("pt_copied", QUADS), ("cx_copied", QUADS),
            ("gate", 24), ("gate_used", 24), ("merged", 1), ("x_mixed", KD),
            ("h2_copied", 2 * TT))}
        E_ = {n: Sig(n, k) for n, k in (
            ("tile_in", 2), ("rows_in", 1), ("scored", 4), ("routed", 2), ("soft_in", 1), ("soft", 1), ("acc_copied", 1), ("tile_out", 1),
            ("idx_used", 1))}
        rows_landed = [sem(f"rows_landed{s}") for s in range(GRP)]
        rows_used = [sem(f"rows_used{s}") for s in range(GRP)]
        dots = [sem(f"dot{s}") for s in range(GRP)]
        diags = [sem(f"diag{s}") for s in range(GRP)]
        idx_ready = sem("idx_ready")
        passed = sem("passed")
        const_set = sem("const_set")
        rstd_ready = sem("rstd_ready")
        scaled = sem("scaled")
        stored_mm = sem("final_sum")

        NJOIN = 7

        def join(eng, lap, k, n=NJOIN):
            eng.sem_inc(passed, 1)
            eng.drain().then_inc(joined, 1)
            eng.wait_ge(joined, 3 * (lap * n + k - 1) + 1)
            eng.sem_inc(passed, 1)

        def block_at(name):
            i = BLOCKS.index(name)
            return ring[i % RING], i % RING, i // RING + 1

        def stop_at(name):
            return stop is not None and stop == name

        def bc(ap, shape):
            return ap.to_broadcast(shape)

        block = ctx.enter_context(nc.Block())

        @block.sync
        def _(sp):
            for dst, src in ((con[:], consts), (allcols[:], cols), (fix[:], fixed),
                             (xT, x_t.rearrange("(k p) t -> p k t", p=P))):
                sp.dma_start(dst, src).then_inc(loaded, 16)
            for s_ in B.freed_sems + T.freed_sems + used + ada_used + rows_used + [joined]:
                sp.sem_inc(s_, 1)
            with sp.Fori(0, depth) as l:
                sp.wait_ge(joined, 3 * (l * NJOIN) + 1)
                sp.sem_inc(passed, 1)

                def fetch(name):
                    dst, slot, turn = block_at(name)
                    kind, i = name

                    def part(to, src):
                        sp.dma_start(to, src).then_inc(landed[slot], 16)
                    sp.wait_ge(used[slot], l * nblock[slot] + turn)
                    sp.sem_inc(passed, 1)
                    if kind == "ada":
                        part(v3(dst[:, 0:4096], 8), w_ada.rearrange("l (k p) n -> l p k n", p=P)[bass.ds(l, 1), :, :, i * 512:(i + 1) * 512].squeeze(0))
                    elif kind in ("rw", "gla", "dsa"):
                        c0, w = {"rw": lambda: (PR + 512 * i, RW_W[i]), "gla": lambda: ((GQ, 512), (GV, 512), (GA, 528))[i],
                                 "dsa": lambda: (QC, 452)}[kind]()
                        src = w_in.rearrange("l (k p) n -> l p k n", p=P)[bass.ds(l, 1), :, :, c0:c0 + w].squeeze(0)
                        part(v3(dst[:, 0:8 * w], 8), src)
                    elif kind == "up":
                        part(v3(dst[:, 0:2048], 2), w_uq.rearrange("l (k p) n -> l p k n", p=P)[bass.ds(l, 1)].squeeze(0))
                        part(v3(dst[:, 2048:2560], 2), w_iq.rearrange("l (k p) n -> l p k n", p=P)[bass.ds(l, 1)].squeeze(0))
                    elif kind in ("mac", "mb"):
                        part(dst[:, 0:24 * P], (w_mac if kind == "mac" else w_mb).rearrange("l m p n -> m l p n")[i, bass.ds(l, 1)].squeeze(0))
                    else:
                        w = w_out if kind == "out" else w_pq
                        part(v3(dst[:, 0:4096], 8), w.rearrange("l (k p) n -> l p k n", p=P)[bass.ds(l, 1), :, :, i * 512:(i + 1) * 512].squeeze(0))

                halves = 0
                for n, name in enumerate(BLOCKS):
                    if name == ("rw", 3):
                        sp.dma_start(sw[:], w_small[bass.ds(l, 1)].squeeze(0)).then_inc(small_landed, 16)
                    fetch(name)
                    for _ in range(ADA_AFTER.get(name, 0)):
                        sp.wait_ge(ada_used[halves % 2], l * (ADA_HALVES // 2) + halves // 2 + 1)
                        sp.sem_inc(passed, 1)
                        c0 = ADA_RING * 512 + halves * 256
                        sp.dma_start(a_half[halves % 2], w_ada.rearrange("l (k p) n -> l p k n", p=P)[bass.ds(l, 1), :, :, c0:c0 + 256].squeeze(0))\
                            .then_inc(ada_landed[halves % 2], 16)
                        halves += 1
                assert halves == ADA_HALVES
            for k in range(KD):
                sp.wait_ge(stored, k + 1)
                sp.dma_start(out[k * P:(k + 1) * P, :], hT[:, k, :]).then_inc(loaded, 16)
            sp.wait_ge(loaded, 16 * (4 + KD))

        LANDED = {name: sum(2 if b == ("up", 0) else 1 for b in BLOCKS[i % RING:i + 1:RING]) for i, name in enumerate(BLOCKS)}
        LAND_N = [sum(2 if b == ("up", 0) else 1 for b in BLOCKS[i::RING]) for i in range(RING)]

        @block.tensor
        def _(pe):
            mm = nc.tensor.matmul

            def arrive(name, l):
                dst, slot, _ = block_at(name)
                pe.wait_ge(landed[slot], 16 * (l * LAND_N[slot] + LANDED[name]))
                return dst

            def leave(ins, name):
                ins.then_inc(used[block_at(name)[1]], 1)

            def opened(name, l, banks=B):
                pe.wait_ge(*banks.free(name, l))
                return psum[banks.bank(name)]

            def need(sig, l, k=None):
                pe.wait_ge(*G[sig].at(l, k))

            def summed(name, l, parts, n=NB):
                ps = opened(name, l)
                for i, (a, b) in enumerate(parts):
                    last = mm(ps[:, 0:n], a, b, start=(i == 0), stop=(i == len(parts) - 1))
                last.then_inc(B.filled(name), 1)
                return last

            def norm(l, w):
                need("squares", l, w + 1)
                summed(("ss", w), l, [(ones, hT[:, k, :]) for k in range(KD)])

            pe.wait_ge(loaded, 64)
            with pe.Fori(0, depth) as l:
                def adaln(part):
                    ps = opened(("mod", part), l)
                    for j in range(16):
                        if part == 0 and j % 4 == 0:
                            need("ada_summed", l, j // 4 + 1)
                        last = mm(ps[:, 16 * part + j:16 * part + j + 1], a_at[4 * part + j // 4][:, j % 4 * P:(j % 4 + 1) * P], ones[:, 0:1],
                                  start=True, stop=True)
                    pe.drain().then_inc(B.filled(("mod", part)), 1)

                norm(l, 0)
                adaln(0)
                need("h_ready", l, KD)

                def block_of(name, l, jobs, width):
                    w = v3(arrive(name, l)[:, 0:8 * width], 8)
                    for i, (job, j, m) in enumerate(jobs):
                        ps = opened(job, l)
                        for k in range(KD):
                            last = mm(ps[0:m, :], w[:, k, j:j + m], hT[:, k, :], start=(k == 0), stop=(k == KD - 1))
                        if i == len(jobs) - 1:
                            leave(last, name)
                            pe.drain().then_inc(B.filled(job), 1)
                        else:
                            last.then_inc(B.filled(job), 1)

                block_of(("rw", 3), l, [(("rp", 12), 0, P), (("rp", 13), P, P)], 256)
                pe.wait_ge(small_landed, 16 * (l + 1))
                need("lr_ready", l, 1)
                for c in range(4):
                    ps = opened(("z", c), l)
                    mm(ps[:, :], sw[0:64, SW_WA + c * P:SW_WA + (c + 1) * P], r_lr[0:64, :], start=True, stop=True).then_inc(B.filled(("z", c)), 1)
                for c in range(4):
                    ps = opened(("za", c), l)
                    mm(ps[:, :], sw[64:P, SW_WA + c * P:SW_WA + (c + 1) * P], r_lr[64:P, :], start=True, stop=True).then_inc(B.filled(("za", c)), 1)

                for i, c0 in ((1, 4), (0, 0), (2, 8)):
                    if i == 2:
                        need("ada_half_summed", l, 7)
                        need("ada_summed", l, 5)
                        adaln(1)
                    block_of(("rw", i), l, [(("rp", c0 + j), j * P, P) for j in range(4)], 512)
                need("kk_sq", l)
                for c in range(4):
                    summed(("kkn", c), l, [(bones, r_t1[:, c, :])])
                need("bon_in", l)
                for c in range(4):
                    summed(("bon", c), l, [(bones, r_t2[:, c, :])])
                need("ada_half_summed", l)
                need("ada_summed", l)
                adaln(2)
                need("rk_ready", l)
                need("s_zero", l)
                for half, t, q, stage in rwkv_steps():
                    ts, heads, cs = slice(t * P, (t + 1) * P), range(4 * q, 4 * q + 4), (2 * q, 2 * q + 1)
                    if stage == 0 and not half:
                        for nm, src in (("ab", r_kk), ("kb", r_k)):
                            for p in range(2):
                                ps = v3(opened((nm, t, p, q), l)[:, :], 2)
                                lo, hi = 64 * p, 64 * p + 64
                                for i, c in enumerate(cs):
                                    last = mm(ps[:, i, :], src[lo:hi, c, ts], r_ar[lo:hi, c, t, :, :].rearrange("p w s -> p (w s)"),
                                              start=True, stop=True)
                                last.then_inc(B.filled((nm, t, p, q)), 1)
                    elif stage == 0:
                        for w, srcs in enumerate(((r_kk, r_k), (r_v,))):
                            ps = opened(("tm", t, q, w), l)
                            for i, (src, c) in enumerate([(x, c) for x in srcs for c in cs]):
                                last = nc.tensor.transpose(ps[:, i * P:(i + 1) * P], src[:, c, ts], ident)
                            last.then_inc(B.filled(("tm", t, q, w)), 1)
                    elif stage == 1 and not half:
                        need(f"level_masked{q}", l, 7 * t + 1)
                        ps = opened(("m0", t, q), l)
                        for i, h in enumerate(heads):
                            last = nc.tensor.transpose(ps[:, i * P:(i + 1) * P], r_m[0][:, h, :], ident)
                        last.then_inc(B.filled(("m0", t, q)), 1)
                    elif 1 < stage < 8 and not half:
                        lv = stage - 1
                        need(f"level_masked{q}", l, 7 * t + lv + 1)
                        need(f"t_updated{q}", l, 13 * t + 2 * lv - 1)
                        ps = opened(("u", t, lv, q), l)
                        for i, h in enumerate(heads):
                            last = mm(ps[:, i * P:(i + 1) * P], r_m[lv % 2][:, h, :], r_tn[:, h, :], start=True, stop=True)
                        last.then_inc(B.filled(("u", t, lv, q)), 1)
                    elif 1 < stage < 8:
                        lv = stage - 1
                        need(f"u_copied{q}", l, 6 * t + lv)
                        need(f"t_updated{q}", l, 13 * t + 2 * lv)
                        for nm, a_, b_ in ((("tu", r_tt, r_u),) if lv < 6 else ()) + (("ut", r_u, r_tt),):
                            ps = opened((nm, t, lv, q), l)
                            for i, h in enumerate(heads):
                                last = mm(ps[:, i * P:(i + 1) * P], a_[:, h, :], b_[:, h, :], start=True, stop=True)
                            last.then_inc(B.filled((nm, t, lv, q)), 1)
                    elif stage == 8 and not half:
                        need("tm_copied", l, 2 * t + q + 1)
                        need("ab_masked", l, 4 * (2 * t + q + 1))
                        if t:
                            need("state", l, 2 * t + q - 1)
                        for p in range(2):
                            ps = opened(("g", t, p, q), l)
                            lo, hi = 64 * p, 64 * p + 64
                            for i, c in enumerate(cs):
                                h = 2 * c + p
                                mm(ps[:, i * 64:i * 64 + 64], r_ar[lo:hi, c, t, 0, :], r_s[lo:hi, c, :], start=True, stop=False)
                                last = mm(ps[:, i * 64:i * 64 + 64], r_ak[:, h, 0:P], r_tm[:, 2, h * 64:h * 64 + 64], start=False, stop=True)
                            last.then_inc(B.filled(("g", t, p, q)), 1)
                    elif stage == 8:
                        need(f"t_updated{q}", l, 13 * (t + 1))
                        need("g_copied", l, 2 * t + q + 1)
                        ps = opened(("sa", t, q), l)
                        for i, h in enumerate(heads):
                            last = mm(ps[:, i * 64:i * 64 + 64], r_tt[:, h, :], r_g[:, h, :], start=True, stop=True)
                        last.then_inc(B.filled(("sa", t, q)), 1)
                    elif stage == 9 and not half:
                        need("sa_copied", l, 2 * t + q + 1)
                        for p in range(2):
                            ps = opened(("y", t, p, q), l)
                            lo, hi = 64 * p, 64 * p + 64
                            pe.sem_inc(passed, 1)
                            for i, c in enumerate(cs):
                                h = 2 * c + p
                                o = ps[lo:hi, i * P:(i + 1) * P]
                                mm(o, r_s[lo:hi, c, :], r_ar[lo:hi, c, t, 1, :], start=True, stop=False)
                                mm(o, r_sa[:, h, :], r_ab[:, h, P:2 * P], start=False, stop=False)
                                last = mm(o, r_tm[:, 2, h * 64:h * 64 + 64], r_ak[:, h, P:2 * P], start=False, stop=True)
                            last.then_inc(B.filled(("y", t, p, q)), 1)
                    elif stage == 9 and t < TT - 1:
                        ps = opened(("s", t, q), l)
                        for h in heads:
                            p, i = h % 2, h // 2 - 2 * q
                            o = ps[64 * p:64 * p + 64, i * 64:i * 64 + 64]
                            mm(o, r_tm[:, 0, h * 64:h * 64 + 64], r_sa[:, h, :], start=True, stop=False)
                            last = mm(o, r_tm[:, 1, h * 64:h * 64 + 64], r_tm[:, 2, h * 64:h * 64 + 64], start=False, stop=True)
                        last.then_inc(B.filled(("s", t, q)), 1)
                need("y_copied", l)
                for c in range(4):
                    summed(("mu", c), l, [(bones, r_y[:, c, :])])
                w = v3(arrive(("gla", 0), l)[:, 0:4096], 8)
                for c in range(2):
                    summed(("gq", c), l, [(w[:, k, c * P:(c + 1) * P], hT[:, k, :]) for k in range(KD)])
                for c in range(4):
                    need("y_sq", l, c + 1)
                    summed(("var", c), l, [(bones, r_t1[:, c, :])])
                for c in (2, 3):
                    summed(("gq", c), l, [(w[:, k, c * P:(c + 1) * P], hT[:, k, :]) for k in range(KD)])
                pe.drain().then_inc(used[block_at(("gla", 0))[1]], 1)
                for c in range(4):
                    summed(("g2", c), l, [(sw[:, SW_G2 + c * P:SW_G2 + (c + 1) * P], r_gl)])
                w = v3(arrive(("gla", 1), l)[:, 0:4096], 8)
                for t in range(TT):
                    ps = opened(("gv", t), l)
                    for k in range(KD):
                        last = mm(ps[:, :], hT[:, k, t * P:(t + 1) * P], w[:, k, :], start=(k == 0), stop=(k == KD - 1))
                    if t == TT - 1:
                        leave(last, ("gla", 1))
                        pe.drain().then_inc(B.filled(("gv", t)), 1)
                    else:
                        last.then_inc(B.filled(("gv", t)), 1)
                w = v3(arrive(("gla", 2), l)[:, 0:4224], 8)
                ps = opened(("ga", 0), l)
                for k in range(KD):
                    last = mm(ps[0:16, :], w[:, k, 0:16], hT[:, k, :], start=(k == 0), stop=(k == KD - 1))
                last.then_inc(B.filled(("ga", 0)), 1)
                need("gla_in", l, 9)
                for c in range(2):
                    ps = opened(("gz", c), l)
                    mm(ps[:, :], sw[0:16, SW_GA + c * P:SW_GA + (c + 1) * P], g_a[0:16, :], start=True, stop=True).then_inc(B.filled(("gz", c)), 1)
                block_of_jobs = [(("gr", c), 16 + c * P, P) for c in range(4)]
                for i, (job, j, m) in enumerate(block_of_jobs):
                    ps = opened(job, l)
                    for k in range(KD):
                        last = mm(ps[:, :], w[:, k, j:j + m], hT[:, k, :], start=(k == 0), stop=(k == KD - 1))
                    if i == 3:
                        leave(last, ("gla", 2))
                        pe.drain().then_inc(B.filled(job), 1)
                    else:
                        last.then_inc(B.filled(job), 1)
                w_d = v3(arrive(("dsa", 0), l)[:, 0:8 * 452], 8)

                def latent(c):
                    summed(("qc", c), l, [(w_d[:, k, c * P:(c + 1) * P], hT[:, k, :]) for k in range(KD)])

                latent(0)
                need("gla_kd", l)
                for c in range(2):
                    ps = opened(("kt", c), l)
                    for t in range(TT):
                        last = nc.tensor.transpose(ps[:, t * P:(t + 1) * P], g_k[:, c, t * P:(t + 1) * P], ident)
                    last.then_inc(B.filled(("kt", c)), 1)
                latent(1)
                need("kt_copied", l)
                need("gla_in", l, 13)
                for n in range(NCH):
                    lo, hi = 64 * (n % 2), 64 * (n % 2) + 64
                    ps = opened(("upd", n), l)
                    for c in range(2):
                        last = mm(ps[:, c * 256:(c + 1) * 256], g_tm[lo:hi, n // 2, c * P:(c + 1) * P],
                                  g_v[lo:hi, n // 2, c * 256:(c + 1) * 256], start=True, stop=True)
                    last.then_inc(B.filled(("upd", n)), 1)
                latent(2)
                ps = opened(("qc", 3), l)
                for p in range(2):
                    for k in range(KD):
                        last = mm(ps[64 * p:64 * p + 64, :], w_d[:, k, 384:448], hT[:, k, :], start=(k == 0), stop=(k == KD - 1))
                last.then_inc(B.filled(("qc", 3)), 1)
                ps = opened(("iw", 0), l)
                for t in range(TT):
                    for k in range(KD):
                        last = mm(ps[:, t * 4:t * 4 + 4], hT[:, k, t * P:(t + 1) * P], w_d[:, k, 448:452], start=(k == 0), stop=(k == KD - 1))
                leave(last, ("dsa", 0))
                pe.drain().then_inc(B.filled(("iw", 0)), 1)
                need("dsa_sq", l, 1)
                summed(("qn", 0), l, [(ones, d_sq[:, c, :]) for c in range(2)])
                need("dsa_sq", l, 2)
                summed(("kn", 0), l, [(ones, d_sq[:, 2, :])])
                need("gla_state", l)
                for h in range(4):
                    lo, hi = 64 * (h % 2), 64 * (h % 2) + 64
                    ps = opened(("o", h), l)
                    for n in range(NCH):
                        last = mm(ps[:, n * 64:n * 64 + 64], g_st[lo:hi, n, h // 2, :], g_q[lo:hi, h // 2, n * 64:n * 64 + 64],
                                  start=True, stop=True)
                    last.then_inc(B.filled(("o", h)), 1)
                up = arrive(("up", 0), l)
                w_q, w_i, w_v = v3(up[:, 0:2048], 2), v3(up[:, 2048:2560], 2), v3(sw[:, SW_UV:SW_N], 8)
                need("dsa_n", l, 1)
                for c in range(2):
                    summed(("iq", c), l, [(w_i[:, k, c * P:(c + 1) * P], d_qc[:, k, :]) for k in range(2)])
                for h in range(4):
                    need("o_sq", l, h + 1)
                    summed(("on", h), l, [(ones, g_o2[:, h, :])])
                join(pe, l, 2)

                need("iq_copied", l)
                need("dsa_in", l, 5)
                for b in range(1, 4):
                    for h in range(4):
                        lo, hi, w = 64 * (h % 2), 64 * (h % 2) + 64, P * (b + 1)
                        ps = opened(("ix", b, h), l)
                        mm(ps[:, 0:w], d_qi[lo:hi, h // 2, b * P:(b + 1) * P], d_ik[lo:hi, 0:w], start=True, stop=True)\
                            .then_inc(B.filled(("ix", b, h)), 1)
                for h in range(8):
                    ps = opened(("uq", h), l)
                    for k in range(2):
                        last = mm(ps[:, :], w_q[:, k, h * P:(h + 1) * P], d_qc[:, k, :], start=(k == 0), stop=(k == 1))
                    if h == 7:
                        leave(last, ("up", 0))
                        pe.drain().then_inc(B.filled(("uq", h)), 1)
                    else:
                        last.then_inc(B.filled(("uq", h)), 1)
                need("dsa_n", l, 2)
                ps = opened(("kvt", 0), l)
                for t in range(TT):
                    last = nc.tensor.transpose(ps[:, t * P:(t + 1) * P], d_kv[:, t * P:(t + 1) * P], ident)
                last.then_inc(B.filled(("kvt", 0)), 1)
                def gated(m, w, branches):
                    for i, (r, y) in enumerate(branches):
                        summed(("gt", m, r), l, [(w[:, i, k, :], hT[:, k, :]) for k in range(KD)])
                        ps = opened(("br", m, r), l)
                        for k in range(4):
                            last = mm(ps[:, :], w[:, i, 8 + k, :], y[:, k, :], start=(k == 0), stop=(k == 3))
                        if i == 0 and len(branches) == 2:
                            last.then_inc(B.filled(("br", m, r)), 1)
                    return last

                for m in range(KD):
                    w = arrive(("mac", m), l)[:, 0:24 * P].rearrange("p (r k n) -> p r k n", r=2, k=12)
                    leave(gated(m, w, ((0, ya), (2, yc))), ("mac", m))
                    pe.drain().then_inc(B.filled(("br", m, 2)), 1)
                need("uq_copied", l)
                need("kvt_copied", l)
                join(pe, l, 3)

                for i in range(QUADS + 3):
                    if 2 <= i < QUADS + 2:
                        n = i - 2
                        need("p_ready", l, n + 1)
                        for j in range(4):
                            ps = opened(("pt", n, j), l)
                            for s_ in range(n // 2 + 1):
                                last = nc.tensor.transpose(ps[:, s_ * P:(s_ + 1) * P], d_p[n % 2][j][:, s_ * P:(s_ + 1) * P], ident)
                            last.then_inc(B.filled(("pt", n, j)), 1)
                    if i < QUADS:
                        b = i // 2
                        for j in range(4):
                            ps = opened(("lg", i, j), l)
                            mm(ps[:, 0:P * (b + 1)], d_q[:, 4 * (i % 2) + j, b * P:(b + 1) * P], d_kv[:, 0:P * (b + 1)], start=True, stop=True)\
                                .then_inc(B.filled(("lg", i, j)), 1)
                    if i >= 3:
                        n = i - 3
                        ps = opened(("cx", n), l)
                        need("pt_copied", l, n + 1)
                        for j in range(4):
                            for s_ in range(n // 2 + 1):
                                last = mm(ps[:, j * P:(j + 1) * P], d_kt[:, s_, :], d_pt[n % 2][j][:, s_ * P:(s_ + 1) * P],
                                          start=(s_ == 0), stop=(s_ == n // 2))
                        last.then_inc(B.filled(("cx", n)), 1)
                need("cx_copied", l)
                for c in range(4):
                    ps = opened(("uv", c), l)
                    for p in range(2):
                        last = mm(ps[64 * p:64 * p + 64, :], w_v[:, 2 * c + p, :], d_cx[:, 2 * c + p, :], start=True, stop=True)
                    last.then_inc(B.filled(("uv", c)), 1)
                join(pe, l, 4)

                for i in range(4):
                    w = arrive(("mb", i), l)[:, 0:24 * P].rearrange("p (m k n) -> p m k n", m=2, k=12)
                    last = gated(2 * i, w[:, 0:1], ((1, yb),))
                    last.then_inc(B.filled(("br", 2 * i, 1)), 1)
                    leave(gated(2 * i + 1, w[:, 1:2], ((1, yb),)), ("mb", i))
                    pe.drain().then_inc(B.filled(("br", 2 * i + 1, 1)), 1)
                need("merged", l)

                for i in range(2):
                    w = v3(arrive(("out", i), l)[:, 0:4096], 8)
                    for j in range(4):
                        m = 4 * i + j
                        ps = opened(("wo", m), l)
                        for k in range(KD):
                            last = mm(ps[:, :], w[:, k, j * P:(j + 1) * P], m_o[:, k, :], start=(k == 0), stop=(k == KD - 1))
                        if j == 3:
                            leave(last, ("out", i))
                            pe.drain().then_inc(B.filled(("wo", m)), 1)
                        else:
                            last.then_inc(B.filled(("wo", m)), 1)
                join(pe, l, 5)
                norm(l, 1)
                need("h_ready", l, 2 * KD)
                join(pe, l, 6)
                def score(lap, banks, turn, q):
                    pe.wait_ge(*E_["tile_in"].at(lap, q + 1))
                    for p in range(2):
                        ps = opened(("sc", p, q), turn, banks)
                        for i in range(4):
                            h = 4 * q + i
                            last = mm(ps[:, i * P:(i + 1) * P], e_qc[64 * p:64 * p + 64, h, :],
                                      sw[64 * p:64 * p + 64, SW_KEY + h * P:SW_KEY + (h + 1) * P], start=True, stop=True)
                        last.then_inc(banks.filled(("sc", p, q)), 1)

                w = [v3(arrive(("pq", i), l)[:, 0:4096], 8) for i in range(2)]

                def queries(h):
                    ps = opened(("pq", h), l)
                    for k in range(KD):
                        last = mm(ps[:, P:S], w[h // 4][:, k, (h % 4) * P:(h % 4 + 1) * P], hT[:, k, P:S], start=(k == 0), stop=(k == KD - 1))
                    if h % 4 == 3:
                        leave(last, ("pq", h // 4))
                        pe.drain().then_inc(B.filled(("pq", h)), 1)
                    else:
                        last.then_inc(B.filled(("pq", h)), 1)

                for i in range(2):
                    ps = opened(("pq0", i), l)
                    for j in range(4):
                        for k in range(KD):
                            last = mm(ps[:, j * P:(j + 1) * P], w[i][:, k, j * P:(j + 1) * P], hT[:, k, 0:P], start=(k == 0), stop=(k == KD - 1))
                    last.then_inc(B.filled(("pq0", i)), 1)
                    queries(i)
                    score(l * TT, B, l, i)
                for h in range(2, EH):
                    queries(h)
                for t in range(TT):
                    for hf in range(2):
                        ps = opened(("h2", t, hf), l)
                        for i in range(4):
                            last = nc.tensor.transpose(ps[:, i * P:(i + 1) * P], hT[:, 4 * hf + i, t * P:(t + 1) * P], ident)
                        last.then_inc(B.filled(("h2", t, hf)), 1)
                join(pe, l, 7)

                def expert_tile(lap, more, t=None):
                    acc = [opened(("acc", j), lap, T) for j in range(2)]
                    pe.wait_ge(*E_["rows_in"].at(lap))
                    for j in range(2):
                        mm(acc[j][:, :], zeros[:], e_hc[:, 0:NB], start=True, stop=False)

                    def groups(g0, g1):
                        with pe.Fori(g0, g1) as g:
                            for s_ in range(GRP):
                                pe.wait_ge(diags[s_], lap * NGRP + g + 1)
                                for j in range(2):
                                    last = mm(acc[j][:, :], e_diag[:, s_, :], e_row[s_][:, D + j * NB:D + (j + 1) * NB], start=False, stop=False)
                                last.then_inc(rows_used[s_], 1)
                    groups(0, 1)
                    if more:
                        for q in range(2):
                            score(lap + 1, T, l * (TT - 1) + t, q)
                    groups(1, NGRP)
                    for j in range(2):
                        mm(acc[j][:, :], zeros[:], e_hc[:, 0:NB], start=False, stop=True).then_inc(T.filled(("acc", j)), 1)
                    pe.wait_ge(*E_["acc_copied"].at(lap))
                    for j in range(2):
                        ps = opened(("xt", j), lap, T)
                        for i in range(4):
                            last = nc.tensor.transpose(ps[:, i * P:(i + 1) * P], e_acc[:, j * NB + i * P:j * NB + (i + 1) * P], ident)
                        last.then_inc(T.filled(("xt", j)), 1)

                with pe.Fori(0, TT - 1) as t:
                    expert_tile(l * TT + t, True, t)
                expert_tile(l * TT + TT - 1, False)
                join(pe, l, 8)
            pe.wait_ge(G["squares"].sem, depth * 2 + 1)
            pe.wait_ge(T.freed_sems[0], 2)
            for k in range(KD):
                last = mm(psum[0][:, :], ones, hT[:, k, :], start=(k == 0), stop=(k == KD - 1))
            last.then_inc(stored_mm, 1)

        @block.scalar
        def _(act):
            A = nc.scalar.activation

            def need(sig, l, k=None):
                act.wait_ge(*G[sig].at(l, k))

            def full(name, l, banks=B):
                act.wait_ge(*banks.full(name, l))
                return psum[banks.bank(name)]

            def inv_roots(jobs, scale, eps, done):
                for out_, name in jobs:
                    ps = full(name, l)
                    A(out_, ps[:, :], ACT.Ln, bias=eps, scale=scale).then_inc(B.freed(name), 1)
                act.drain()
                for out_, name in jobs:
                    A(out_, out_, ACT.Exp, scale=-0.5).then_inc(done, 1)

            act.wait_ge(loaded, 64)
            act.wait_ge(const_set, 1)
            A(cond[:], fix[:, 0:KD], ACT.Silu)
            act.drain()
            with act.Fori(0, depth) as l:
                act.nop().then_inc(G["cond_ready"].sem, 1)

                def norm(w):
                    for k in range(KD):
                        last = A(hT[:, k, :], xT[:, k, :], ACT.Square)
                    last.then_inc(G["squares"].sem, 1)
                    inv_roots([(rstd[:], ("ss", w))], 1.0 / D, sc[:, 0:1], rstd_ready)
                    for k in range(KD):
                        act.wait_ge(scaled, (l * 2 + w) * KD + k + 1)
                        A(hT[:, k, :], hT[:, k, :], ACT.Identity, bias=modc[:, 24 * w + k:24 * w + k + 1]).then_inc(G["h_ready"].sem, 1)

                norm(0)
                def raw(i, c):
                    ps = full(("rp", c), l)
                    if i >= 2:
                        need("pt_used", l, i - 1)
                    A(r_pt[i % 2][:, 1:513], ps[:, :], ACT.Copy).then_inc(B.freed(("rp", c)), 1)
                    act.drain().then_inc(G["pt_ready"].sem, 1)

                order = (12, 13, 4, 5, 6, 7, 0, 1, 2, 3, 8, 9, 10, 11)
                for i in range(2):
                    raw(i, order[i])
                need("mixed", l, 1)
                A(r_lr[0:64, :], r_lr[0:64, :], ACT.Tanh).then_inc(G["lr_ready"].sem, 1)
                need("mixed", l, 2)
                A(r_gl, r_gl, ACT.Sigmoid).then_inc(G["lr_ready"].sem, 1)
                for nm, dst, b in (("z", r_sg, "rwkv_w0"), ("za", r_a, "rwkv_a0")):
                    for c in range(4):
                        ps = full((nm, c), l)
                        last = A(dst[:, c, :], ps[:, :], ACT.Sigmoid, bias=cl(b, c)).then_inc(B.freed((nm, c)), 1)
                    act.drain().then_inc(G["sig_ready"].sem, 1)
                for i in range(2, 14):
                    raw(i, order[i])
                need("kk_raw", l)
                A(r_t1, r_kk, ACT.Square).then_inc(G["kk_sq"].sem, 1)
                inv_roots([(r_t1[:, c, :], ("kkn", c)) for c in range(4)], 1.0, sc[:, 2:3], G["kk_rs"].sem)
                need("cs_done", l)
                A(r_sg, r_sg, ACT.Exp, scale=-KAPPA).then_inc(G["eprev"].sem, 1)
                A(r_f, r_f, ACT.Exp, scale=-KAPPA).then_inc(G["f_ready"].sem, 1)
                need("ar_half", l)
                A(r_sg, r_cs, ACT.Exp, scale=-KAPPA)
                act.drain().then_inc(G["ep"].sem, 1)
                A(r_cs, r_cs, ACT.Exp, scale=KAPPA).then_inc(G["em"].sem, 1)
                for half, t, q, stage in rwkv_steps():
                    hs = slice(4 * q, 4 * q + 4)
                    if stage == 0 and half:
                        if t:
                            need("state", l, 2 * t + q - 1)
                        for w, rows in enumerate((slice(0, 2), slice(2, 3))):
                            ps = full(("tm", t, q, w), l)
                            n = 2 - w
                            A(r_tm[:, rows, q * 256:(q + 1) * 256], v3(ps[:, 0:n * 256], n), ACT.Copy).then_inc(B.freed(("tm", t, q, w)), 1)
                        act.drain().then_inc(G["tm_copied"].sem, 1)
                    elif 1 < stage < 8 and not half:
                        lv = stage - 1
                        ps = full(("u", t, lv, q), l)
                        if lv > 1:
                            full(("ut", t, lv - 1, q), l)
                        A(r_u[:, hs, :], ps[:, :], ACT.Copy).then_inc(B.freed(("u", t, lv, q)), 1)
                        act.drain().then_inc(G[f"u_copied{q}"].sem, 1)
                    elif stage == 8 and not half:
                        for p in range(2):
                            ps = full(("g", t, p, q), l)
                            A(r_g[:, 4 * q + p:4 * q + 4:2, :], v3(ps[:, 0:P], 2), ACT.Copy).then_inc(B.freed(("g", t, p, q)), 1)
                        act.drain().then_inc(G["g_copied"].sem, 1)
                    elif stage == 8:
                        ps = full(("sa", t, q), l)
                        A(r_sa[:, hs, :], ps[:, 0:256], ACT.Copy).then_inc(B.freed(("sa", t, q)), 1)
                        act.drain().then_inc(G["sa_copied"].sem, 1)
                    elif stage == 9 and not half:
                        for p in range(2):
                            lo, hi = 64 * p, 64 * p + 64
                            ps = full(("y", t, p, q), l)
                            A(r_y[lo:hi, 2 * q:2 * q + 2, t * P:(t + 1) * P], v3(ps[lo:hi, 0:256], 2), ACT.Copy).then_inc(B.freed(("y", t, p, q)), 1)
                        act.drain().then_inc(G["y_copied"].sem, 1)
                for c in range(4):
                    need("y_cent", l, c + 1)
                    A(r_t1[:, c, :], r_y[:, c, :], ACT.Square).then_inc(G["y_sq"].sem, 1)
                n_in = G["gla_in"].sem

                def copied(name, dst, func=ACT.Copy, scale=1.0, ps_of=lambda ps: ps[:, :]):
                    ps = full(name, l)
                    A(dst, ps_of(ps), func, scale=scale).then_inc(B.freed(name), 1)
                    return act.drain()

                for c in range(2):
                    copied(("gq", c), g_q[:, c, :], scale=0.125).then_inc(n_in, 1)
                inv_roots([(r_t1[:, c, :], ("var", c)) for c in range(4)], 1.0 / 64, sc[:, 1:2], G["y_rs"].sem)
                for c in range(2):
                    copied(("gq", c + 2), g_k[:, c, :]).then_inc(n_in, 1)
                for t in range(TT):
                    copied(("gv", t), g_v[:, t, :]).then_inc(n_in, 1)
                copied(("ga", 0), g_a[0:16, :], ps_of=lambda ps: ps[0:16, :]).then_inc(n_in, 1)
                for c in range(2):
                    ps = full(("gz", c), l)
                    A(g_ab[:, c, :], ps[:, :], ACT.Abs, bias=cl("gla_b_a", c)).then_inc(G["gz_abs"].sem, 1)
                act.drain()
                for c in range(2):
                    A(g_ab[:, c, :], g_ab[:, c, :], ACT.Exp, scale=-1.0)
                act.drain()
                for c in range(2):
                    A(g_ab[:, c, :], g_ab[:, c, :], ACT.Ln, bias=sc[:, 3:4]).then_inc(G["gz_exp"].sem, 1)
                for c in range(4):
                    copied(("gr", c), g_r[:, c, :], ACT.Silu).then_inc(n_in, 1)
                need("gla_la", l)
                A(g_la, g_la, ACT.Exp, scale=1.0 / 16).then_inc(G["gla_dec"].sem, 1)
                A(g_dec, g_tot, ACT.Exp, scale=1.0 / 16).then_inc(G["gla_dec"].sem, 1)
                d_in = G["dsa_in"].sem

                def latent(c):
                    copied(("qc", c), d_qc[:, c, :]).then_inc(d_in, 1)
                    return A(d_sq[:, c, :], d_qc[:, c, :], ACT.Square)

                latent(0)
                for c in range(2):
                    ps = full(("kt", c), l)
                    A(g_tm[:, :, c * P:(c + 1) * P], v3(ps[:, :], 4), ACT.Copy).then_inc(B.freed(("kt", c)), 1)
                    act.drain().then_inc(G["kt_copied"].sem, 1)
                latent(1).then_inc(G["dsa_sq"].sem, 1)
                copied(("qc", 2), d_kv).then_inc(d_in, 1)
                A(d_sq[:, 2, :], d_kv, ACT.Square).then_inc(G["dsa_sq"].sem, 1)
                copied(("qc", 3), d_ik).then_inc(d_in, 1)
                copied(("iw", 0), d_iw.rearrange("p c t -> p (c t)"), ps_of=lambda ps: ps[:, 0:16]).then_inc(d_in, 1)
                inv_roots([(d_sq[:, 0, :], ("qn", 0))], 1.0 / 256, sc[:, 0:1], G["dsa_rs"].sem)
                inv_roots([(d_sq[:, 2, :], ("kn", 0))], 1.0 / 128, sc[:, 0:1], G["dsa_rs"].sem)
                for h in range(4):
                    ps = full(("o", h), l)
                    A(g_o2[:, h, :], ps[:, :], ACT.Square).then_inc(G["o_sq"].sem, 1)
                    A(g_o[:, h, :], ps[:, :], ACT.Copy).then_inc(B.freed(("o", h)), 1)
                for c in range(2):
                    copied(("iq", c), d_qi[:, c, :]).then_inc(G["iq_copied"].sem, 1)
                inv_roots([(g_o2[:, h, :], ("on", h)) for h in range(4)], 1.0 / 128, sc[:, 0:1], G["o_rs"].sem)
                join(act, l, 2)

                for i in range(12):
                    b, h = 1 + i // 4, i % 4
                    w = P * (b + 1)
                    ps = full(("ix", b, h), l)
                    if i >= 4:
                        need("relu_used", l, i - 3)
                    A(d_rl[h][:, 0:w], ps[:, 0:w], ACT.Relu).then_inc(B.freed(("ix", b, h)), 1)
                    act.drain().then_inc(G["relu"].sem, 1)
                for h in range(8):
                    copied(("uq", h), d_q[:, h, :]).then_inc(G["uq_copied"].sem, 1)
                copied(("kvt", 0), d_kt.rearrange("p c t -> p (c t)")).then_inc(G["kvt_copied"].sem, 1)

                def gates(i0, order):
                    for i, (m, r) in enumerate(order, i0):
                        ps = full(("gt", m, r), l)
                        if i >= 2:
                            need("gate_used", l, i - 1)
                        A(m_g[i % 2], ps[:, :], ACT.Sigmoid).then_inc(B.freed(("gt", m, r)), 1)
                        act.drain().then_inc(G["gate"].sem, 1)

                gates(0, [(m, r) for m in range(KD) for r in (0, 2)])
                join(act, l, 3)
                for i in range(QUADS + 3):
                    if i < QUADS:
                        w = P * (i // 2 + 1)
                        need("lg_max", l, i + 1)
                        for j in range(4):
                            A(d_p[i % 2][j][:, 0:w], d_p[i % 2][j][:, 0:w], ACT.Exp, bias=d_n[:, 4 * i + j:4 * i + j + 1], scale=P ** -0.5,
                              accum_out=d_sm[:, 4 * i + j:4 * i + j + 1])
                        act.drain().then_inc(G["lg_exp"].sem, 1)
                    if 2 <= i < QUADS + 2:
                        n = i - 2
                        w = P * (n // 2 + 1)
                        if n >= 2:
                            act.wait_ge(*B.full(("cx", n - 2), l))
                        for j in range(4):
                            ps = full(("pt", n, j), l)
                            A(d_pt[n % 2][j][:, 0:w], ps[:, 0:w], ACT.Copy).then_inc(B.freed(("pt", n, j)), 1)
                        act.drain().then_inc(G["pt_copied"].sem, 1)
                    if i >= 3:
                        n = i - 3
                        ps = full(("cx", n), l)
                        A(d_cx[:, 4 * (n % 2):4 * (n % 2) + 4, (n // 2) * P:(n // 2 + 1) * P], v3(ps[:, :], 4), ACT.Copy)\
                            .then_inc(B.freed(("cx", n)), 1)
                        act.drain().then_inc(G["cx_copied"].sem, 1)
                for c in range(4):
                    ps = full(("uv", c), l)
                    A(yb[:, c, :], ps[:, :], ACT.Copy).then_inc(B.freed(("uv", c)), 1)
                join(act, l, 4)
                gates(2 * KD, [(m, 1) for m in range(KD)])
                need("x_mixed", l)
                join(act, l, 5)
                norm(1)
                join(act, l, 6)
                def scores(banks, turn, q):
                    for p in range(2):
                        ps = full(("sc", p, q), turn, banks)
                        A(e_s[:, 8 * q + p:8 * q + 8:2, :], v3(ps[:, :], 4), ACT.Copy).then_inc(banks.freed(("sc", p, q)), 1)
                        act.drain().then_inc(E_["scored"].sem, 1)

                def soft(lap):
                    act.wait_ge(*E_["soft_in"].at(lap))
                    A(e_ex, e_ex, ACT.Exp).then_inc(E_["soft"].sem, 1)

                def queries(h):
                    ps = full(("pq", h), l)
                    A(e_q[:, h, P:S], ps[:, P:S], ACT.Copy).then_inc(B.freed(("pq", h)), 1)

                for i in range(2):
                    ps = full(("pq0", i), l)
                    A(e_qc[:, 4 * i:4 * i + 4, :], v3(ps[:, :], 4), ACT.Copy).then_inc(B.freed(("pq0", i)), 1)
                    act.drain().then_inc(E_["tile_in"].sem, 1)
                    queries(i)
                    scores(B, l, i)
                for h in range(2, EH):
                    queries(h)
                for t in range(TT):
                    for hf in range(2):
                        copied(("h2", t, hf), e_h[:, t, hf * NB:(hf + 1) * NB]).then_inc(G["h2_copied"].sem, 1)
                soft(l * TT)
                join(act, l, 7)

                def expert_tile(lap, t, more):
                    A(e_hc, e_h[:, t, :] if isinstance(t, int) else e_h.rearrange("p t d -> p (t d)")[:, bass.ds(t * D, D)], ACT.Copy)
                    act.drain().then_inc(E_["rows_in"].sem, 1)
                    act.wait_ge(*E_["routed"].at(lap))

                    def groups(g0, g1):
                        with act.Fori(g0, g1) as g:
                            turn = lap * NGRP + g
                            A(e_gc, e_gate[:, bass.ds(t * SLOTS + g * GRP, GRP)], ACT.Copy)
                            for s_ in range(GRP):
                                act.wait_ge(dots[s_], turn + 1)
                                A(e_ge[:, s_:s_ + 1], e_dot[:, s_:s_ + 1], ACT.Gelu)
                                act.drain()
                                A(e_wg[:, s_:s_ + 1], e_gc[:, s_:s_ + 1], ACT.Copy, scale=e_ge[:, s_:s_ + 1])
                                act.drain()
                                act.wait_ge(rows_used[s_], turn + 1)
                                A(e_diag[:, s_, :], ident, ACT.Copy, scale=e_wg[:, s_:s_ + 1]).then_inc(diags[s_], 1)
                    groups(0, 1)
                    if more:
                        A(e_qc, e_q[:, :, bass.ds((t + 1) * P, P)], ACT.Copy)
                        act.drain().then_inc(E_["tile_in"].sem, 2)
                        for q in range(2):
                            scores(T, l * (TT - 1) + t, q)
                        groups(1, PIECES[5] + 1)
                        soft(lap + 1)
                        groups(PIECES[5] + 1, NGRP)
                    else:
                        groups(1, NGRP)
                    for j in range(2):
                        ps = full(("acc", j), lap, T)
                        A(e_acc[:, j * NB:(j + 1) * NB], ps[:, :], ACT.Copy).then_inc(T.freed(("acc", j)), 1)
                    act.drain().then_inc(E_["acc_copied"].sem, 1)

                with act.Fori(0, TT - 1) as t:
                    expert_tile(l * TT + t, t, True)
                expert_tile(l * TT + TT - 1, TT - 1, False)
                join(act, l, 8)
            for k in range(KD):
                last = A(hT[:, k, :], xT[:, k, :], ACT.Square)
            last.then_inc(G["squares"].sem, 1)
            act.wait_ge(stored_mm, 1)
            A(rstd[:], psum[0][:, :], ACT.Ln, bias=sc[:, 0:1], scale=1.0 / D)
            act.drain()
            A(rstd[:], rstd[:], ACT.Exp, scale=-0.5).then_inc(rstd_ready, 1)

        @block.vector
        def _(dve):
            V = nc.vector

            def need(sig, l, k=None):
                dve.wait_ge(*G[sig].at(l, k))

            def full(name, l, banks=B):
                dve.wait_ge(*banks.full(name, l))
                return psum[banks.bank(name)]

            for i, e in enumerate((EPS, LN_EPS, KK_EPS, 1.0)):
                V.memset(sc[:, i:i + 1], e)
            V.memset(zeros[:], 0.0)
            V.memset(e_off[:], 0.0)
            dve.drain().then_inc(const_set, 1)
            dve.wait_ge(loaded, 64)
            with dve.Fori(0, depth) as l:
                V.tensor_copy(col[:], allcols[:, bass.ds(l * NCOL, NCOL)])
                V.memset(r_pt[0][:, 0:1], 0.0)
                V.memset(r_pt[1][:, 0:1], 0.0)
                dve.drain()
                need("cond_ready", l)
                def lane_sums(out_, w):
                    V.tensor_scalar(out_, w[:, 0, :], cond[:, 0:1], None, ALU.mult)
                    for k in range(1, KD):
                        dve.drain()
                        V.scalar_tensor_tensor(out=out_, in0=w[:, k, :], scalar=cond[:, k:k + 1], in1=out_, op0=ALU.mult, op1=ALU.add)

                for i in range(ADA_RING):
                    dst, slot, _ = block_at(("ada", i))
                    dve.wait_ge(landed[slot], 16 * (l * LAND_N[slot] + LANDED[("ada", i)]))
                    dve.sem_inc(passed, 1)
                    lane_sums(a_at[i], v3(dst[:, 0:4096], 8))
                    dve.drain().then_inc(used[slot], 1)
                    dve.sem_inc(G["ada_summed"].sem, 1)

                def half_block(n):
                    dve.wait_ge(ada_landed[n % 2], 16 * (l * (ADA_HALVES // 2) + n // 2 + 1))
                    dve.sem_inc(passed, 1)
                    lane_sums(a_at[ADA_RING + n // 2][:, n % 2 * 256:(n % 2 + 1) * 256], a_half[n % 2])
                    dve.drain().then_inc(ada_used[n % 2], 1)

                half_block(0)
                half_block(1)
                dve.sem_inc(G["ada_summed"].sem, 1)

                def modulation(part):
                    ps = full(("mod", part), l)
                    m = slice(16 * part, 16 * part + 16)
                    V.tensor_tensor(modc[:, m], ps[:, m], cl("b_ada", 16 * part, 16), ALU.add).then_inc(B.freed(("mod", part)), 1)

                modulation(0)
                dve.drain()

                def gains(w, g):
                    V.scalar_tensor_tensor(out=gain[:, KD * w:KD * w + KD], in0=modc[:, 24 * w + 8:24 * w + 16], scalar=1.0,
                                           in1=cl(g, 0, KD), op0=ALU.add, op1=ALU.mult)
                gains(0, "g_norm_mix")
                V.tensor_scalar(omka[:], cl("rwkv_k_a", 0, 4), -1.0, 1.0, ALU.mult, ALU.add)
                dve.drain()

                def norm(w):
                    dve.wait_ge(rstd_ready, l * 2 + w + 1)
                    for k in range(KD):
                        V.scalar_tensor_tensor(out=hT[:, k, :], in0=xT[:, k, :], scalar=gain[:, KD * w + k:KD * w + k + 1],
                                               in1=rstd[:], op0=ALU.mult, op1=ALU.mult).then_inc(scaled, 1)

                norm(0)
                half_block(ADA_LENT[0])
                dve.sem_inc(G["ada_summed"].sem, 1)
                dst_of = {12: r_lr, 13: r_gl, **{c: r_r[:, c, :] for c in range(4)},
                          **{4 + c: r_k[:, c, :] for c in range(4)}, **{8 + c: r_v[:, c, :] for c in range(4)}}
                for i, c in enumerate((12, 13, 4, 5, 6, 7, 0, 1, 2, 3, 8, 9, 10, 11)):
                    need("pt_ready", l, i + 1)
                    pt, d = r_pt[i % 2], dst_of[c]
                    V.tensor_tensor(d, pt[:, 0:512], pt[:, 1:513], ALU.subtract)
                    dve.drain()
                    V.scalar_tensor_tensor(out=d, in0=d, scalar=cl("rwkv_mu", c), in1=pt[:, 1:513], op0=ALU.mult, op1=ALU.add)\
                        .then_inc(G["mixed"].sem, 1)
                    dve.drain().then_inc(G["pt_used"].sem, 1)
                    if i == 9:
                        modulation(1)
                    if i == 5:
                        need("sig_ready", l, 2)
                        for c_ in range(4):
                            V.tensor_tensor_scan(r_cs[:, c_, :], m128, r_sg[:, c_, :], 0.0, ALU.mult, ALU.add)
                        for c_ in range(4):
                            V.tensor_scalar(r_kk[:, c_, :], r_k[:, c_, :], cl("rwkv_k_k", c_), None, ALU.mult)
                        dve.drain().then_inc(G["kk_raw"].sem, 1)
                        cs16 = r_cs.rearrange("p c (t s) -> p (c t) s", t=4)
                        V.tensor_copy(r_mid, cs16[:, :, 63])
                        dve.drain()
                        V.tensor_tensor(cs16, cs16, bc(r_mid.unsqueeze(2), [P, 16, P]), ALU.subtract)
                        dve.drain()
                        V.tensor_tensor(r_sg, r_cs, r_sg, ALU.subtract)
                        V.tensor_tensor(v3(r_f, 4), r_cs.rearrange("p c (t s) -> p c t s", t=4)[:, :, 0:3, 127],
                                        v3(r_mid, 4)[:, :, 1:4], ALU.add)
                        dve.drain().then_inc(G["cs_done"].sem, 1)
                        for c_ in range(4):
                            V.tensor_scalar(r_t2[:, c_, :], r_a[:, c_, :], cl("rwkv_k_a", c_), omka[:, c_:c_ + 1], ALU.mult, ALU.add)
                        dve.drain()
                        V.tensor_tensor(r_k, r_k, r_t2, ALU.mult)
                        dve.drain()
                for c in range(4):
                    V.scalar_tensor_tensor(out=r_t2[:, c, :], in0=r_r[:, c, :], scalar=cl("rwkv_r_k", c), in1=r_k[:, c, :],
                                           op0=ALU.mult, op1=ALU.mult)
                dve.drain().then_inc(G["bon_in"].sem, 1)
                full(("mod", 1), l)
                half_block(ADA_LENT[1])
                dve.sem_inc(G["ada_summed"].sem, 1)
                for c in range(4):
                    need("kk_rs", l, c + 1)
                    V.tensor_tensor(r_kk[:, c, :], r_kk[:, c, :], r_t1[:, c, :], ALU.mult)
                need("ada_half_summed", l, ADA_HALVES - 5)
                for c in range(4):
                    ps = full(("bon", c), l)
                    V.tensor_tensor(r_bon[:, c, :], ps[:, :], r_v[:, c, :], ALU.mult).then_inc(B.freed(("bon", c)), 1)
                need("eprev", l)
                dve.sem_inc(passed, 1)
                dve.drain()
                half = [r_ar[:, :, :, w, :].rearrange("p c t s -> p (c t) s") for w in range(2)]

                def by_tile(x):
                    return x.rearrange("p c (t s) -> p (c t) s", t=4)
                V.scalar_tensor_tensor(out=half[0], in0=by_tile(r_kk), scalar=-1.0, in1=by_tile(r_sg), op0=ALU.mult, op1=ALU.mult)
                V.tensor_tensor(r_kk, r_kk, r_a, ALU.mult)
                dve.drain().then_inc(G["ar_half"].sem, 1)
                need("ep", l)
                V.tensor_tensor(half[1], by_tile(r_r), by_tile(r_sg), ALU.mult)
                need("em", l)
                V.tensor_tensor(r_kk, r_kk, r_cs, ALU.mult)
                V.tensor_tensor(r_k, r_k, r_cs, ALU.mult)
                dve.drain().then_inc(G["rk_ready"].sem, 1)
                V.memset(r_s, 0.0).then_inc(G["s_zero"].sem, 1)
                need("f_ready", l)
                for half, t, q, stage in rwkv_steps():
                    hs = slice(4 * q, 4 * q + 4)
                    if stage == 0 and not half:
                        if t + q == 0:
                            modulation(2)
                        if t:
                            need("y_copied", l, 2 * t + q - 1)
                            need(f"level_masked{q}", l, 7 * t)
                        for nm, dst in (("ab", r_ab), ("kb", r_ak)):
                            for p in range(2):
                                ps = full((nm, t, p, q), l)
                                V.tensor_tensor(dst[:, 4 * q + p:4 * q + 4:2, :], v3(ps[:, :], 2), bc(tri.unsqueeze(1), [P, 2, 2 * P]), ALU.mult)\
                                    .then_inc(B.freed((nm, t, p, q)), 1)
                                dve.drain().then_inc(G["ab_masked"].sem, 1)
                    elif stage == 1 and not half:
                        if t:
                            need("sa_copied", l, 2 * t + q - 1)
                        need(f"level_masked{q}", l, 7 * t + 1)
                        ps = full(("m0", t, q), l)
                        V.tensor_tensor(r_tn[:, hs, :], v3(ps[:, :], 4), bc(ident.unsqueeze(1), [P, 4, P]), ALU.add)\
                            .then_inc(B.freed(("m0", t, q)), 1)
                        dve.drain().then_inc(G[f"t_updated{q}"].sem, 1)
                        V.tensor_tensor(r_tt[:, hs, :], r_m[0][:, hs, :], bc(ident.unsqueeze(1), [P, 4, P]), ALU.add)
                        dve.drain().then_inc(G[f"t_updated{q}"].sem, 1)
                    elif 1 < stage < 8 and half:
                        lv = stage - 1
                        if lv < 6:
                            ps = full(("tu", t, lv, q), l)
                            V.tensor_tensor(r_tn[:, hs, :], v3(ps[:, :], 4), r_tn[:, hs, :], ALU.add).then_inc(B.freed(("tu", t, lv, q)), 1)
                            dve.drain().then_inc(G[f"t_updated{q}"].sem, 1)
                        ps = full(("ut", t, lv, q), l)
                        V.tensor_tensor(r_tt[:, hs, :], v3(ps[:, :], 4), r_tt[:, hs, :], ALU.add).then_inc(B.freed(("ut", t, lv, q)), 1)
                        dve.drain().then_inc(G[f"t_updated{q}"].sem, 1)
                    elif stage == 9 and half and t < TT - 1:
                        ps = full(("s", t, q), l)
                        st = r_s[:, 2 * q:2 * q + 2, :]
                        V.tensor_tensor(st, v3(ps[:, 0:P], 2), st, ALU.add).then_inc(B.freed(("s", t, q)), 1)
                        dve.drain()
                        V.tensor_tensor(st, st, bc(v3(r_f, 4)[:, 2 * q:2 * q + 2, t:t + 1], [P, 2, 64]), ALU.mult)
                        dve.drain().then_inc(G["state"].sem, 1)
                dve.drain()
                gains(1, "g_norm_ffn")
                need("y_copied", l)
                for c in range(4):
                    ps = full(("mu", c), l)
                    V.scalar_tensor_tensor(out=r_y[:, c, :], in0=ps[:, :], scalar=-1.0 / 64, in1=r_y[:, c, :], op0=ALU.mult, op1=ALU.add)\
                        .then_inc(B.freed(("mu", c)), 1)
                    dve.drain().then_inc(G["y_cent"].sem, 1)
                for c in range(4):
                    need("y_rs", l, c + 1)
                    V.tensor_tensor(r_y[:, c, :], r_y[:, c, :], r_t1[:, c, :], ALU.mult)
                    dve.drain()
                    V.tensor_scalar(r_y[:, c, :], r_y[:, c, :], cl("rwkv_ln_g", c), cl("rwkv_ln_b", c), ALU.mult, ALU.add)
                    dve.drain()
                    V.tensor_tensor(r_y[:, c, :], r_y[:, c, :], r_bon[:, c, :], ALU.add)
                    dve.drain()
                    ps = full(("g2", c), l)
                    V.tensor_tensor(yc[:, c, :], ps[:, :], r_y[:, c, :], ALU.mult).then_inc(B.freed(("g2", c)), 1)
                for c in range(2):
                    need("gz_abs", l, c + 1)
                    ps = full(("gz", c), l)
                    V.tensor_scalar(g_la[:, c, :], ps[:, :], cl("gla_b_a", c), 0.0, ALU.add, ALU.min).then_inc(B.freed(("gz", c)), 1)
                need("gz_exp", l)
                dve.sem_inc(passed, 1)
                dve.drain()
                V.tensor_tensor(g_la, g_la, g_ab, ALU.subtract)
                dve.drain()
                for c in range(2):
                    V.tensor_tensor_scan(g_cum[:, c, :], m64, g_la[:, c, :], 0.0, ALU.mult, ALU.add)
                dve.drain()
                cum = g_cum.rearrange("p c (n s) -> p (c n) s", n=NCH)
                V.tensor_copy(g_tot.rearrange("p c n -> p (c n)"), cum[:, :, 63])
                dve.drain()
                V.tensor_tensor(g_la.rearrange("p c (n s) -> p (c n) s", n=NCH), bc(g_tot.rearrange("p c n -> p (c n)").unsqueeze(2), [P, 16, 64]),
                                cum, ALU.subtract)
                dve.drain().then_inc(G["gla_la"].sem, 1)
                need("gla_dec", l)
                need("gla_in", l, 4)
                V.tensor_tensor(g_k, g_k, g_la, ALU.mult).then_inc(G["gla_kd"].sem, 1)
                for n in range(NCH):
                    ps = full(("upd", n), l)
                    for c in range(2):
                        for p in range(2):
                            lo, hi = 64 * p, 64 * p + 64
                            src = ps[lo:hi, c * 256 + p * P:c * 256 + (p + 1) * P]
                            if n == 0:
                                last = V.tensor_copy(g_st[lo:hi, n, c, :], src)
                            else:
                                last = V.scalar_tensor_tensor(out=g_st[lo:hi, n, c, :], in0=g_st[lo:hi, n - 1, c, :],
                                                              scalar=g_dec[lo:hi, c, n:n + 1], in1=src, op0=ALU.mult, op1=ALU.add)
                    last.then_inc(B.freed(("upd", n)), 1)
                    dve.drain().then_inc(G["gla_state"].sem, 1)
                need("dsa_rs", l, 1)
                for c in range(2):
                    last = V.scalar_tensor_tensor(out=d_qc[:, c, :], in0=d_qc[:, c, :], scalar=cl("dsa_g_qc", c), in1=d_sq[:, 0, :],
                                                  op0=ALU.mult, op1=ALU.mult)
                dve.drain().then_inc(G["dsa_n"].sem, 1)
                need("dsa_rs", l, 2)
                V.scalar_tensor_tensor(out=d_kv, in0=d_kv, scalar=cl("dsa_g_kv"), in1=d_sq[:, 2, :], op0=ALU.mult, op1=ALU.mult)\
                    .then_inc(G["dsa_n"].sem, 1)
                need("gla_in", l, 13)
                for h in range(4):
                    need("o_rs", l, h + 1)
                    V.scalar_tensor_tensor(out=g_o[:, h, :], in0=g_o[:, h, :], scalar=cl("gla_g_o"), in1=g_o2[:, h, :], op0=ALU.mult, op1=ALU.mult)
                    dve.drain()
                    V.tensor_tensor(ya[:, h, :], g_o[:, h, :], g_r[:, h, :], ALU.mult)
                join(dve, l, 2)

                V.memset(d_nm[:, 0, 0:P], 0.0)
                dve.drain()
                V.memset(d_nm[0:64, 0, 64:P], DROP)
                for b in range(1, 4):
                    w = P * (b + 1)
                    s_ = d_nm[:, b, 0:w]
                    for h in range(4):
                        need("relu", l, (b - 1) * 4 + h + 1)
                        if h == 0:
                            V.tensor_scalar(s_, d_rl[h][:, 0:w], d_iw[:, b, h:h + 1], None, ALU.mult).then_inc(G["relu_used"].sem, 1)
                        else:
                            V.scalar_tensor_tensor(out=s_, in0=d_rl[h][:, 0:w], scalar=d_iw[:, b, h:h + 1], in1=s_, op0=ALU.mult, op1=ALU.add)\
                                .then_inc(G["relu_used"].sem, 1)
                        dve.drain()
                    V.memset(d_nm[0:64, b, w - 64:w], NEG)
                    dve.drain()

                def pick(n):
                    b = 1 + n // (TOPK // 8)
                    s_ = d_nm[:, b, 0:P * (b + 1)]
                    V.max(d_m8, s_)
                    dve.drain()
                    V.match_replace(s_, d_m8, s_, MARK)
                    dve.drain()
                    if n % (TOPK // 8) == TOPK // 8 - 1:
                        V.tensor_scalar(s_, s_, MARK, -DROP, ALU.is_equal, ALU.mult)
                        dve.drain()
                        V.tensor_scalar(s_, s_, DROP, None, ALU.add)
                        dve.drain()

                def merge(i, m, r):
                    need("gate", l, i + 1)
                    ps = full(("br", m, r), l)
                    dst = m_o[:, m, :] if r == 0 else m_t
                    V.tensor_tensor(dst, ps[:, :], m_g[i % 2], ALU.mult).then_inc(B.freed(("br", m, r)), 1)
                    dve.drain().then_inc(G["gate_used"].sem, 1)
                    if r:
                        V.tensor_tensor(m_o[:, m, :], m_o[:, m, :], m_t, ALU.add)
                        dve.drain()

                rounds = 3 * (TOPK // 8) // KD
                for m in range(KD):
                    for n in range(rounds * m, rounds * (m + 1)):
                        if n == rounds * m + rounds // 2:
                            merge(2 * m, m, 0)
                        pick(n)
                    merge(2 * m + 1, m, 2)
                join(dve, l, 3)
                for i in range(QUADS + 1):
                    if i >= 1:
                        n = i - 1
                        w = P * (n // 2 + 1)
                        need("lg_exp", l, n + 1)
                        V.reciprocal(d_mx[:, 4 * n:4 * n + 4], d_sm[:, 4 * n:4 * n + 4])
                        dve.drain()
                        for j in range(4):
                            V.tensor_scalar(d_p[n % 2][j][:, 0:w], d_p[n % 2][j][:, 0:w], d_mx[:, 4 * n + j:4 * n + j + 1], None, ALU.mult)
                        dve.drain().then_inc(G["p_ready"].sem, 1)
                    if i < QUADS:
                        b = i // 2
                        w = P * (b + 1)
                        for j in range(4):
                            ps = full(("lg", i, j), l)
                            if i >= 2:
                                dve.wait_ge(*B.full(("pt", i - 2, j), l))
                            dve.sem_inc(passed, 1)
                            V.tensor_tensor_reduce(d_p[i % 2][j][:, 0:w], ps[:, 0:w], d_nm[:, b, 0:w], 1.0, NEG, ALU.add, ALU.max,
                                                   d_mx[:, 4 * i + j:4 * i + j + 1]).then_inc(B.freed(("lg", i, j)), 1)
                        dve.drain()
                        V.tensor_scalar(d_n[:, 4 * i:4 * i + 4], d_mx[:, 4 * i:4 * i + 4], -(P ** -0.5), None, ALU.mult)
                        dve.drain().then_inc(G["lg_max"].sem, 1)
                join(dve, l, 4)

                for m in range(KD):
                    merge(2 * KD + m, m, 1)
                V.nop().then_inc(G["merged"].sem, 1)
                for m in range(KD):
                    ps = full(("wo", m), l)
                    V.scalar_tensor_tensor(out=xT[:, m, :], in0=ps[:, :], scalar=modc[:, 16 + m:17 + m], in1=xT[:, m, :], op0=ALU.mult, op1=ALU.add)\
                        .then_inc(B.freed(("wo", m)), 1)
                    dve.drain().then_inc(G["x_mixed"].sem, 1)
                join(dve, l, 5)
                norm(1)
                join(dve, l, 6)

                c4 = e_c.rearrange("p h (a b) -> p h a b", a=ET)
                pos = e_pos.rearrange("p h k -> p (h k)")

                def best(r, vals, src, rows):
                    for g in rows:
                        V.max(vals[:, g, 8 * r:8 * r + 8], src[:, g, :])
                    dve.drain()

                def places_of(r, vals, places, src, rows):
                    for g in rows:
                        V.max_index(places[:, g, 8 * r:8 * r + 8], vals[:, g, 8 * r:8 * r + 8], src[:, g, :])
                    dve.drain()

                def strike(vals, src, rows):
                    for g in rows:
                        V.match_replace(src[:, g, :], vals[:, g, 0:8], src[:, g, :], NEG)
                    dve.drain()

                def piece(i, lap, t, h0, h1):
                    heads, keys, top = range(h0, h1), range(2 * h0, 2 * h1), slice(h0 * ET, h1 * ET)
                    if i == 0:
                        dve.wait_ge(*E_["scored"].at(lap, h1 // 2))
                        dve.sem_inc(passed, 1)
                        best(0, e_v, e_s, keys)
                        places_of(0, e_v, e_i, e_s, keys)
                    elif i == 1:
                        strike(e_v, e_s, keys)
                        best(1, e_v, e_s, keys)
                    elif i == 2:
                        places_of(1, e_v, e_i, e_s, keys)
                        V.tensor_copy(e_if[:, 2 * h0:2 * h1, :], e_i[:, 2 * h0:2 * h1, :])
                        for h in heads:
                            V.tensor_tensor(c4[:, h], bc(e_v[:, 2 * h, :].unsqueeze(2), [P, ET, ET]),
                                            bc(e_v[:, 2 * h + 1, :].unsqueeze(1), [P, ET, ET]), ALU.add)
                        dve.drain()
                    elif i == 3:
                        best(0, e_top, e_c, heads)
                        places_of(0, e_top, e_pos, e_c, heads)
                    elif i == 4:
                        strike(e_top, e_c, heads)
                        best(1, e_top, e_c, heads)
                    elif i == 5:
                        places_of(1, e_top, e_pos, e_c, heads)
                        V.tensor_tensor(e_ex[:, h0:h1, :], e_top[:, h0:h1, :], bc(e_top[:, h0:h1, 0:1], [P, h1 - h0, ET]), ALU.subtract)
                        V.tensor_scalar(e_pa[:, top], pos[:, top], 4, None, ALU.logical_shift_right)
                        V.tensor_scalar(e_pb[:, top], pos[:, top], 15, None, ALU.bitwise_and)
                        dve.drain()
                        if h1 == EH:
                            dve.sem_inc(E_["soft_in"].sem, 1)
                        V.tensor_copy(e_paf[:, top], e_pa[:, top])
                        V.tensor_copy(e_pbf[:, top], e_pb[:, top])
                        dve.drain()
                    elif i == 6:
                        n = (h1 - h0) * ET
                        for pf, oh in ((e_paf, e_oh), (e_pbf, e_oh2)):
                            V.tensor_tensor(oh.rearrange("p (k j) -> p k j", j=ET)[:, top, :], bc(pf[:, top].unsqueeze(2), [P, n, ET]),
                                            bc(iota16.unsqueeze(1), [P, n, ET]), ALU.is_equal)
                        dve.drain()
                        for half_, oh in enumerate((e_oh, e_oh2)):
                            o4 = oh.rearrange("p (h k j) -> p h k j", h=EH, j=ET)
                            for h in heads:
                                V.tensor_tensor(o4[:, h], o4[:, h], bc(e_if[:, 2 * h + half_, :].unsqueeze(1), [P, ET, ET]), ALU.mult)
                        dve.drain()
                    else:
                        for oh, dst in ((e_oh, e_n1), (e_oh2, e_n2)):
                            V.tensor_reduce(dst[:, top], oh.rearrange("p (k j) -> p k j", j=ET)[:, top, :], AX.X, ALU.add)
                        dve.drain()
                        V.scalar_tensor_tensor(out=e_n1[:, top], in0=e_n1[:, top], scalar=float(NK), in1=e_n2[:, top], op0=ALU.mult, op1=ALU.add)
                        dve.drain()
                        V.tensor_scalar(e_idx[:, bass.ds(t * SLOTS + h0 * ET, (h1 - h0) * ET)], e_n1[:, top], e_off[:, 0:1], None, ALU.add)
                        if h1 < EH:
                            dve.drain().then_inc(E_["routed"].sem, 1)
                        else:
                            dve.wait_ge(*E_["soft"].at(lap))
                            V.tensor_reduce(e_sum, e_ex, AX.X, ALU.add)
                            dve.drain()
                            V.reciprocal(e_sum, e_sum)
                            dve.drain()
                            V.tensor_tensor(v3(e_gate[:, bass.ds(t * SLOTS, SLOTS)], 8), e_ex, bc(e_sum.unsqueeze(2), [P, EH, ET]), ALU.mult)
                            dve.drain().then_inc(E_["routed"].sem, 2 if h0 == 0 else 1)

                def expert_tile(lap, t, more):
                    dve.wait_ge(*E_["rows_in"].at(lap))
                    dve.sem_inc(passed, 1)

                    def groups(g0, g1):
                        with dve.Fori(g0, g1) as g:
                            turn = lap * NGRP + g
                            for s_ in range(GRP):
                                dve.wait_ge(rows_landed[s_], 16 * (turn + 1))
                                dve.wait_ge(rows_used[s_], turn + 1)
                                V.tensor_tensor_reduce(e_row[s_][:, 0:D], e_row[s_][:, 0:D], e_hc, 1.0, 0.0, ALU.mult, ALU.add, e_dot[:, s_:s_ + 1])
                                dve.drain().then_inc(dots[s_], 1)
                    g0 = 0
                    if more:
                        for i, g1 in enumerate(PIECES):
                            groups(g0, g1 + 1)
                            piece(i, lap + 1, t + 1, 0, EH)
                            g0 = g1 + 1
                    groups(g0, NGRP)
                    for j in range(2):
                        ps = full(("xt", j), lap, T)
                        for i in range(4):
                            k = 4 * j + i
                            xs = xT[:, k, bass.ds(t * P, P)]
                            last = V.scalar_tensor_tensor(out=xs, in0=ps[:, i * P:(i + 1) * P], scalar=modc[:, 40 + k:41 + k], in1=xs,
                                                          op0=ALU.mult, op1=ALU.add)
                        last.then_inc(T.freed(("xt", j)), 1)
                    dve.drain().then_inc(E_["tile_out"].sem, 1)

                for h0 in (0, EH // 2):
                    for i in range(len(PIECES)):
                        piece(i, l * TT, 0, h0, h0 + EH // 2)
                join(dve, l, 7)
                with dve.Fori(0, TT - 1) as t:
                    expert_tile(l * TT + t, t, True)
                expert_tile(l * TT + TT - 1, TT - 1, False)
                V.tensor_scalar(e_off[:], e_off[:], float(NE), None, ALU.add)
                join(dve, l, 8)
            dve.wait_ge(rstd_ready, depth * 2 + 1)
            for k in range(KD):
                V.scalar_tensor_tensor(out=hT[:, k, :], in0=xT[:, k, :], scalar=fix[:, KD + k:KD + k + 1], in1=rstd[:],
                                       op0=ALU.mult, op1=ALU.mult).then_inc(stored, 1)

        @block.gpsimd
        def _(pool):
            def need(sig, l, k=None):
                pool.wait_ge(*G[sig].at(l, k))

            pool.wait_ge(loaded, 64)
            with pool.Fori(0, depth) as l:
                need("cond_ready", l)
                for n in range(2, ADA_HALVES):
                    if n in ADA_LENT:
                        continue
                    block_i = ADA_RING + n // 2
                    if n % 2 == 0 and block_i in (7, 11):
                        pool.wait_ge(*B.full(("mod", block_i // 4 - 1), l))
                    pool.wait_ge(ada_landed[n % 2], 16 * (l * (ADA_HALVES // 2) + n // 2 + 1))
                    pool.sem_inc(passed, 1)
                    w = a_half[n % 2]
                    nc.gpsimd.tensor_tensor(w, w, bc(cond[:].unsqueeze(2), [P, 8, 256]), ALU.mult)
                    pool.drain()
                    for m in (4, 2):
                        nc.gpsimd.tensor_tensor(w[:, 0:m, :], w[:, 0:m, :], w[:, m:2 * m, :], ALU.add)
                        pool.drain()
                    nc.gpsimd.tensor_tensor(a_at[block_i][:, n % 2 * 256:(n % 2 + 1) * 256], w[:, 0, :], w[:, 1, :], ALU.add)
                    pool.drain().then_inc(ada_used[n % 2], 1)
                    pool.sem_inc(G["ada_half_summed"].sem, 1)
                pool.wait_ge(*B.full(("mod", 2), l))
                for half, t, q, lv in rwkv_steps():
                    if half or lv > 6:
                        continue
                    if lv == 0:
                        if t:
                            need(f"u_copied{q}", l, 6 * t)
                        need("ab_masked", l, 4 * (2 * t + q) + 2)
                    elif lv == 2:
                        need(f"t_updated{q}", l, 13 * t + 2)
                    elif lv > 2:
                        need(f"u_copied{q}", l, 6 * t + lv - 2)
                    hs = slice(4 * q, 4 * q + 4)
                    nc.gpsimd.tensor_tensor(r_m[lv % 2][:, hs, :], r_ab[:, hs, 0:P], bc(lvl[:, lv, :].unsqueeze(1), [P, 4, P]), ALU.mult)\
                        .then_inc(G[f"level_masked{q}"].sem, 1)
                with pool.Fori(0, TT) as t:
                    lap = l * TT + t
                    for part in range(2):
                        pool.wait_ge(*E_["routed"].at(lap, part + 1))
                        pool.sem_inc(passed, 1)
                        with pool.Fori(part * NGRP // 2, (part + 1) * NGRP // 2) as g:
                            turn = lap * NGRP + g
                            for s_ in range(GRP):
                                if s_ in (3, 5):
                                    i = free_first if s_ == 3 else 1 - free_first
                                    pool.wait_ge(used[i], (l + 1) * nblock[i] + 1)
                                    pool.sem_inc(passed, 1)
                                pool.wait_ge(rows_used[s_], turn + 1)
                                pool.sem_inc(passed, 1)
                                pool.tensor_copy(e_ic[:, s_:s_ + 1], e_idx[:, bass.ds(t * SLOTS + g * GRP + s_, 1)]).then_inc(idx_ready, 1)
                                pool.wait_ge(idx_ready, turn * GRP + s_ + 1)
                                pool.sem_inc(passed, 1)
                                pool.indirect_dma_start(e_row[s_], None, uv, bass.IndirectOffsetOnAxis(ap=e_ic[:, s_:s_ + 1], axis=0))\
                                    .then_inc(rows_landed[s_], 16)


_COLS = ('b_ada', 'g_norm_mix', 'g_norm_ffn', 'gla_b_a', 'gla_g_o', 'dsa_g_qc', 'dsa_g_kv', 'rwkv_mu', 'rwkv_w0', 'rwkv_a0',
         'rwkv_k_k', 'rwkv_k_a', 'rwkv_r_k', 'rwkv_ln_g', 'rwkv_ln_b')


def constants():
    i = np.arange(P)
    s, t = i[:, None], i[None, :]
    lv = [((t >> j) % 2 == 1) & ((s >> j) == (t >> j) - 1) for j in range(7)]
    col = np.arange(S)[None, :] + 0 * s
    parts = [s == t, s >= 0 * t, s // 64 == t // 64, s < t, s <= t, *lv, col % CH != 0, col % P != 0]
    iota = np.arange(ET)[None, :] + 0 * s
    return np.concatenate([np.broadcast_to(p, (P, p.shape[1])) for p in parts] + [iota], axis=1).astype(np.float32)


def laid_out(a):
    f = {k: np.asarray(v) for k, v in a.items()}

    def column(v):
        return np.swapaxes(v.reshape(L, -1, P), 1, 2)

    cols = np.concatenate([column(f[n].reshape(L, -1)) for n in _COLS], axis=2)
    cols = np.ascontiguousarray(cols.transpose(1, 0, 2).reshape(P, L * NCOL))
    fixed = np.concatenate([f['c'].reshape(KD, P).T, f['g_final'].reshape(KD, P).T], axis=1)
    keys = f['peer_keys'].transpose(0, 2, 4, 1, 3).reshape(L, P, EH * NK)
    ga = np.concatenate([f['gla_w_a2'], np.zeros((L, P - 16, 256), np.float32)], axis=1)
    small = np.concatenate([ga, np.concatenate([f['rwkv_w_w2'], f['rwkv_w_a2']], axis=1), f['rwkv_w_g2'], keys,
                            f['dsa_w_uv'].transpose(0, 2, 1, 3).reshape(L, P, 512)], axis=2)
    gates = f['w_in'][:, :, GATES:].reshape(L, 8, P, 3, 8, P).transpose(0, 4, 2, 3, 1, 5)
    branch = f['w_branch'].reshape(L, 3, 4, P, 8, P).transpose(0, 4, 3, 1, 2, 5)
    merge = np.concatenate([gates, branch], axis=4)
    w_mac = merge[:, :, :, 0::2].reshape(L, 8, P, 24 * P)
    w_mb = merge[:, :, :, 1].reshape(L, 4, 2, P, 12, P).transpose(0, 1, 3, 2, 4, 5).reshape(L, 4, P, 24 * P)
    return dict(fixed=fixed, cols=cols, consts=constants(), x_t=f['x'].reshape(S, D).T, w_ada=f['w_ada'], w_in=f['w_in'],
                w_small=small, w_uq=f['dsa_w_uq'], w_iq=f['dsa_w_iq'], w_mac=w_mac, w_mb=w_mb, w_out=f['w_out'],
                w_pq=f['peer_w_q'], uv=np.concatenate([f['peer_u'], f['peer_v']], axis=2).reshape(L * NE, 2 * D))


def kernel(**inputs):
    import concourse.bacc as _bacc
    from concourse.bass_utils import run_bass_kernel_spmd as _run

    nc = _bacc.Bacc("TRN2", target_bir_lowering=False, num_devices=1)
    arrays = {k: np.ascontiguousarray(v) for k, v in laid_out(inputs).items()}
    args = [nc.dram_tensor(k, v.shape, F32, kind="ExternalInput").ap() for k, v in arrays.items()]
    out = nc.dram_tensor("out", (D, S), F32, kind="ExternalOutput").ap()
    trunk(nc, *args, out)
    r = _run(nc, [arrays], core_ids=[0])
    return np.ascontiguousarray(r.results[0]["out"].T).reshape(1, S, D)
```
